# Optimizing a Trainium2 kernel written in Bass

```python
import math
import jax, jax.numpy as jnp
from jax import lax
import numpy as np

D_MODEL = 1024
BATCH = 1
SEQ = 512
DEPTH = 2

ATTN_HEADS = 8
ATTN_KV_HEADS = 2
ATTN_HEAD_DIM = D_MODEL // ATTN_HEADS
ATTN_WIDTH = ATTN_HEADS * ATTN_HEAD_DIM
ATTN_KV_WIDTH = ATTN_KV_HEADS * ATTN_HEAD_DIM
ATTN_ROT_DIM = ATTN_HEAD_DIM // 4
IDX_HEADS = 8
IDX_DIM = 64
IDX_ROT_DIM = IDX_DIM // 4
INDEX_TOPK = 256
Q_BLOCK = 128
ROPE_THETA = 500000.0
GDN_HEADS = 8
GDN_DK = 128
GDN_DV = 128
GDN_QK_WIDTH = GDN_HEADS * GDN_DK
GDN_WIDTH = GDN_HEADS * GDN_DV
GDN_QKV_WIDTH = 2 * GDN_QK_WIDTH + GDN_WIDTH
CONV_K = 4
CHUNK = 64
N_BRANCH = 2
NORM_EPS = 1e-6

IN_SPLITS = [
    ATTN_WIDTH,
    ATTN_KV_WIDTH,
    ATTN_KV_WIDTH,
    ATTN_WIDTH,
    IDX_HEADS * IDX_DIM,
    IDX_DIM,
    IDX_HEADS,
    GDN_QKV_WIDTH,
    GDN_WIDTH,
    GDN_HEADS,
    GDN_HEADS,
    N_BRANCH * D_MODEL,
]
IN_COLS = sum(IN_SPLITS)
IN_SPLIT_IDX = [sum(IN_SPLITS[:i + 1]) for i in range(len(IN_SPLITS) - 1)]


def rms_norm(x, gain):
    xf = x.astype(jnp.float32)
    y = xf * lax.rsqrt(jnp.mean(xf * xf, axis=-1, keepdims=True) + NORM_EPS)
    return (y * gain.astype(jnp.float32)).astype(x.dtype)

def l2_normalize(x):
    xf = x.astype(jnp.float32)
    return xf * lax.rsqrt(jnp.sum(xf * xf, axis=-1, keepdims=True) + NORM_EPS)

def rope_tables(positions, rot_dim):
    inv_freq = ROPE_THETA ** (-jnp.arange(0, rot_dim, 2, dtype=jnp.float32) / rot_dim)
    ang = positions.astype(jnp.float32)[..., None] * inv_freq
    return jnp.cos(ang)[:, :, None, :], jnp.sin(ang)[:, :, None, :]

def apply_partial_rope(x, cos, sin):
    half = cos.shape[-1]
    rot = 2 * half
    x1, x2, xp = x[..., :half], x[..., half:rot], x[..., rot:]
    c, s = cos.astype(x.dtype), sin.astype(x.dtype)
    return jnp.concatenate([x1 * c - x2 * s, x2 * c + x1 * s, xp], axis=-1)

def dsa_attention(q, k, v, q_idx, k_idx, w_idx):
    B, S = q.shape[0], q.shape[1]
    topk = min(INDEX_TOPK, S // 4)
    nb = S // Q_BLOCK
    group = ATTN_HEADS // ATTN_KV_HEADS
    scale = ATTN_HEAD_DIM ** -0.5
    key_pos = jnp.arange(S, dtype=jnp.int32)

    def blocks(t):
        return t.reshape(B, nb, Q_BLOCK, *t.shape[2:]).swapaxes(0, 1)

    def one_block(args):
        qb, qib, wb, tb = args
        raw = jnp.einsum('bqhd,bsd->bqhs', qib, k_idx)
        iscore = jnp.einsum('bqhs,bqh->bqs', jax.nn.relu(raw), wb).astype(jnp.float32)
        causal = key_pos[None, :] <= tb[:, None]
        iscore = jnp.where(causal[None], iscore, -jnp.inf)
        _, sel = lax.top_k(iscore, topk)
        valid = sel <= tb[None, :, None]
        k_sel = jax.vmap(lambda kb, ib: kb[ib])(k, sel)
        v_sel = jax.vmap(lambda vb, ib: vb[ib])(v, sel)
        qg = qb.reshape(B, Q_BLOCK, ATTN_KV_HEADS, group, ATTN_HEAD_DIM)
        logits = jnp.einsum('bqhgd,bqkhd->bqhgk', qg, k_sel).astype(jnp.float32) * scale
        logits = jnp.where(valid[:, :, None, None, :], logits, -jnp.inf)
        p = jax.nn.softmax(logits, axis=-1).astype(v.dtype)
        o = jnp.einsum('bqhgk,bqkhd->bqhgd', p, v_sel)
        return o.reshape(B, Q_BLOCK, ATTN_WIDTH)

    out = lax.map(one_block, (blocks(q), blocks(q_idx), blocks(w_idx),
                              key_pos.reshape(nb, Q_BLOCK)))
    return out.swapaxes(0, 1).reshape(B, S, ATTN_WIDTH)

def causal_depthwise_conv(x, w):
    C = x.shape[-1]
    return lax.conv_general_dilated(
        x, w[:, None, :].astype(x.dtype), window_strides=(1,),
        padding=[(CONV_K - 1, 0)], dimension_numbers=('NWC', 'WIO', 'NWC'),
        feature_group_count=C)

def chunked_gated_delta_rule(q, k, v, beta, g):
    B, S, H, dk = q.shape
    dv = v.shape[-1]
    nc = S // CHUNK

    def c4(t):
        return t.reshape(B, nc, CHUNK, H, t.shape[-1]).transpose(0, 3, 1, 2, 4)

    def c3(t):
        return t.reshape(B, nc, CHUNK, H).transpose(0, 3, 1, 2)

    q, k, v = c4(q) * (dk ** -0.5), c4(k), c4(v)
    beta, gc = c3(beta), jnp.cumsum(c3(g), axis=-1)
    incl = jnp.tril(jnp.ones((CHUNK, CHUNK), dtype=bool))
    strict = jnp.tril(jnp.ones((CHUNK, CHUNK), dtype=bool), k=-1)
    decay = jnp.exp(jnp.where(incl, gc[..., :, None] - gc[..., None, :], -jnp.inf))
    kb = k * beta[..., None]
    lower = jnp.where(strict, jnp.einsum('bhnid,bhnjd->bhnij', kb, k) * decay, 0.0)
    tmat = jnp.eye(CHUNK, dtype=jnp.float32) + lower
    u = lax.linalg.triangular_solve(tmat, v * beta[..., None], left_side=True,
                                    lower=True, unit_diagonal=True)
    w = lax.linalg.triangular_solve(tmat, kb * jnp.exp(gc)[..., None], left_side=True,
                                    lower=True, unit_diagonal=True)
    qk = jnp.einsum('bhnid,bhnjd->bhnij', q, k) * decay
    q_dec = q * jnp.exp(gc)[..., None]
    k_dec = k * jnp.exp(gc[..., -1:] - gc)[..., None]
    g_tot = jnp.exp(gc[..., -1])
    xs = (jnp.moveaxis(qk, 2, 0), jnp.moveaxis(q_dec, 2, 0), jnp.moveaxis(k_dec, 2, 0),
          jnp.moveaxis(u, 2, 0), jnp.moveaxis(w, 2, 0), jnp.moveaxis(g_tot, 2, 0))

    def step(state, xc):
        qk_c, qd_c, kd_c, u_c, w_c, gt_c = xc
        v_new = u_c - jnp.einsum('bhcd,bhde->bhce', w_c, state)
        o_c = (jnp.einsum('bhcd,bhde->bhce', qd_c, state)
               + jnp.einsum('bhij,bhje->bhie', qk_c, v_new))
        state = state * gt_c[..., None, None] + jnp.einsum('bhcd,bhce->bhde', kd_c, v_new)
        return state, o_c

    state0 = jnp.zeros((B, H, dk, dv), dtype=jnp.float32)
    _, o = lax.scan(step, state0, xs)
    return o.transpose(1, 0, 3, 2, 4).reshape(B, S, H, dv)

def first_inputs(seed: int = 0) -> dict:
    key = jax.random.key(seed)
    ks = jax.random.split(key, 12)
    x = jax.random.normal(ks[0], (BATCH, SEQ, D_MODEL), jnp.float32)
    positions = jnp.broadcast_to(jnp.arange(SEQ, dtype=jnp.int32), (BATCH, SEQ))
    norm_gain = 1.0 + 0.02 * jax.random.normal(ks[1], (DEPTH, D_MODEL), jnp.float32)
    w_in = jax.random.normal(ks[2], (DEPTH, D_MODEL, IN_COLS), jnp.float32) * D_MODEL ** -0.5
    conv_w = jax.random.normal(ks[3], (DEPTH, CONV_K, GDN_QKV_WIDTH), jnp.float32) * CONV_K ** -0.5
    a_log = jnp.log(jax.random.uniform(ks[4], (DEPTH, GDN_HEADS), jnp.float32, 1.0, 16.0))
    dt = jnp.exp(jax.random.uniform(ks[5], (DEPTH, GDN_HEADS), jnp.float32,
                                    math.log(1e-3), math.log(1e-1)))
    dt_bias = dt + jnp.log(-jnp.expm1(-dt))
    gdn_norm_gain = 1.0 + 0.02 * jax.random.normal(ks[6], (DEPTH, GDN_DV), jnp.float32)
    idx_k_gain = 1.0 + 0.02 * jax.random.normal(ks[7], (DEPTH, IDX_DIM), jnp.float32)
    w_out = jax.random.normal(ks[8], (DEPTH, D_MODEL, D_MODEL), jnp.float32) * D_MODEL ** -0.5
    final_gain = 1.0 + 0.02 * jax.random.normal(ks[9], (D_MODEL,), jnp.float32)
    return {"x": x, "positions": positions, "norm_gain": norm_gain, "w_in": w_in,
            "conv_w": conv_w, "a_log": a_log, "dt_bias": dt_bias,
            "gdn_norm_gain": gdn_norm_gain, "idx_k_gain": idx_k_gain,
            "w_out": w_out, "final_gain": final_gain}

def first_block(x, positions, norm_gain, w_in, conv_w, a_log, dt_bias, gdn_norm_gain,
              idx_k_gain, w_out, final_gain):
    B, S = x.shape[0], x.shape[1]
    cos_a, sin_a = rope_tables(positions, ATTN_ROT_DIM)
    cos_i, sin_i = rope_tables(positions, IDX_ROT_DIM)
    idx_scale = IDX_HEADS ** -0.5 * IDX_DIM ** -0.5
    for layer in range(DEPTH):
        h = rms_norm(x, norm_gain[layer])
        proj = h @ w_in[layer]
        (q_a, k_a, v_a, z_a, q_i, k_i, w_i, qkv_b, z_b, beta_l, a_l, gate_l) = jnp.split(
            proj, IN_SPLIT_IDX, axis=-1)

        q_a = apply_partial_rope(q_a.reshape(B, S, ATTN_HEADS, ATTN_HEAD_DIM), cos_a, sin_a)
        k_a = apply_partial_rope(k_a.reshape(B, S, ATTN_KV_HEADS, ATTN_HEAD_DIM), cos_a, sin_a)
        v_a = v_a.reshape(B, S, ATTN_KV_HEADS, ATTN_HEAD_DIM)
        q_i = apply_partial_rope(q_i.reshape(B, S, IDX_HEADS, IDX_DIM), cos_i, sin_i)
        k_i = apply_partial_rope(rms_norm(k_i, idx_k_gain[layer])[:, :, None, :],
                                 cos_i, sin_i)[:, :, 0, :]
        w_i = w_i * idx_scale
        y_a = dsa_attention(q_a, k_a, v_a, q_i, k_i, w_i) * jax.nn.silu(z_a)

        qkv_b = jax.nn.silu(causal_depthwise_conv(qkv_b, conv_w[layer]))
        q_b, k_b, v_b = jnp.split(qkv_b, [GDN_QK_WIDTH, 2 * GDN_QK_WIDTH], axis=-1)
        q_b = l2_normalize(q_b.reshape(B, S, GDN_HEADS, GDN_DK))
        k_b = l2_normalize(k_b.reshape(B, S, GDN_HEADS, GDN_DK))
        v_b = v_b.reshape(B, S, GDN_HEADS, GDN_DV).astype(jnp.float32)
        beta = jax.nn.sigmoid(beta_l.astype(jnp.float32))
        g = -jnp.exp(a_log[layer].astype(jnp.float32)) * jax.nn.softplus(
            a_l.astype(jnp.float32) + dt_bias[layer].astype(jnp.float32))
        o_b = chunked_gated_delta_rule(q_b, k_b, v_b, beta, g).astype(x.dtype)
        y_b = (rms_norm(o_b, gdn_norm_gain[layer])
               * jax.nn.silu(z_b.reshape(B, S, GDN_HEADS, GDN_DV))).reshape(B, S, GDN_WIDTH)

        gates = jax.nn.sigmoid(gate_l).reshape(B, S, N_BRANCH, D_MODEL)
        mixed = gates[:, :, 0, :] * y_a + gates[:, :, 1, :] * y_b
        x = x + mixed @ w_out[layer]
    return rms_norm(x, final_gain)


N_MIXERS = 2
N_LAYERS_A = (DEPTH + 1) // 2
N_LAYERS_B = DEPTH // 2
PLE_DIM = 256
CONV_A_WIDTH = 3
D_RNN = D_MODEL
LRU_BLOCK = 256
N_LRU_BLOCKS = D_RNN // LRU_BLOCK
CONV_B_WIDTH = 4
RG_C = 8.0
N_GROUPS = 4
EXPERTS_PER_GROUP = 8
N_EXPERTS = N_GROUPS * EXPERTS_PER_GROUP
TOP_K = 2
D_EXPERT = 512
ROUTE_BLOCK = 128
EPS = 1e-6


def rmsnorm(x, g):
    x32 = x.astype(jnp.float32)
    y = x32 * lax.rsqrt(jnp.mean(x32 * x32, axis=-1, keepdims=True) + EPS)
    return (y * g.astype(jnp.float32)).astype(x.dtype)

def depthwise_conv(x, w, pad):
    return lax.conv_general_dilated(
        x, w[:, None, :], window_strides=(1,), padding=[pad],
        dimension_numbers=('NWC', 'WIO', 'NWC'), feature_group_count=x.shape[-1])

def short_conv_mixer(xn, w_in, conv_w, w_out):
    bgate, cgate, h = jnp.split(xn @ w_in, 3, axis=-1)
    u = depthwise_conv(cgate * h, conv_w, (1, 1))
    return (bgate * u) @ w_out

def _linear_combine(earlier, later):
    a_e, b_e = earlier
    a_l, b_l = later
    return a_l * a_e, a_l * b_e + b_l

def rglru_direction(uh, w_r, b_r, w_i, b_i, lam, reverse):
    bsz, s, nh, dh = uh.shape
    u = uh.reshape(bsz, s, nh * dh)
    r = jax.nn.sigmoid((jnp.einsum('bshd,hde->bshe', uh, w_r).reshape(bsz, s, -1) + b_r).astype(jnp.float32))
    i = jax.nn.sigmoid((jnp.einsum('bshd,hde->bshe', uh, w_i).reshape(bsz, s, -1) + b_i).astype(jnp.float32))
    log_a = -RG_C * r * jax.nn.softplus(-lam.astype(jnp.float32))
    a = jnp.exp(log_a)
    gated = jnp.sqrt(-jnp.expm1(2.0 * log_a)) * (i * u.astype(jnp.float32))
    _, h = lax.associative_scan(_linear_combine, (a, gated), axis=1, reverse=reverse)
    return h.astype(uh.dtype)

def rglru_mixer(xn, w_in, conv_w, conv_bias, w_rg, b_rg, w_ig, b_ig, lam, w_out):
    y_branch, u = jnp.split(xn @ w_in, 2, axis=-1)
    y_branch = jax.nn.gelu(y_branch)
    u = depthwise_conv(u, conv_w, (2, 1)) + conv_bias
    bsz, s, _ = u.shape
    uh = u.reshape(bsz, s, N_LRU_BLOCKS, LRU_BLOCK)
    h = (rglru_direction(uh, w_rg[0], b_rg[0], w_ig[0], b_ig[0], lam[0], False)
         + rglru_direction(uh, w_rg[1], b_rg[1], w_ig[1], b_ig[1], lam[1], True))
    return (y_branch * h) @ w_out

def hier_moe(x, w_rg, b_rg, w_re, b_re, w_gate, w_up, w_down):
    bsz, s, d = x.shape
    n = bsz * s
    xf = x.reshape(n, d)
    pg = jax.nn.softmax((xf @ w_rg).astype(jnp.float32) + b_rg.astype(jnp.float32), axis=-1)
    pg_top, g_top = lax.top_k(pg, 1)
    le = ((xf @ w_re).astype(jnp.float32) + b_re.astype(jnp.float32)).reshape(n, N_GROUPS, EXPERTS_PER_GROUP)
    le_sel = jnp.take_along_axis(le, g_top[:, :, None], axis=1)[:, 0]
    pe = jax.nn.softmax(le_sel, axis=-1)
    top_p, top_i = lax.top_k(pe, TOP_K)
    top_p = top_p / jnp.sum(top_p, axis=-1, keepdims=True)
    expert = g_top * EXPERTS_PER_GROUP + top_i
    weight = pg_top * top_p

    n_slots = n * TOP_K
    e_flat = expert.reshape(-1)
    tok_flat = jnp.arange(n_slots, dtype=jnp.int32) // TOP_K
    w_flat = weight.reshape(-1)
    order = jnp.argsort(e_flat)
    e_sorted = e_flat[order]
    counts = jnp.bincount(e_flat, length=N_EXPERTS)
    start = jnp.cumsum(counts) - counts
    padded = ((counts + ROUTE_BLOCK - 1) // ROUTE_BLOCK) * ROUTE_BLOCK
    pend = jnp.cumsum(padded)
    pstart = pend - padded
    dest = pstart[e_sorted] + (jnp.arange(n_slots) - start[e_sorted])
    n_blocks = -(-n_slots // ROUTE_BLOCK) + N_EXPERTS
    slot_of_pos = jnp.full((n_blocks * ROUTE_BLOCK,), n_slots, jnp.int32).at[dest].set(order.astype(jnp.int32))
    tok_pad = jnp.concatenate([tok_flat, jnp.array([n], jnp.int32)])[slot_of_pos]
    w_pad = jnp.concatenate([w_flat, jnp.zeros((1,), jnp.float32)])[slot_of_pos]
    block_expert = jnp.clip(jnp.searchsorted(pend, jnp.arange(n_blocks) * ROUTE_BLOCK, side='right'), 0, N_EXPERTS - 1)
    x_pad = jnp.concatenate([xf, jnp.zeros((1, d), xf.dtype)], axis=0)

    def expert_block(args):
        idx, e = args
        xb = x_pad[idx]
        hb = jax.nn.silu(xb @ w_gate[e]) * (xb @ w_up[e])
        return hb @ w_down[e]

    y_blocks = lax.map(expert_block, (tok_pad.reshape(n_blocks, ROUTE_BLOCK), block_expert))
    contrib = y_blocks.reshape(-1, d) * w_pad[:, None].astype(x.dtype)
    y = jnp.zeros((n + 1, d), x.dtype).at[tok_pad].add(contrib)
    return y[:n].reshape(bsz, s, d)

def _normal(key, shape, fan_in):
    return jax.random.normal(key, shape, jnp.float32) * (fan_in ** -0.5)

def second_inputs(seed: int = 0) -> dict:
    key = jax.random.key(seed)
    ks = jax.random.split(key, 28)
    f32 = jnp.float32
    D, R, H, Bk = D_MODEL, D_RNN, N_LRU_BLOCKS, LRU_BLOCK
    x = jax.random.normal(ks[0], (BATCH, SEQ, D), f32)
    p = jax.random.normal(ks[1], (DEPTH, BATCH, SEQ, PLE_DIM), f32)
    norm_mix = 1.0 + 0.05 * jax.random.normal(ks[2], (DEPTH, D), f32)
    w_in_a = _normal(ks[3], (N_LAYERS_A, D, 3 * D), D)
    conv_a = _normal(ks[4], (N_LAYERS_A, CONV_A_WIDTH, D), CONV_A_WIDTH)
    w_out_a = _normal(ks[5], (N_LAYERS_A, D, D), D)
    w_in_b = _normal(ks[6], (N_LAYERS_B, D, 2 * R), D)
    conv_b = _normal(ks[7], (N_LAYERS_B, CONV_B_WIDTH, R), CONV_B_WIDTH)
    conv_bias_b = 0.01 * jax.random.normal(ks[8], (N_LAYERS_B, R), f32)
    w_rgate_b = _normal(ks[9], (N_LAYERS_B, 2, H, Bk, Bk), Bk)
    b_rgate_b = 0.01 * jax.random.normal(ks[10], (N_LAYERS_B, 2, R), f32)
    w_igate_b = _normal(ks[11], (N_LAYERS_B, 2, H, Bk, Bk), Bk)
    b_igate_b = 0.01 * jax.random.normal(ks[12], (N_LAYERS_B, 2, R), f32)
    a0 = jax.random.uniform(ks[13], (N_LAYERS_B, 2, R), f32, minval=0.9, maxval=0.999)
    sig = a0 ** (1.0 / RG_C)
    lam_b = jnp.log(sig) - jnp.log1p(-sig)
    w_out_b = _normal(ks[14], (N_LAYERS_B, R, D), R)
    norm_ffn = 1.0 + 0.05 * jax.random.normal(ks[15], (DEPTH, D), f32)
    w_router_group = _normal(ks[16], (DEPTH, D, N_GROUPS), D)
    b_router_group = 0.01 * jax.random.normal(ks[17], (DEPTH, N_GROUPS), f32)
    w_router_expert = _normal(ks[18], (DEPTH, D, N_EXPERTS), D)
    b_router_expert = 0.01 * jax.random.normal(ks[19], (DEPTH, N_EXPERTS), f32)
    w_exp_gate = _normal(ks[20], (DEPTH, N_EXPERTS, D, D_EXPERT), D)
    w_exp_up = _normal(ks[21], (DEPTH, N_EXPERTS, D, D_EXPERT), D)
    w_exp_down = _normal(ks[22], (DEPTH, N_EXPERTS, D_EXPERT, D), D_EXPERT)
    norm_ple = 1.0 + 0.05 * jax.random.normal(ks[23], (DEPTH, D), f32)
    w_ple = _normal(ks[24], (DEPTH, PLE_DIM, D), PLE_DIM)
    w_ple_gate = _normal(ks[25], (DEPTH, D, D), D)
    b_ple_gate = 0.01 * jax.random.normal(ks[26], (DEPTH, D), f32)
    norm_final = 1.0 + 0.05 * jax.random.normal(ks[27], (D,), f32)
    return {'x': x, 'p': p, 'norm_mix': norm_mix,
            'w_in_a': w_in_a, 'conv_a': conv_a, 'w_out_a': w_out_a,
            'w_in_b': w_in_b, 'conv_b': conv_b, 'conv_bias_b': conv_bias_b,
            'w_rgate_b': w_rgate_b, 'b_rgate_b': b_rgate_b,
            'w_igate_b': w_igate_b, 'b_igate_b': b_igate_b,
            'lam_b': lam_b, 'w_out_b': w_out_b, 'norm_ffn': norm_ffn,
            'w_router_group': w_router_group, 'b_router_group': b_router_group,
            'w_router_expert': w_router_expert, 'b_router_expert': b_router_expert,
            'w_exp_gate': w_exp_gate, 'w_exp_up': w_exp_up, 'w_exp_down': w_exp_down,
            'norm_ple': norm_ple, 'w_ple': w_ple, 'w_ple_gate': w_ple_gate,
            'b_ple_gate': b_ple_gate, 'norm_final': norm_final}

def second_block(x, p, norm_mix, w_in_a, conv_a, w_out_a, w_in_b, conv_b, conv_bias_b,
              w_rgate_b, b_rgate_b, w_igate_b, b_igate_b, lam_b, w_out_b, norm_ffn,
              w_router_group, b_router_group, w_router_expert, b_router_expert,
              w_exp_gate, w_exp_up, w_exp_down, norm_ple, w_ple, w_ple_gate,
              b_ple_gate, norm_final):
    h = x
    for i in range(DEPTH):
        xn = rmsnorm(h, norm_mix[i])
        j = i // N_MIXERS
        if i % N_MIXERS == 0:
            mix = short_conv_mixer(xn, w_in_a[j], conv_a[j], w_out_a[j])
        else:
            mix = rglru_mixer(xn, w_in_b[j], conv_b[j], conv_bias_b[j], w_rgate_b[j], b_rgate_b[j],
                              w_igate_b[j], b_igate_b[j], lam_b[j], w_out_b[j])
        h = h + mix
        h = h + hier_moe(rmsnorm(h, norm_ffn[i]), w_router_group[i], b_router_group[i],
                         w_router_expert[i], b_router_expert[i],
                         w_exp_gate[i], w_exp_up[i], w_exp_down[i])
        gate = jax.nn.sigmoid(rmsnorm(h, norm_ple[i]) @ w_ple_gate[i] + b_ple_gate[i])
        h = h + gate * (p[i] @ w_ple[i])
    return rmsnorm(h, norm_final)


def setup_inputs(seed=0):
    out = dict(first_inputs(seed))
    for name, value in second_inputs(seed + 1).items():
        if name != "x":
            out[name + "_2"] = value
    return out


def reference(
    x, positions, norm_gain, w_in, conv_w, a_log, dt_bias, gdn_norm_gain, idx_k_gain, w_out,
    final_gain, p_2, norm_mix_2, w_in_a_2, conv_a_2, w_out_a_2, w_in_b_2, conv_b_2,
    conv_bias_b_2, w_rgate_b_2, b_rgate_b_2, w_igate_b_2, b_igate_b_2, lam_b_2, w_out_b_2,
    norm_ffn_2, w_router_group_2, b_router_group_2, w_router_expert_2, b_router_expert_2,
    w_exp_gate_2, w_exp_up_2, w_exp_down_2, norm_ple_2, w_ple_2, w_ple_gate_2, b_ple_gate_2,
    norm_final_2,
):
    x = first_block(
        x, positions, norm_gain, w_in, conv_w, a_log, dt_bias, gdn_norm_gain, idx_k_gain, w_out,
        final_gain,
    )
    return second_block(
        x, p_2, norm_mix_2, w_in_a_2, conv_a_2, w_out_a_2, w_in_b_2, conv_b_2, conv_bias_b_2,
        w_rgate_b_2, b_rgate_b_2, w_igate_b_2, b_igate_b_2, lam_b_2, w_out_b_2, norm_ffn_2,
        w_router_group_2, b_router_group_2, w_router_expert_2, b_router_expert_2, w_exp_gate_2,
        w_exp_up_2, w_exp_down_2, norm_ple_2, w_ple_2, w_ple_gate_2, b_ple_gate_2, norm_final_2,
    )


_drawn_inputs = setup_inputs


def setup_inputs(seed=0):
    import zlib

    import numpy as np

    out = dict(_drawn_inputs(seed))
    spreads = {}
    factors = {'b_rgate_b_2': 43.559,
     'b_igate_b_2': 27.326,
     'b_router_group_2': 3.048,
     'b_router_expert_2': 3.177,
     'norm_ple_2': 4.115,
     'b_ple_gate_2': 31.044,
     'idx_k_gain': 2.67}
    for name, (base, spread) in spreads.items():
        noise = np.random.default_rng([zlib.crc32(name.encode()), seed]).standard_normal(out[name].shape)
        drawn = base * np.exp(spread * noise) if base else spread * noise
        out[name] = __import__('jax').numpy.asarray(drawn.astype(out[name].dtype))
    for name, factor in factors.items():
        out[name] = (out[name] * factor).astype(out[name].dtype)
    return out
```

```python
from collections import namedtuple
from contextlib import ExitStack, contextmanager

import concourse.bass as bass
import numpy as np
from concourse import mybir

F32 = mybir.dt.float32
I32 = mybir.dt.int32
U32 = mybir.dt.uint32
ALU = mybir.AluOpType
ACT = mybir.ActivationFunctionType
AX = mybir.AxisListType

P = 128
S = 512
T = S // P
D = 1024
K = D // P
DEPTH = 2
EPS = 1e-6

HEADS, KV_HEADS, DH = 8, 2, 128
GROUP = HEADS // KV_HEADS
IDX_HEADS, IDX_DIM = 8, 64
TOPK = min(256, S // 4)
C_Q = 0
C_K = C_Q + HEADS * DH
C_V = C_K + KV_HEADS * DH
C_Z = C_V + KV_HEADS * DH
C_QI = C_Z + HEADS * DH
C_KI = C_QI + IDX_HEADS * IDX_DIM
C_WI = C_KI + IDX_DIM
C_QKV = C_WI + IDX_HEADS
C_ZB = C_QKV + 3 * D
C_BETA = C_ZB + D
C_A = C_BETA + HEADS
C_GATE = C_A + HEADS
IN_COLS = C_GATE + 2 * D
SMALL = IDX_DIM + IDX_HEADS
ROPE_THETA = 500000.0
ROT_A, ROT_I = DH // 4, IDX_DIM // 4
CONV = 4
NEVER = -1e30
TAKEN = -3e38

LEVELS = 7
CONSTS = ["ident", "upto", "before", "ones", "causal", "rot_a", "rot_i"] + \
         [f"low{i}" for i in range(LEVELS)] + [f"up{i}" for i in range(LEVELS)]


def shape_constants():
    i = np.arange(P)
    row, col = i[:, None], i[None, :]
    parts = {
        "ident": row == col,
        "upto": row <= col,
        "before": row < col,
        "ones": np.ones((P, P)),
        "causal": np.where(col > row, NEVER, 0.0),
    }
    for name, dim, rot in (("rot_a", DH, ROT_A), ("rot_i", IDX_DIM, ROT_I)):
        half = rot // 2
        m = np.zeros((P, P))
        for base in range(0, P, dim):
            for j in range(half):
                m[base + j, base + j + half] = -1.0
                m[base + j + half, base + j] = 1.0
        parts[name] = m.T
    for lvl in range(LEVELS):
        b = 1 << lvl
        low = (row // (2 * b) == col // (2 * b)) & (row % (2 * b) >= b) & (col % (2 * b) < b)
        parts[f"low{lvl}"], parts[f"up{lvl}"] = low, low.T
    table = np.concatenate([np.asarray(parts[n], np.float32) for n in CONSTS], axis=1)
    freq = np.zeros((P, 2), np.float32)
    for c, (dim, rot) in enumerate(((DH, ROT_A), (IDX_DIM, ROT_I))):
        half = rot // 2
        inv = np.float32(ROPE_THETA) ** (-np.arange(0, rot, 2, dtype=np.float32) / np.float32(rot))
        for base in range(0, P, dim):
            freq[base:base + half, c] = inv
            freq[base + half:base + rot, c] = inv
    token = np.tile(np.arange(S, dtype=np.float32), (P, 1))
    fall = np.tile(P - np.arange(P, dtype=np.float32), (P, 1))
    return np.concatenate([table, freq, token, fall, i[:, None].astype(np.float32)], axis=1)


class Parts:
    pass


Norm = namedtuple("Norm", "rows stat")


def slab(w, c=512):
    return w[:, :].rearrange("p (k c) -> p k c", c=c)


def over(ap, n):
    return ap.unsqueeze(2).to_broadcast([ap.shape[0], ap.shape[1], n])


def each(ap, n):
    return ap.unsqueeze(1).to_broadcast([ap.shape[0], n, ap.shape[1]])


@contextmanager
def stage(nc, tag, names, **kept):
    with ExitStack() as ctx:
        sems = {n: ctx.enter_context(nc.semaphore(f"{n}_{tag}")) for n in names.split()}
        with nc.Block() as block:
            yield block, namedtuple("Signals", [*sems, *kept])(*sems.values(), *kept.values())
        if kept:
            first = min(sem.num for sem in kept.values())
            nc.gpsimd.dma_reset(range(first, first + len(kept)))
        for sem in (*sems.values(), *kept.values()):
            nc.gpsimd.sem_clear(sem)
        nc.all_engine_barrier()


@contextmanager
def memory(nc, tag):
    with ExitStack() as ctx:
        def tensor(name, shape, dt=F32):
            return ctx.enter_context(nc.sbuf_tensor(f"{name}_{tag}", shape, dt))
        yield tensor


NORM_SEMS = "squared meaned rooted scaled turned feat_a feat_v"
FEAT_EACH = K // 2


def norm_scalar(nc, act, g, s, m, gain):
    for t in range(T):
        nc.scalar.activation(m.rows[:, t, :], g.X[:, t, :], ACT.Square,
                             accum_out=m.stat[:, t:t + 1]).then_inc(s.squared, 1)
    act.wait_ge(s.meaned, 1)
    nc.scalar.activation(m.stat[:, 2 * T:3 * T], m.stat[:, T:2 * T], ACT.Sqrt).then_inc(s.rooted, 1)
    for k in range(0, K, 2):
        act.wait_ge(s.turned, k + 1)
        nc.scalar.activation(g.feat[:, k, :], g.PS[:, k, :], ACT.Copy,
                             scale=gain[:, k:k + 1]).then_inc(s.feat_a, 1)


def norm_vector(nc, dve, g, s, m, gain):
    dve.wait_ge(s.squared, T)
    nc.vector.tensor_scalar(m.stat[:, T:2 * T], m.stat[:, 0:T], 1.0 / D, EPS,
                            ALU.mult, ALU.add).then_inc(s.meaned, 1)
    dve.wait_ge(s.rooted, 1)
    nc.vector.reciprocal(m.stat[:, 3 * T:4 * T], m.stat[:, 2 * T:3 * T])
    dve.drain()
    for t in range(T):
        nc.vector.tensor_scalar(m.rows[:, t, :], g.X[:, t, :], m.stat[:, 3 * T + t:3 * T + t + 1], None,
                                ALU.mult).then_inc(s.scaled, 1)
    for k in range(1, K, 2):
        dve.wait_ge(s.turned, k + 1)
        nc.vector.tensor_scalar(g.feat[:, k, :], g.PS[:, k, :], gain[:, k:k + 1], None,
                                ALU.mult).then_inc(s.feat_v, 1)


def norm_tensor(nc, pe, g, s, m):
    for k in range(K):
        for t in range(T):
            if k == 0:
                pe.wait_ge(s.scaled, t + 1)
            last = nc.tensor.transpose(g.PS[:, k, t * P:(t + 1) * P], m.rows[:, t, k * P:(k + 1) * P],
                                       g.ident)
        last.then_inc(s.turned, 1)
    pe.wait_ge(s.feat_a, FEAT_EACH)
    pe.wait_ge(s.feat_v, FEAT_EACH)


def to_feat(nc, g, out, weight, c0, width=P):
    for k in range(K):
        last = nc.tensor.matmul(out, weight[:, k, c0:c0 + width], g.feat[:, k, :], start=k == 0, stop=k == K - 1)
    return last


def to_rows(nc, g, out, weight, t, c0, width):
    for k in range(K):
        last = nc.tensor.matmul(out, g.feat[:, k, t * P:(t + 1) * P], weight[:, k, c0:c0 + width],
                                start=k == 0, stop=k == K - 1)
    return last


def gate_tensor(nc, pe, g, s, slabs, loaded):
    n = 0
    for i, slab in enumerate(slabs):
        pe.wait_ge(loaded[i], 16)
        for t in range(T):
            if n >= 8:
                pe.wait_ge(s.gate_on, n - 7)
            to_rows(nc, g, g.PS[:, n % 8, :], slab, t, 0, 512).then_inc(s.gate_full, 1)
            n += 1


def gate_scalar(nc, act, g, s, buf, funcs):
    n = 0
    for func in funcs:
        for t in range(T):
            act.wait_ge(s.gate_full, n + 1)
            if n >= 4:
                act.wait_ge(s.gated, n - 3)
            nc.scalar.activation(buf[:, n % 4, :], g.PS[:, n % 8, :], func).then_inc(s.gate_on, 1)
            n += 1


def gate_vector(nc, dve, s, buf, y, halves):
    n = 0
    for half in halves:
        for t in range(T):
            dve.wait_ge(s.gate_on, n + 1)
            part = y[:, t, half * 512:(half + 1) * 512]
            dve.drain()
            nc.vector.tensor_tensor(part, part, buf[:, n % 4, :], ALU.mult).then_inc(s.gated, 1)
            n += 1


def setup(nc, g, a):
    with memory(nc, "setup") as mem, stage(nc, "setup", "x_in const_in pos_in wrapped table") as (block, s):
        pos_i = mem("pos_i", [P, S], I32)
        pos = mem("pos", [P, S])
        ang = mem("ang", [P, 4, S])
        turn = mem("turn", [P, 4, S])
        whole = mem("whole", [P, 4, S], I32)

        @block.sync
        def _(sp):
            sp.dma_start(g.C[:, :], a.consts).then_inc(s.const_in, 16)
            sp.dma_start(pos_i[:, :], a.positions[0, :].partition_broadcast(P)).then_inc(s.pos_in, 16)
            sp.dma_start(g.X[:, :, :], a.x[0].rearrange("(t p) d -> p t d", p=P)).then_inc(s.x_in, 16)
            sp.wait_ge(s.x_in, 16)

        @block.vector
        def _(dve):
            dve.wait_ge(s.pos_in, 16)
            dve.wait_ge(s.const_in, 16)
            nc.vector.tensor_copy(pos[:, :], pos_i[:, :])
            dve.drain()
            for n in range(4):
                nc.vector.tensor_scalar(ang[:, n, :], pos[:, :], g.freq[:, n // 2:n // 2 + 1], None, ALU.mult)
            dve.drain()
            for n in range(4):
                nc.vector.tensor_scalar(turn[:, n, :], ang[:, n, :], 1.0 / (2 * np.pi), 0.25 * (1 - n % 2),
                                        ALU.mult, ALU.add)
            dve.drain()
            nc.vector.tensor_copy(whole[:, :, :], turn[:, :, :])
            dve.drain()
            nc.vector.tensor_copy(turn[:, :, :], whole[:, :, :])
            dve.drain()
            for part in (6.28125, 2 * np.pi - 6.28125):
                nc.vector.scalar_tensor_tensor(ang[:, :, :], turn[:, :, :], -part, ang[:, :, :], ALU.mult, ALU.add)
                dve.drain()
            for n in (0, 2):
                nc.vector.tensor_scalar(ang[:, n, :], ang[:, n, :], float(np.pi / 2), None, ALU.add)
            dve.drain()
            edge = 3.1415925
            nc.vector.tensor_scalar(ang[:, :, :], ang[:, :, :], edge, -edge, ALU.min, ALU.max).then_inc(s.wrapped, 1)

        @block.scalar
        def _(act):
            act.wait_ge(s.wrapped, 1)
            nc.scalar.activation(g.TAB[:, :, :], ang[:, :, :], ACT.Sin).then_inc(s.table, 1)


def rotary_vector(nc, dst, raw, rot, cos, sin, dve, tmp):
    nc.vector.tensor_tensor(tmp, rot, sin, ALU.mult)
    nc.vector.tensor_tensor(dst, raw, cos, ALU.mult)
    dve.drain()
    return nc.vector.tensor_tensor(dst, dst, tmp, ALU.add)


def mixer_inputs(nc, g, a, layer):
    names = NORM_SEMS + """ gain_in small_in kv_in qi_in row_in small_full small_done v_full v_done
        proj_full raw_done rot_full roped ki_squared ki_rooted ki_ready parted soft_e
        score_full relu_done summed"""
    with memory(nc, "inputs") as mem, stage(nc, "inputs", names) as (block, s):
        m = Norm(rows=g.YA, stat=mem("stat", [P, 4 * T]))
        gain = mem("gain", [P, K])
        w_small = mem("w_small", [P, K, 2 * SMALL])
        w_kv = mem("w_kv", [P, K, 512])
        w_qi = mem("w_qi", [P, K, 512])
        small = mem("small", [P, T, 2 * SMALL])
        raw = mem("raw", [P, 2, S])
        tmp = mem("tmp", [P, S])
        qi = mem("qi", [P, IDX_HEADS // 2, S])
        ki = mem("ki", [P, 2, S])
        ki_rows = mem("ki_rows", [P, T, 2, P])
        ki_sq = mem("ki_sq", [P, T, IDX_DIM])
        ki_gain = mem("ki_gain", [P, IDX_DIM])
        wi = mem("wi", [P, T, IDX_HEADS])
        rowp = mem("rowp", [P, 2 * HEADS])
        soft = mem("soft", [P, 6, T * HEADS])
        relu = mem("relu", [P, 4, S])
        top8 = mem("top8", [P, 8])
        UNITS = [("k", j) for j in range(KV_HEADS)] + [("q", j) for j in range(IDX_HEADS // 2)] + \
                [("i", j) for j in range(2)]

        @block.sync
        def _(sp):
            sp.dma_start(gain[:, :], a.norm_gain[layer]).then_inc(s.gain_in, 16)
            sp.dma_start(w_small[:, :, 0:SMALL], a.w_in[layer][:, :, C_KI:C_KI + SMALL]).then_inc(s.small_in, 16)
            sp.dma_start(w_small[:, :, SMALL:], a.w_in[layer][:, :, C_BETA:C_BETA + SMALL]).then_inc(s.small_in, 16)
            sp.dma_start(w_kv[:, :, :], a.w_in[layer][:, :, C_K:C_Z]).then_inc(s.kv_in, 16)
            sp.dma_start(w_qi[:, :, :], a.w_in[layer][:, :, C_QI:C_KI]).then_inc(s.qi_in, 16)
            sp.dma_start(ki_gain[:, :], a.idx_k_gain[layer].partition_broadcast(P)).then_inc(s.row_in, 16)
            sp.dma_start(rowp[:, 0:HEADS], a.dt_bias[layer].partition_broadcast(P)).then_inc(s.row_in, 16)
            sp.dma_start(rowp[:, HEADS:], a.a_log[layer].partition_broadcast(P)).then_inc(s.row_in, 16)

        @block.tensor
        def _(pe):
            norm_tensor(nc, pe, g, s, m)
            pe.wait_ge(s.small_in, 32)
            for t in range(T):
                to_rows(nc, g, g.PS[:, 4 + t, 0:2 * SMALL], w_small, t, 0, 2 * SMALL).then_inc(s.small_full, 1)
            pe.wait_ge(s.kv_in, 16)
            for t in range(T):
                pe.wait_ge(s.small_done, t + 1)
                to_rows(nc, g, g.PS[:, 4 + t, 0:256], w_kv, t, 256, 256).then_inc(s.v_full, 1)

            def project(u):
                kind, j = UNITS[u]
                if u >= 2:
                    pe.wait_ge(s.raw_done, u - 1)
                if kind == "k":
                    to_feat(nc, g, g.PS[:, u % 2, :], w_kv, j * P).then_inc(s.proj_full, 1)
                elif kind == "q":
                    if j == 0:
                        pe.wait_ge(s.qi_in, 16)
                    to_feat(nc, g, g.PS[:, u % 2, :], w_qi, j * P).then_inc(s.proj_full, 1)
                else:
                    if j == 0:
                        pe.wait_ge(s.ki_ready, 1)
                    for t in range(T):
                        last = nc.tensor.transpose(g.PS[:, u % 2, t * P:(t + 1) * P], ki_rows[:, t, j, :], g.ident)
                    last.then_inc(s.proj_full, 1)

            project(0)
            for u, (kind, _j) in enumerate(UNITS):
                if u + 1 < len(UNITS):
                    project(u + 1)
                pe.wait_ge(s.raw_done, u + 1)
                if u >= 2:
                    pe.wait_ge(s.roped, u - 1)
                nc.tensor.matmul(g.PS[:, 2 + u % 2, :], g.rot_a if kind == "k" else g.rot_i, raw[:, u % 2, :],
                                 start=True, stop=True).then_inc(s.rot_full, 1)
            pe.wait_ge(s.roped, len(UNITS))
            pe.wait_ge(s.v_done, T)
            n = 0
            for tb in range(1, T):
                keys = P * (tb + 1)
                for h in range(IDX_HEADS):
                    if n >= 8:
                        pe.wait_ge(s.relu_done, n - 7)
                    nc.tensor.matmul(g.PS[:, n % 8, 0:keys], qi[:, h // 2, tb * P:(tb + 1) * P],
                                     ki[:, h % 2, 0:keys], start=True, stop=True).then_inc(s.score_full, 1)
                    n += 1

        @block.scalar
        def _(act):
            act.wait_ge(s.gain_in, 16)
            norm_scalar(nc, act, g, s, m, gain)
            for t in range(T):
                act.wait_ge(s.small_full, t + 1)
                nc.scalar.activation(small[:, t, :], g.PS[:, 4 + t, 0:2 * SMALL], ACT.Copy).then_inc(s.small_done, 1)
            for t in range(T):
                act.wait_ge(s.v_full, t + 1)
                nc.scalar.activation(g.V[:, t, :], g.PS[:, 4 + t, 0:256], ACT.Copy).then_inc(s.v_done, 1)
            act.wait_ge(s.ki_squared, 1)
            nc.scalar.activation(m.stat[:, 2 * T:3 * T], m.stat[:, T:2 * T], ACT.Sqrt).then_inc(s.ki_rooted, 1)
            for u in range(len(UNITS)):
                act.wait_ge(s.proj_full, u + 1)
                if u >= 2:
                    act.wait_ge(s.roped, u - 1)
                nc.scalar.activation(raw[:, u % 2, :], g.PS[:, u % 2, :], ACT.Copy).then_inc(s.raw_done, 1)
            n = 0
            for tb in range(1, T):
                keys = P * (tb + 1)
                for h in range(IDX_HEADS):
                    act.wait_ge(s.score_full, n + 1)
                    if n >= 4:
                        act.wait_ge(s.summed, n - 3)
                    nc.scalar.activation(relu[:, n % 4, 0:keys], g.PS[:, n % 8, 0:keys],
                                         ACT.Relu).then_inc(s.relu_done, 1)
                    n += 1
            for t in range(T):
                nc.scalar.activation(g.beta[:, t, :], small[:, t, SMALL:SMALL + HEADS], ACT.Sigmoid)
            act.wait_ge(s.parted, 1)
            act.wait_ge(s.row_in, 48)
            nc.scalar.activation(soft[:, 2, :], soft[:, 1, :], ACT.Exp, scale=-1.0)
            nc.scalar.activation(soft[:, 4, 0:HEADS], rowp[:, HEADS:], ACT.Exp).then_inc(s.soft_e, 1)

        @block.vector
        def _(dve):
            dve.wait_ge(s.gain_in, 16)
            norm_vector(nc, dve, g, s, m, gain)
            nc.vector.memset(ki_rows[:, :, :, :], 0.0)
            dve.wait_ge(s.small_done, T)
            dve.wait_ge(s.row_in, 48)
            nc.vector.tensor_tensor(ki_sq[:, :, :], small[:, :, 0:IDX_DIM], small[:, :, 0:IDX_DIM], ALU.mult)
            nc.vector.tensor_scalar(wi[:, :, :], small[:, :, IDX_DIM:SMALL],
                                    IDX_HEADS ** -0.5 * IDX_DIM ** -0.5, None, ALU.mult)
            dve.drain()
            nc.vector.tensor_reduce(m.stat[:, 0:T], ki_sq[:, :, :], AX.X, ALU.add)
            dve.drain()
            nc.vector.tensor_scalar(m.stat[:, T:2 * T], m.stat[:, 0:T], 1.0 / IDX_DIM, EPS,
                                    ALU.mult, ALU.add).then_inc(s.ki_squared, 1)
            dve.wait_ge(s.ki_rooted, 1)
            nc.vector.reciprocal(m.stat[:, 3 * T:4 * T], m.stat[:, 2 * T:3 * T])
            dve.drain()
            nc.vector.tensor_tensor(ki_sq[:, :, :], small[:, :, 0:IDX_DIM], over(m.stat[:, 3 * T:4 * T], IDX_DIM),
                                    ALU.mult)
            dve.drain()
            for j in range(2):
                last = nc.vector.tensor_tensor(ki_rows[:, :, j, j * IDX_DIM:(j + 1) * IDX_DIM], ki_sq[:, :, :],
                                               each(ki_gain[:, :], T), ALU.mult)
            dve.drain().then_inc(s.ki_ready, 1)
            for u, (kind, j) in enumerate(UNITS):
                dve.wait_ge(s.rot_full, u + 1)
                dst = {"k": g.KT, "q": qi, "i": ki}[kind][:, j, :]
                table = 0 if kind == "k" else 2
                rotary_vector(nc, dst, raw[:, u % 2, :], g.PS[:, 2 + u % 2, :], g.TAB[:, table, :],
                              g.TAB[:, table + 1, :], dve, tmp[:, :]).then_inc(s.roped, 1)
                dve.drain()
            nc.vector.tensor_copy(g.BIAS[:, 0:P], g.causal)
            n = 0
            for tb in range(1, T):
                keys, at = P * (tb + 1), g.bias_at[tb]
                score = g.BIAS[:, at:at + keys]
                for h in range(IDX_HEADS):
                    dve.wait_ge(s.relu_done, n + 1)
                    w = wi[:, tb, h:h + 1]
                    if h == 0:
                        nc.vector.tensor_scalar(score, relu[:, n % 4, 0:keys], w, None, ALU.mult).then_inc(s.summed, 1)
                    else:
                        nc.vector.scalar_tensor_tensor(score, relu[:, n % 4, 0:keys], w, score, ALU.mult,
                                                       ALU.add).then_inc(s.summed, 1)
                    dve.drain()
                    n += 1
                edge = g.BIAS[:, at + keys - P:at + keys]
                nc.vector.tensor_tensor(edge, edge, g.causal, ALU.add)
                dve.drain()
            for tb in range(1, T):
                keys, at = P * (tb + 1), g.bias_at[tb]
                score = g.BIAS[:, at:at + keys]
                for _round in range(TOPK // 8):
                    nc.vector.max(top8[:, :], score)
                    dve.drain()
                    nc.vector.match_replace(score, top8[:, :], score, TAKEN)
                    dve.drain()
                nc.vector.tensor_scalar(score, score, -2e38, NEVER, ALU.is_gt, ALU.mult)
            dve.wait_ge(s.row_in, 48)
            nc.vector.tensor_tensor(soft[:, 0, :].rearrange("p (t h) -> p t h", t=T),
                                    small[:, :, SMALL + HEADS:SMALL + 2 * HEADS], each(rowp[:, 0:HEADS], T), ALU.add)
            dve.drain()
            nc.vector.scalar_tensor_tensor(soft[:, 1, :], soft[:, 0, :], -1.0, soft[:, 0, :], ALU.mult, ALU.max)
            dve.drain().then_inc(s.parted, 1)
            dve.wait_ge(s.soft_e, 1)
            log1p_vector(nc, dve, soft[:, 2, :], soft[:, 3, :], soft[:, 5, :], soft[:, 1, :])
            nc.vector.scalar_tensor_tensor(soft[:, 0, :], soft[:, 0, :], 0.0, soft[:, 2, :], ALU.max, ALU.add)
            dve.drain()
            nc.vector.scalar_tensor_tensor(g.decay[:, :, :], soft[:, 0, :].rearrange("p (t h) -> p t h", t=T), -1.0,
                                           each(soft[:, 4, 0:HEADS], T), ALU.mult, ALU.mult)


def log1p_vector(nc, dve, x, z, z2, acc):
    nc.vector.tensor_scalar(z, x, 2.0, None, ALU.add)
    dve.drain()
    nc.vector.reciprocal(z, z)
    dve.drain()
    nc.vector.tensor_tensor(z, z, x, ALU.mult)
    dve.drain()
    nc.vector.tensor_tensor(z2, z, z, ALU.mult)
    dve.drain()
    nc.vector.tensor_scalar(acc, z2, 1.0 / 15, 1.0 / 13, ALU.mult, ALU.add)
    dve.drain()
    for odd in (11, 9, 7, 5, 3, 1):
        nc.vector.tensor_tensor(acc, acc, z2, ALU.mult)
        dve.drain()
        nc.vector.tensor_scalar(acc, acc, 1.0 / odd, None, ALU.add)
        dve.drain()
    nc.vector.scalar_tensor_tensor(x, acc, 2.0, z, ALU.mult, ALU.mult)
    dve.drain()


def attention(nc, g, a, layer):
    names = """wq0 wq1 wz0 wz1 wz2 wz3 proj_full raw_done rot_full roped score_full masked max_done exp_done
        turned turned_done out_full out_done gate_full gate_on gated w_free"""
    scale = DH ** -0.5
    with memory(nc, "attn") as mem, stage(nc, "attn", names) as (block, s):
        loaded = (s.wz0, s.wz1, s.wz2, s.wz3)
        w = [mem(f"w{i}", [P, K, 512]) for i in range(4)]
        q_raw = mem("q_raw", [P, S])
        tmp = mem("tmp", [P, S])
        qt = mem("qt", [P, 2, S])
        score = mem("score", [P, 2, S])
        prob = mem("prob", [P, 2, S])
        prob_t = mem("prob_t", [P, 2, S])
        neg_max = mem("neg_max", [P, HEADS * T])
        total = mem("total", [P, HEADS * T])
        part = mem("part", [P, 4, 512])
        steps = [(h, tb) for h in range(HEADS) for tb in range(T)]
        N = len(steps)

        @block.sync
        def _(sp):
            for i, sem in enumerate((s.wq0, s.wq1)):
                sp.dma_start(w[i][:, :, :], a.w_in[layer][:, :, C_Q + i * 512:C_Q + (i + 1) * 512]).then_inc(sem, 16)
            for i, c in enumerate((C_Z, C_Z + 512)):
                sp.dma_start(w[2 + i][:, :, :], a.w_in[layer][:, :, c:c + 512]).then_inc(loaded[i], 16)
            sp.wait_ge(s.proj_full, HEADS)
            for i, c in enumerate((C_GATE, C_GATE + 512)):
                sp.dma_start(w[i][:, :, :], a.w_in[layer][:, :, c:c + 512]).then_inc(loaded[2 + i], 16)

        @block.tensor
        def _(pe):
            def project(h):
                if h % GROUP == 0:
                    pe.wait_ge((s.wq0, s.wq1)[h // GROUP], 16)
                if h >= 1:
                    pe.wait_ge(s.raw_done, h)
                to_feat(nc, g, g.PS[:, 0, :], w[h // GROUP], (h % GROUP) * P).then_inc(s.proj_full, 1)

            def rotate(h):
                pe.wait_ge(s.raw_done, h + 1)
                if h >= 1:
                    pe.wait_ge(s.roped, h)
                nc.tensor.matmul(g.PS[:, 1, :], g.rot_a, q_raw[:, :], start=True, stop=True).then_inc(s.rot_full, 1)

            def turn(n):
                tb = steps[n][1]
                pe.wait_ge(s.exp_done, n + 1)
                if n >= 2:
                    pe.wait_ge(s.turned_done, n - 1)
                for kb in range(tb + 1):
                    last = nc.tensor.transpose(g.PS[:, 4 + n % 2, kb * P:(kb + 1) * P],
                                               prob[:, n % 2, kb * P:(kb + 1) * P], g.ident)
                last.then_inc(s.turned, 1)

            def weigh(n):
                h, tb = steps[n]
                v0 = (h // GROUP) * DH
                pe.wait_ge(s.turned_done, n + 1)
                if n >= 2:
                    pe.wait_ge(s.out_done, n - 1)
                for kb in range(tb + 1):
                    last = nc.tensor.matmul(g.PS[:, 6 + n % 2, 0:DH], prob_t[:, n % 2, kb * P:(kb + 1) * P],
                                            g.V[:, kb, v0:v0 + DH], start=kb == 0, stop=kb == tb)
                last.then_inc(s.out_full, 1)

            project(0)
            rotate(0)
            for n, (h, tb) in enumerate(steps):
                if tb == 0:
                    pe.wait_ge(s.roped, h + 1)
                if n >= 2:
                    pe.wait_ge(s.masked, n - 1)
                keys = P * (tb + 1)
                nc.tensor.matmul(g.PS[:, 2 + n % 2, 0:keys], qt[:, h % 2, tb * P:(tb + 1) * P],
                                 g.KT[:, h // GROUP, 0:keys], start=True, stop=True).then_inc(s.score_full, 1)
                if tb == 0 and h + 1 < HEADS:
                    project(h + 1)
                if tb == 2 and h + 1 < HEADS:
                    rotate(h + 1)
                if n >= 1:
                    turn(n - 1)
                if n >= 2:
                    weigh(n - 2)
            turn(N - 1)
            weigh(N - 2)
            weigh(N - 1)
            pe.wait_ge(s.out_done, N)
            gate_tensor(nc, pe, g, s, [w[2], w[3], w[0], w[1]], loaded)

        @block.scalar
        def _(act):
            def keep(h):
                act.wait_ge(s.proj_full, h + 1)
                if h >= 1:
                    act.wait_ge(s.roped, h)
                nc.scalar.activation(q_raw[:, :], g.PS[:, 0, :], ACT.Copy).then_inc(s.raw_done, 1)

            def move(n):
                keys = P * (steps[n][1] + 1)
                act.wait_ge(s.turned, n + 1)
                if n >= 2:
                    act.wait_ge(s.out_full, n - 1)
                nc.scalar.activation(prob_t[:, n % 2, 0:keys], g.PS[:, 4 + n % 2, 0:keys],
                                     ACT.Copy).then_inc(s.turned_done, 1)

            keep(0)
            for n, (h, tb) in enumerate(steps):
                keys = P * (tb + 1)
                act.wait_ge(s.max_done, n + 1)
                if n >= 2:
                    act.wait_ge(s.turned, n - 1)
                nc.scalar.activation(prob[:, n % 2, 0:keys], score[:, n % 2, 0:keys], ACT.Exp,
                                     bias=neg_max[:, n:n + 1], accum_out=total[:, n:n + 1]).then_inc(s.exp_done, 1)
                if tb == 1 and h + 1 < HEADS:
                    keep(h + 1)
                if n >= 1:
                    move(n - 1)
            move(N - 1)
            gate_scalar(nc, act, g, s, part, [ACT.Silu] * 2 + [ACT.Sigmoid] * 2)

        @block.vector
        def _(dve):
            def rope(h):
                dve.wait_ge(s.rot_full, h + 1)
                if h >= 2:
                    dve.wait_ge(s.score_full, T * (h - 1))
                rotary_vector(nc, qt[:, h % 2, :], q_raw[:, :], g.PS[:, 1, :], g.TAB[:, 0, :], g.TAB[:, 1, :],
                              dve, tmp[:, :]).then_inc(s.roped, 1)

            def finish(n):
                h, tb = steps[n]
                dve.wait_ge(s.out_full, n + 1)
                nc.vector.reciprocal(total[:, n:n + 1], total[:, n:n + 1])
                dve.drain()
                nc.vector.tensor_scalar(g.YA[:, tb, h * DH:(h + 1) * DH], g.PS[:, 6 + n % 2, 0:DH],
                                        total[:, n:n + 1], None, ALU.mult).then_inc(s.out_done, 1)

            rope(0)
            for n, (h, tb) in enumerate(steps):
                keys, at = P * (tb + 1), g.bias_at[tb]
                dve.wait_ge(s.score_full, n + 1)
                if n >= 2:
                    dve.wait_ge(s.exp_done, n - 1)
                nc.vector.scalar_tensor_tensor(score[:, n % 2, 0:keys], g.PS[:, 2 + n % 2, 0:keys], scale,
                                               g.BIAS[:, at:at + keys], ALU.mult, ALU.add).then_inc(s.masked, 1)
                dve.drain()
                nc.vector.tensor_reduce(neg_max[:, n:n + 1], score[:, n % 2, 0:keys], AX.X, ALU.max,
                                        negate=True).then_inc(s.max_done, 1)
                if tb == 3 and h + 1 < HEADS:
                    rope(h + 1)
                if n >= 2:
                    finish(n - 2)
            finish(N - 2)
            finish(N - 1)
            gate_vector(nc, dve, s, part, g.YA, [0, 1, 0, 1])


def delta_heads(nc, g, a, layer, pair):
    names = """w0 w1 cw_in proj_full padded silu_done conv_done q_squared k_turned v_turned norm_in stat_done root_done
        factors cum_full cum_copied rows_full diag_done clipped decayed qk_full kk_full masks_done first_full
        y_full y_done xy_full yx_full xt_done x_done x_sub xt_sub dk_done
        ks_full r_done vn_full vn_done qs_full o_full o_done su_full s_done"""
    A2 = range(2)
    with memory(nc, "delta") as mem, stage(nc, "delta", names) as (block, s):
        w = [mem(f"w{i}", [P, K, 3, P]) for i in A2]
        cw = mem("cw", [P, 2, 3, CONV])
        pad = mem("pad", [P, 2, 3, S + CONV - 1])
        cv = mem("cv", [P, 2, 3, S])
        sq = mem("sq", [P, 2, S])
        kd = mem("kd", [P, 2, T, P])
        bv = mem("bv", [P, 2, T, P])
        st = mem("st", [P, 12, T, 2])
        cum = mem("cum", [P, 3, T, 2])
        diag = mem("diag", [P, 2, 2, S])
        et = mem("et", [P, 2, S])
        ea = mem("ea", [P, 2, S])
        qkt = mem("qkt", [P, 2, S])
        lt = mem("lt", [P, 2, S])
        x = mem("x", [P, 2, S])
        xt = mem("xt", [P, 2, S])
        y = mem("y", [P, 2, S])
        mx = mem("mx", [P, 2, S])
        mxt = mem("mxt", [P, 2, S])
        state = mem("state", [P, 2, P])
        r = mem("r", [P, 2, P])
        vn = mem("vn", [P, 2, P])
        o1 = mem("o1", [P, 2, P])
        PS = g.PS

        def tile(ap, h, t):
            return ap[:, h, t * P:(t + 1) * P]

        def tiles(ap):
            return ap.rearrange("p (t c) -> p t c", t=T)

        end_decay = cum[:, 2, :, :]

        @block.sync
        def _(sp):
            sp.dma_start(cw[:, :, :, :], a.conv_w[layer, pair]).then_inc(s.cw_in, 16)
            for h, sem in zip(A2, (s.w0, s.w1)):
                for k in range(K):
                    sp.dma_start(w[h][:, k, :, :], a.w_heads[layer, pair][h, k]).then_inc(sem, 16)

        @block.tensor
        def _(pe):
            for h, sem in zip(A2, (s.w0, s.w1)):
                pe.wait_ge(sem, 16 * K)
                for j in range(3):
                    for k in range(K):
                        last = nc.tensor.matmul(PS[:, 3 * h + j, :], w[h][:, k, j, :], g.feat[:, k, :],
                                                start=k == 0, stop=k == K - 1)
                    last.then_inc(s.proj_full, 1)
            pe.wait_ge(s.dk_done, 1)
            nc.tensor.matmul(PS[:, 6, 0:2 * T], g.upto, cum[:, 0, :, :].rearrange("p t h -> p (t h)"), start=True, stop=True)
            nc.tensor.matmul(PS[:, 6, 2 * T:4 * T], g.ones, cum[:, 0, :, :].rearrange("p t h -> p (t h)"),
                             start=True, stop=True).then_inc(s.cum_full, 1)
            for h in A2:
                pe.wait_ge(s.conv_done, 3 * (h + 1))
                for t in range(T):
                    last = nc.tensor.transpose(PS[:, 3 * h, t * P:(t + 1) * P], cv[:, h, 1, t * P:(t + 1) * P], g.ident)
                last.then_inc(s.k_turned, 1)
                for t in range(T):
                    last = nc.tensor.transpose(PS[:, 3 * h + 1, t * P:(t + 1) * P], cv[:, h, 2, t * P:(t + 1) * P], g.ident)
                last.then_inc(s.v_turned, 1)
                pe.wait_ge(s.q_squared, h + 1)
                if h == 1:
                    pe.wait_ge(s.cum_copied, 1)
                for t in range(T):
                    last = nc.tensor.matmul(PS[:, 7 - h, t:t + 1], tile(sq, h, t), g.ones[:, 0:1],
                                            start=True, stop=True)
                last.then_inc(s.norm_in, 1)
            for h in A2:
                pe.wait_ge(s.diag_done, h + 1)
                for j in A2:
                    last = nc.tensor.matmul(PS[:, 2 * h + j, :], g.ones, diag[:, h, j, :], start=True, stop=True)
                last.then_inc(s.rows_full, 1)
            for h in A2:
                for j in A2:
                    for t in range(T):
                        last = nc.tensor.matmul(PS[:, 4 + 2 * h + j, t * P:(t + 1) * P],
                                                cv[:, h, 1, t * P:(t + 1) * P], cv[:, h, j, t * P:(t + 1) * P],
                                                start=True, stop=True)
                last.then_inc(s.qk_full, 1)
            for h in A2:
                pe.wait_ge(s.masks_done, h + 1)
                for t in range(T):
                    last = nc.tensor.matmul(PS[:, h, t * P:(t + 1) * P], tile(lt, h, t), g.ident, start=True, stop=True)
                last.then_inc(s.first_full, 1)
            for lvl in range(1, LEVELS):
                for h in A2:
                    pe.wait_ge(s.x_sub, 2 * (lvl - 1) + h + 1)
                    for t in range(T):
                        last = nc.tensor.matmul(PS[:, 2 + h, t * P:(t + 1) * P], tile(lt, h, t), tile(x, h, t),
                                                start=True, stop=True)
                    last.then_inc(s.y_full, 1)
                for h in A2:
                    n = 2 * (lvl - 1) + h
                    pe.wait_ge(s.y_done, n + 1)
                    if lvl > 1:
                        pe.wait_ge(s.xt_sub, n - 1)
                    for t in range(T):
                        last = nc.tensor.matmul(PS[:, 4 + h, t * P:(t + 1) * P], tile(y, h, t), tile(xt, h, t),
                                                start=True, stop=True)
                    last.then_inc(s.yx_full, 1)
                    if lvl < LEVELS - 1:
                        for t in range(T):
                            last = nc.tensor.matmul(PS[:, 6 + h, t * P:(t + 1) * P], tile(xt, h, t), tile(y, h, t),
                                                    start=True, stop=True)
                        last.then_inc(s.xy_full, 1)
            for t in range(T):
                for h in A2:
                    n = 2 * t + h
                    if t == 0:
                        pe.wait_ge(s.xt_sub, 2 * (LEVELS - 2) + h + 1)
                    if t > 0:
                        pe.wait_ge(s.s_done, n - 1)
                        nc.tensor.matmul(PS[:, h, 0:P], cv[:, h, 1, t * P:(t + 1) * P], state[:, h, :],
                                         start=True, stop=True).then_inc(s.ks_full, 1)
                        pe.wait_ge(s.o_done, n - 1)
                        nc.tensor.matmul(PS[:, 4 + h, 0:P], cv[:, h, 0, t * P:(t + 1) * P], state[:, h, :],
                                         start=True, stop=True).then_inc(s.qs_full, 1)
                for h in A2:
                    n = 2 * t + h
                    pe.wait_ge(s.r_done, n + 1)
                    nc.tensor.matmul(PS[:, 2 + h, 0:P], tile(xt, h, t), r[:, h, :], start=True,
                                     stop=True).then_inc(s.vn_full, 1)
                for h in A2:
                    n = 2 * t + h
                    pe.wait_ge(s.vn_done, n + 1)
                    nc.tensor.matmul(PS[:, 6 + h, P:2 * P], tile(qkt, h, t), vn[:, h, :], start=True,
                                     stop=True).then_inc(s.o_full, 1)
                    if t < T - 1:
                        nc.tensor.matmul(PS[:, 2 + h, P:2 * P], kd[:, h, t, :], vn[:, h, :], start=True,
                                         stop=True).then_inc(s.su_full, 1)

        @block.scalar
        def _(act):
            for h in A2:
                for j in range(3):
                    act.wait_ge(s.proj_full, 3 * h + j + 1)
                    nc.scalar.activation(pad[:, h, j, CONV - 1:], PS[:, 3 * h + j, :], ACT.Copy).then_inc(s.padded, 1)
            act.wait_ge(s.cum_full, 1)
            nc.scalar.activation(cum[:, 1:3, :, :].rearrange("p a t h -> p (a t h)"), PS[:, 6, 0:4 * T],
                                 ACT.Copy).then_inc(s.cum_copied, 1)
            act.drain()
            nc.scalar.activation(st[:, 10, :, :], cum[:, 1, :, :], ACT.Exp)
            for h in A2:
                for j in range(3):
                    act.wait_ge(s.silu_done, 3 * h + j + 1)
                    nc.scalar.activation(cv[:, h, j, :], cv[:, h, j, :], ACT.Silu).then_inc(s.conv_done, 1)
                act.drain()
                nc.scalar.activation(sq[:, h, :], cv[:, h, 0, :], ACT.Square).then_inc(s.q_squared, 1)
            act.wait_ge(s.stat_done, 1)
            nc.scalar.activation(st[:, 2:4, :, :], st[:, 0:2, :, :], ACT.Sqrt).then_inc(s.root_done, 1)
            act.wait_ge(s.factors, 1)
            nc.scalar.activation(st[:, 11, :, :], st[:, 11, :, :], ACT.Exp)
            nc.scalar.activation(end_decay, end_decay, ACT.Exp).then_inc(s.decayed, 1)
            for h in A2:
                act.wait_ge(s.clipped, h + 1)
                nc.scalar.activation(et[:, h, :], et[:, h, :], ACT.Exp).then_inc(s.decayed, 1)
            for lvl in range(1, LEVELS):
                for h in A2:
                    n = 2 * (lvl - 1) + h
                    act.wait_ge(s.y_full, n + 1)
                    nc.scalar.activation(y[:, h, :], PS[:, 2 + h, :], ACT.Copy).then_inc(s.y_done, 1)
            for t in range(T):
                for h in A2:
                    act.wait_ge(s.vn_full, 2 * t + h + 1)
                    if t > 0:
                        act.wait_ge(s.su_full, 2 * t + h - 1)
                        act.wait_ge(s.o_full, 2 * t + h - 1)
                    nc.scalar.activation(vn[:, h, :], PS[:, 2 + h, 0:P], ACT.Copy).then_inc(s.vn_done, 1)

        @block.vector
        def _(dve):
            for h in A2:
                nc.vector.memset(pad[:, h, :, 0:CONV - 1], 0.0)
            nc.vector.tensor_copy(cum[:, 0, :, :], g.decay[:, :, bass.ds(2 * pair, 2)])
            nc.vector.tensor_copy(g.beta_pair[:, :, :], g.beta[:, :, bass.ds(2 * pair, 2)])
            dve.drain().then_inc(s.dk_done, 1)
            dve.wait_ge(s.cw_in, 16)
            for h in A2:
                for j in range(3):
                    dve.wait_ge(s.padded, 3 * h + j + 1)
                    acc = cv[:, h, j, :]
                    nc.vector.tensor_scalar(acc, pad[:, h, j, 0:S], cw[:, h, j, 0:1], None, ALU.mult)
                    for tap in range(1, CONV):
                        dve.drain()
                        last = nc.vector.scalar_tensor_tensor(acc, pad[:, h, j, tap:tap + S], cw[:, h, j, tap:tap + 1],
                                                              acc, ALU.mult, ALU.add)
                    last.then_inc(s.silu_done, 1)
            for h in A2:
                dve.wait_ge(s.k_turned, h + 1)
                nc.vector.tensor_copy(kd[:, h, :, :], tiles(PS[:, 3 * h, :]))
                dve.wait_ge(s.v_turned, h + 1)
                nc.vector.tensor_tensor(bv[:, h, :, :], tiles(PS[:, 3 * h + 1, :]), over(g.beta_pair[:, :, h], P), ALU.mult)
                dve.drain()
                nc.vector.tensor_tensor(tiles(ea[:, h, :]), kd[:, h, :, :], kd[:, h, :, :], ALU.mult)
                dve.drain()
                nc.vector.tensor_reduce(st[:, 1, :, h], tiles(ea[:, h, :]), AX.X, ALU.add)
                dve.wait_ge(s.norm_in, h + 1)
                nc.vector.tensor_copy(st[:, 0, :, h], PS[:, 7 - h, 0:T])
            dve.drain()
            nc.vector.tensor_scalar(st[:, 0:2, :, :], st[:, 0:2, :, :], EPS, None, ALU.add)
            dve.drain().then_inc(s.stat_done, 1)
            dve.wait_ge(s.root_done, 1)
            nc.vector.reciprocal(st[:, 4:6, :, :], st[:, 2:4, :, :])
            dve.drain()
            nc.vector.tensor_scalar(st[:, 4, :, :], st[:, 4, :, :], DH ** -0.5, None, ALU.mult)
            nc.vector.tensor_tensor(st[:, 6, :, :], st[:, 5, :, :], g.beta_pair[:, :, :], ALU.mult)
            dve.wait_ge(s.cum_copied, 1)
            nc.vector.tensor_tensor(st[:, 11, :, :], end_decay, cum[:, 1, :, :], ALU.subtract)
            dve.drain().then_inc(s.factors, 1)
            for h in A2:
                nc.vector.tensor_tensor(tiles(diag[:, h, 0, :]), each(g.upto, T), over(cum[:, 0, :, h], P), ALU.mult)
                nc.vector.tensor_tensor(tiles(diag[:, h, 1, :]), each(g.ident, T), over(st[:, 6, :, h], P), ALU.mult)
                dve.drain().then_inc(s.diag_done, 1)
            dve.wait_ge(s.decayed, 1)
            nc.vector.tensor_tensor(st[:, 7, :, :], st[:, 6, :, :], st[:, 10, :, :], ALU.mult)
            nc.vector.tensor_tensor(st[:, 8, :, :], st[:, 4, :, :], st[:, 10, :, :], ALU.mult)
            nc.vector.tensor_tensor(st[:, 9, :, :], st[:, 5, :, :], st[:, 11, :, :], ALU.mult)
            dve.drain()
            nc.vector.tensor_scalar(st[:, 7, :, :], st[:, 7, :, :], -1.0, None, ALU.mult)
            for h in A2:
                nc.vector.tensor_tensor(kd[:, h, :, :], kd[:, h, :, :], over(st[:, 9, :, h], P), ALU.mult)
                dve.wait_ge(s.rows_full, h + 1)
                nc.vector.tensor_tensor(tiles(et[:, h, :]), tiles(PS[:, 2 * h, :]), over(cum[:, 1, :, h], P), ALU.subtract)
                dve.drain()
                nc.vector.tensor_scalar(et[:, h, :], et[:, h, :], 0.0, None, ALU.min)
                dve.drain().then_inc(s.clipped, 1)
            for h in A2:
                dve.wait_ge(s.decayed, h + 2)
                nc.vector.tensor_tensor(tiles(ea[:, h, :]), tiles(et[:, h, :]), over(st[:, 5, :, h], P), ALU.mult)
                dve.drain()
                nc.vector.tensor_tensor(tiles(ea[:, h, :]), tiles(ea[:, h, :]), each(g.upto, T), ALU.mult)
                dve.drain()
                dve.wait_ge(s.qk_full, h + 1)
                nc.vector.tensor_tensor(qkt[:, h, :], PS[:, 4 + 2 * h, :], ea[:, h, :], ALU.mult)
                nc.vector.tensor_tensor(lt[:, h, :], PS[:, 5 + 2 * h, :], ea[:, h, :], ALU.mult)
                dve.drain()
                nc.vector.tensor_tensor(lt[:, h, :], lt[:, h, :], PS[:, 2 * h + 1, :], ALU.mult)
                dve.drain()
                nc.vector.tensor_tensor(tiles(mxt[:, h, :]), tiles(lt[:, h, :]), each(g.up[0], T), ALU.mult)
                dve.drain()
                nc.vector.tensor_tensor(tiles(xt[:, h, :]), each(g.ident, T), tiles(mxt[:, h, :]), ALU.subtract)
                dve.drain().then_inc(s.masks_done, 1)
            for h in A2:
                dve.wait_ge(s.first_full, h + 1)
                nc.vector.tensor_tensor(tiles(mx[:, h, :]), tiles(PS[:, h, :]), each(g.low[0], T), ALU.mult)
                dve.drain()
                nc.vector.tensor_tensor(tiles(x[:, h, :]), each(g.ident, T), tiles(mx[:, h, :]), ALU.subtract).then_inc(s.x_sub, 1)
            for lvl in range(1, LEVELS):
                for h in A2:
                    n = 2 * (lvl - 1) + h
                    dve.wait_ge(s.yx_full, n + 1)
                    nc.vector.tensor_tensor(tiles(mxt[:, h, :]), tiles(PS[:, 4 + h, :]), each(g.up[lvl], T), ALU.mult)
                    if lvl < LEVELS - 1:
                        dve.wait_ge(s.xy_full, n + 1)
                        nc.vector.tensor_tensor(tiles(mx[:, h, :]), tiles(PS[:, 6 + h, :]), each(g.low[lvl], T), ALU.mult)
                        dve.drain()
                        nc.vector.tensor_tensor(x[:, h, :], x[:, h, :], mx[:, h, :], ALU.subtract).then_inc(s.x_sub, 1)
                    else:
                        dve.drain()
                    nc.vector.tensor_tensor(xt[:, h, :], xt[:, h, :], mxt[:, h, :], ALU.subtract).then_inc(s.xt_sub, 1)
            for t in range(T):
                for h in A2:
                    if t == 0:
                        nc.vector.tensor_copy(r[:, h, :], bv[:, h, t, :]).then_inc(s.r_done, 1)
                    else:
                        dve.wait_ge(s.ks_full, 2 * (t - 1) + h + 1)
                        nc.vector.scalar_tensor_tensor(r[:, h, :], PS[:, h, 0:P], st[:, 7, t, h:h + 1], bv[:, h, t, :],
                                                       ALU.mult, ALU.add).then_inc(s.r_done, 1)
                for h in A2:
                    if t < T - 1:
                        dve.wait_ge(s.su_full, 2 * t + h + 1)
                        if t == 0:
                            nc.vector.tensor_copy(state[:, h, :], PS[:, 2 + h, P:2 * P]).then_inc(s.s_done, 1)
                        else:
                            nc.vector.scalar_tensor_tensor(state[:, h, :], state[:, h, :], end_decay[:, t, h:h + 1],
                                                           PS[:, 2 + h, P:2 * P], ALU.mult, ALU.add).then_inc(s.s_done, 1)
                for h in A2:
                    dst = g.YB[:, t, bass.ds((2 * pair + h) * P, P)]
                    dve.wait_ge(s.o_full, 2 * t + h + 1)
                    if t == 0:
                        nc.vector.tensor_scalar(dst, PS[:, 6 + h, P:2 * P], st[:, 4, t, h:h + 1], None,
                                                ALU.mult).then_inc(s.o_done, 1)
                    else:
                        dve.wait_ge(s.qs_full, 2 * (t - 1) + h + 1)
                        nc.vector.tensor_scalar(o1[:, h, :], PS[:, 4 + h, 0:P], st[:, 8, t, h:h + 1], None, ALU.mult)
                        dve.drain()
                        nc.vector.scalar_tensor_tensor(dst, PS[:, 6 + h, P:2 * P], st[:, 4, t, h:h + 1], o1[:, h, :],
                                                       ALU.mult, ALU.add).then_inc(s.o_done, 1)


def out_tensor(nc, pe, g, s, feat, slabs, sems):
    n = 0
    for half in range(2):
        pe.wait_ge(sems[half], 16)
        for t in range(T):
            for k in range(K):
                last = nc.tensor.matmul(g.PS[:, n, :], feat[:, k, t * P:(t + 1) * P], slabs[half][:, k, :],
                                        start=k == 0, stop=k == K - 1)
            last.then_inc(s.out_full, 1)
            n += 1


def out_vector(nc, dve, g, s):
    n = 0
    for half in range(2):
        for t in range(T):
            dve.wait_ge(s.out_full, n + 1)
            part = g.X[:, t, half * 512:(half + 1) * 512]
            nc.vector.tensor_tensor(part, g.PS[:, n, :], part, ALU.add)
            n += 1


def merge(nc, g, a, layer):
    names = """wg0 wg1 wg2 wg3 wo0 wo1 row_in squared rooted gate_full gate_on gated mixed turned feat_a feat_v out_full"""
    with memory(nc, "merge") as mem, stage(nc, "merge", names) as (block, s):
        loaded = (s.wg0, s.wg1, s.wg2, s.wg3)
        w = [mem(f"w{i}", [P, K, 512]) for i in range(4)]
        row = mem("row", [P, DH])
        square = mem("square", [P, D])
        stat = mem("stat", [P, 4, T * HEADS])
        part = mem("part", [P, 4, 512])
        GATES = (C_ZB, C_ZB + 512, C_GATE + D, C_GATE + D + 512)

        @block.sync
        def _(sp):
            sp.dma_start(row[:, :], a.gdn_norm_gain[layer].partition_broadcast(P)).then_inc(s.row_in, 16)
            for i, c in enumerate(GATES):
                sp.dma_start(w[i][:, :, :], a.w_in[layer][:, :, c:c + 512]).then_inc(loaded[i], 16)
            for half, sem in enumerate((s.wo0, s.wo1)):
                sp.wait_ge(s.gate_full, T * (half + 1))
                sp.dma_start(w[half][:, :, :], a.w_out[layer][:, :, half * 512:(half + 1) * 512]).then_inc(sem, 16)

        @block.tensor
        def _(pe):
            gate_tensor(nc, pe, g, s, w, loaded)
            for k in range(K):
                for t in range(T):
                    if k == 0:
                        pe.wait_ge(s.mixed, t + 1)
                    last = nc.tensor.transpose(g.PS[:, k, t * P:(t + 1) * P], g.YA[:, t, k * P:(k + 1) * P], g.ident)
                last.then_inc(s.turned, 1)
            pe.wait_ge(s.feat_a, FEAT_EACH)
            pe.wait_ge(s.feat_v, FEAT_EACH)
            out_tensor(nc, pe, g, s, g.feat, w, (s.wo0, s.wo1))

        @block.scalar
        def _(act):
            act.wait_ge(s.squared, 1)
            nc.scalar.activation(stat[:, 2, :], stat[:, 1, :], ACT.Sqrt).then_inc(s.rooted, 1)
            gate_scalar(nc, act, g, s, part, [ACT.Silu] * 2 + [ACT.Sigmoid] * 2)
            for k in range(0, K, 2):
                act.wait_ge(s.turned, k + 1)
                nc.scalar.activation(g.feat[:, k, :], g.PS[:, k, :], ACT.Copy).then_inc(s.feat_a, 1)

        @block.vector
        def _(dve):
            for t in range(T):
                nc.vector.tensor_tensor(square[:, :], g.YB[:, t, :], g.YB[:, t, :], ALU.mult)
                dve.drain()
                nc.vector.tensor_reduce(stat[:, 0, t * HEADS:(t + 1) * HEADS],
                                        square[:, :].rearrange("p (h c) -> p h c", h=HEADS), AX.X, ALU.add)
                dve.drain()
            nc.vector.tensor_scalar(stat[:, 1, :], stat[:, 0, :], 1.0 / DH, EPS, ALU.mult, ALU.add).then_inc(s.squared, 1)
            dve.wait_ge(s.rooted, 1)
            nc.vector.reciprocal(stat[:, 3, :], stat[:, 2, :])
            dve.wait_ge(s.row_in, 16)
            dve.drain()
            for t in range(T):
                y = g.YB[:, t, :].rearrange("p (h c) -> p h c", h=HEADS)
                nc.vector.tensor_tensor(y, y, over(stat[:, 3, t * HEADS:(t + 1) * HEADS], DH), ALU.mult)
                dve.drain()
                nc.vector.tensor_tensor(y, y, each(row[:, :], HEADS), ALU.mult)
            gate_vector(nc, dve, s, part, g.YB, [0, 1, 0, 1])
            dve.drain()
            for t in range(T):
                nc.vector.tensor_tensor(g.YA[:, t, :], g.YA[:, t, :], g.YB[:, t, :], ALU.add).then_inc(s.mixed, 1)
            for k in range(1, K, 2):
                dve.wait_ge(s.turned, k + 1)
                nc.vector.tensor_copy(g.feat[:, k, :], g.PS[:, k, :]).then_inc(s.feat_v, 1)
            out_vector(nc, dve, g, s)


def short_conv(nc, g, a, layer):
    names = NORM_SEMS + " gain_in taps_in w0 w1 w2 wo0 wo1 full c_done tile_done out_full"
    with memory(nc, "conv") as mem, stage(nc, "conv", names) as (block, s):
        m = Norm(rows=g.YA, stat=mem("stat", [P, 4 * T]))
        gain = mem("gain", [P, K])
        taps = mem("taps", [P, K, 3])
        w = [g.W[i][:, 0:K * 3 * P].rearrange("p (k s c) -> p k s c", k=K, s=3) for i in range(3)]
        w_sems = (s.w0, s.w1, s.w2)
        wo = [slab(g.W[3 + i]) for i in range(2)]
        c = mem("c", [P, 2, S])
        pad = mem("pad", [P, S + 2])
        u = mem("u", [P, S])
        out = g.YA[:, :, :].rearrange("p t d -> p (t d)").rearrange("p (k t) -> p k t", k=K)

        @block.sync
        def _(sp):
            sp.dma_start(gain[:, :], a.norm_mix[layer]).then_inc(s.gain_in, 16)
            sp.dma_start(taps[:, :, :], a.conv_a).then_inc(s.taps_in, 16)
            for f in range(K):
                if f >= 3:
                    sp.wait_ge(s.full, f - 2)
                for k in range(K):
                    sp.dma_start(w[f % 3][:, k, :, :], a.w_in_a[f, k]).then_inc(w_sems[f % 3], 16)
            for half, sem in enumerate((s.wo0, s.wo1)):
                sp.dma_start(wo[half][:, :, :], a.w_out_a[:, :, half * 512:(half + 1) * 512]).then_inc(sem, 16)

        @block.tensor
        def _(pe):
            norm_tensor(nc, pe, g, s, m)
            for f in range(K):
                pe.wait_ge(w_sems[f % 3], 16 * K * (f // 3 + 1))
                if f >= 2:
                    pe.wait_ge(s.tile_done, f - 1)
                for j in range(3):
                    for k in range(K):
                        last = nc.tensor.matmul(g.PS[:, 3 * (f % 2) + j, :], w[f % 3][:, k, j, :], g.feat[:, k, :],
                                                start=k == 0, stop=k == K - 1)
                last.then_inc(s.full, 1)
            pe.wait_ge(s.tile_done, K)
            out_tensor(nc, pe, g, s, out, wo, (s.wo0, s.wo1))

        @block.scalar
        def _(act):
            act.wait_ge(s.gain_in, 16)
            norm_scalar(nc, act, g, s, m, gain)
            for f in range(K):
                act.wait_ge(s.full, f + 1)
                if f >= 2:
                    act.wait_ge(s.tile_done, f - 1)
                nc.scalar.activation(c[:, f % 2, :], g.PS[:, 3 * (f % 2) + 1, :], ACT.Copy).then_inc(s.c_done, 1)

        @block.vector
        def _(dve):
            dve.wait_ge(s.gain_in, 16)
            norm_vector(nc, dve, g, s, m, gain)
            nc.vector.memset(pad[:, 0:1], 0.0)
            nc.vector.memset(pad[:, S + 1:S + 2], 0.0)
            dve.wait_ge(s.taps_in, 16)
            for f in range(K):
                dve.wait_ge(s.c_done, f + 1)
                nc.vector.tensor_tensor(pad[:, 1:S + 1], c[:, f % 2, :], g.PS[:, 3 * (f % 2) + 2, :], ALU.mult)
                dve.drain()
                nc.vector.tensor_scalar(u[:, :], pad[:, 0:S], taps[:, f, 0:1], None, ALU.mult)
                for tap in (1, 2):
                    dve.drain()
                    nc.vector.scalar_tensor_tensor(u[:, :], pad[:, tap:tap + S], taps[:, f, tap:tap + 1], u[:, :],
                                                   ALU.mult, ALU.add)
                dve.drain()
                nc.vector.tensor_tensor(out[:, f, :], u[:, :], g.PS[:, 3 * (f % 2), :], ALU.mult).then_inc(s.tile_done, 1)
            out_vector(nc, dve, g, s)


LRU_BLOCKS = 4
LRU = D // LRU_BLOCKS
RG_C = 8.0


def rg_lru(nc, g, a, layer):
    names = NORM_SEMS + """ gain_in cols_in wb0 wb1 wg0 wg1 wo0 wo1 neg_abs exp_lam yu_full y_done u_done conv_done
        ri_full r_done i_done a_done th_done root_in root_done scanned tile_done out_full"""
    with memory(nc, "lru") as mem, stage(nc, "lru", names) as (block, s):
        m = Norm(rows=g.YA, stat=mem("stat", [P, 4 * T]))
        gain = mem("gain", [P, K])
        cols = mem("cols", [P, 11, K])
        wb = [g.W[i][:, :].rearrange("p (k a c) -> p k a c", k=K, a=2) for i in range(2)]
        wg = [g.W[2 + i][:, 0:8 * LRU].rearrange("p (k a c) -> p k a c", k=2, a=4) for i in range(2)]
        wo = wb
        rate = mem("rate", [P, 6, 2 * K])
        pad = mem("pad", [P, 2, S + CONV - 1])
        y, u, r, i_ = (slab(g.W[4])[:, n:n + 2, :] for n in range(0, 8, 2))
        aa, th = (slab(g.W[5])[:, n:n + 2, :] for n in (0, 2))
        h = g.W[5][:, 4 * S:].rearrange("p (d e c) -> p d e c", d=2, e=2)
        out = g.YA[:, :, :].rearrange("p t d -> p (t d)").rearrange("p (k t) -> p k t", k=K)
        NB = LRU_BLOCKS

        def wo_slab(half):
            return wo[half][:, :, :, :].rearrange("p k a b -> p k (a b)")

        @block.sync
        def _(sp):
            sp.dma_start(gain[:, :], a.norm_mix[layer]).then_inc(s.gain_in, 16)
            sp.dma_start(cols[:, :, :], a.lru_cols).then_inc(s.cols_in, 16)
            for n in range(NB):
                if n >= 2:
                    sp.wait_ge(s.ri_full, 4 * (n - 1))
                for j in range(2):
                    sp.dma_start(wb[n % 2][:, :, j, :], a.w_in_b[:, :, j, n * LRU:(n + 1) * LRU]).then_inc((s.wb0, s.wb1)[n % 2], 16)
                for d in range(2):
                    for j, gate in enumerate((a.w_rgate, a.w_igate)):
                        sp.dma_start(wg[n % 2][:, :, 2 * d + j, :], gate[d, n]).then_inc((s.wg0, s.wg1)[n % 2], 16)
            sp.wait_ge(s.yu_full, NB)
            for half, sem in enumerate((s.wo0, s.wo1)):
                sp.dma_start(wo_slab(half), a.w_out_b[:, :, half * 512:(half + 1) * 512]).then_inc(sem, 16)

        @block.tensor
        def _(pe):
            norm_tensor(nc, pe, g, s, m)
            for n in range(NB):
                pe.wait_ge((s.wb0, s.wb1)[n % 2], 32 * (n // 2 + 1))
                if n >= 1:
                    pe.wait_ge(s.y_done, n)
                    pe.wait_ge(s.u_done, n)
                for j in range(4):
                    for k in range(K):
                        last = nc.tensor.matmul(g.PS[:, j, :], wb[n % 2][:, k, j // 2, (j % 2) * P:(j % 2 + 1) * P],
                                                g.feat[:, k, :], start=k == 0, stop=k == K - 1)
                last.then_inc(s.yu_full, 1)
                pe.wait_ge((s.wg0, s.wg1)[n % 2], 64 * (n // 2 + 1))
                pe.wait_ge(s.conv_done, n + 1)
                for d in range(2):
                    for j in range(2):
                        if 2 * n + d >= 1:
                            pe.wait_ge((s.r_done, s.i_done)[j], 2 * (2 * n + d))
                        for e in range(2):
                            for kk in range(2):
                                last = nc.tensor.matmul(g.PS[:, 4 + 2 * j + e, :],
                                                        wg[n % 2][:, kk, 2 * d + j, e * P:(e + 1) * P], u[:, kk, :],
                                                        start=kk == 0, stop=kk == 1)
                        last.then_inc(s.ri_full, 1)
            pe.wait_ge(s.tile_done, NB)
            out_tensor(nc, pe, g, s, out, [wo_slab(0), wo_slab(1)], (s.wo0, s.wo1))

        @block.scalar
        def _(act):
            act.wait_ge(s.gain_in, 16)
            norm_scalar(nc, act, g, s, m, gain)
            act.wait_ge(s.neg_abs, 1)
            nc.scalar.activation(rate[:, 1, :], rate[:, 0, :], ACT.Exp, scale=-1.0).then_inc(s.exp_lam, 1)
            for n in range(NB):
                act.wait_ge(s.yu_full, n + 1)
                if n >= 1:
                    act.wait_ge(s.tile_done, n)
                nc.scalar.activation(y[:, :, :], g.PS[:, 0:2, :], ACT.Gelu_apprx_tanh).then_inc(s.y_done, 1)
                nc.scalar.activation(pad[:, :, 2:S + 2], g.PS[:, 2:4, :], ACT.Copy).then_inc(s.u_done, 1)
                for d in range(2):
                    step = 2 * n + d
                    if step >= 1:
                        act.wait_ge(s.scanned, step)
                    act.wait_ge(s.ri_full, 2 * step + 1)
                    for e in range(2):
                        f = 2 * n + e
                        nc.scalar.activation(r[:, e, :], g.PS[:, 4 + e, :], ACT.Sigmoid,
                                             bias=cols[:, 5 + d, f:f + 1]).then_inc(s.r_done, 1)
                    act.wait_ge(s.ri_full, 2 * step + 2)
                    for e in range(2):
                        f = 2 * n + e
                        nc.scalar.activation(i_[:, e, :], g.PS[:, 6 + e, :], ACT.Sigmoid,
                                             bias=cols[:, 7 + d, f:f + 1]).then_inc(s.i_done, 1)
                    act.drain()
                    if step == 0:
                        act.wait_ge(s.conv_done, 1)
                    for e in range(2):
                        f = 8 * d + 2 * n + e
                        nc.scalar.activation(aa[:, e, :], r[:, e, :], ACT.Exp, scale=rate[:, 4, f:f + 1]).then_inc(s.a_done, 1)
                    for e in range(2):
                        f = 8 * d + 2 * n + e
                        nc.scalar.activation(th[:, e, :], r[:, e, :], ACT.Tanh, scale=rate[:, 5, f:f + 1]).then_inc(s.th_done, 1)
                    act.wait_ge(s.root_in, step + 1)
                    nc.scalar.activation(th[:, :, :], th[:, :, :], ACT.Sqrt).then_inc(s.root_done, 1)

        @block.vector
        def _(dve):
            dve.wait_ge(s.gain_in, 16)
            norm_vector(nc, dve, g, s, m, gain)
            nc.vector.memset(pad[:, :, 0:2], 0.0)
            nc.vector.memset(pad[:, :, S + 2:], 0.0)
            dve.wait_ge(s.cols_in, 16)
            lam = cols[:, 9:11, :].rearrange("p d k -> p (d k)")
            nc.vector.scalar_tensor_tensor(rate[:, 0, :], lam, -1.0, lam, ALU.mult, ALU.max)
            dve.drain().then_inc(s.neg_abs, 1)
            dve.wait_ge(s.exp_lam, 1)
            log1p_vector(nc, dve, rate[:, 1, :], rate[:, 2, :], rate[:, 3, :], rate[:, 5, :])
            nc.vector.tensor_scalar(rate[:, 2, :], lam, -1.0, 0.0, ALU.mult, ALU.max)
            dve.drain()
            nc.vector.tensor_tensor(rate[:, 1, :], rate[:, 1, :], rate[:, 2, :], ALU.add)
            dve.drain()
            nc.vector.tensor_scalar(rate[:, 4, :], rate[:, 1, :], -RG_C, None, ALU.mult)
            nc.vector.tensor_scalar(rate[:, 5, :], rate[:, 1, :], RG_C, None, ALU.mult)
            for n in range(NB):
                dve.wait_ge(s.u_done, n + 1)
                for e in range(2):
                    f = 2 * n + e
                    nc.vector.tensor_scalar(u[:, e, :], pad[:, e, 0:S], cols[:, 0, f:f + 1], cols[:, 4, f:f + 1],
                                            ALU.mult, ALU.add)
                    for tap in range(1, CONV):
                        dve.drain()
                        nc.vector.scalar_tensor_tensor(u[:, e, :], pad[:, e, tap:tap + S], cols[:, tap, f:f + 1],
                                                       u[:, e, :], ALU.mult, ALU.add)
                dve.drain().then_inc(s.conv_done, 1)
                for d in range(2):
                    step = 2 * n + d
                    dve.wait_ge(s.i_done, 2 * step + 2)
                    nc.vector.tensor_tensor(i_[:, :, :], i_[:, :, :], u[:, :, :], ALU.mult)
                    dve.wait_ge(s.a_done, 2 * step + 2)
                    dve.wait_ge(s.th_done, 2 * step + 2)
                    nc.vector.tensor_tensor(r[:, :, :], aa[:, :, :], aa[:, :, :], ALU.mult)
                    dve.drain()
                    nc.vector.scalar_tensor_tensor(th[:, :, :], r[:, :, :], 1.0, th[:, :, :], ALU.add, ALU.mult)
                    dve.drain().then_inc(s.root_in, 1)
                    dve.wait_ge(s.root_done, step + 1)
                    nc.vector.tensor_tensor(i_[:, :, :], i_[:, :, :], th[:, :, :], ALU.mult)
                    dve.drain()
                    for e in range(2):
                        way = slice(None, None, -1) if d else slice(None)
                        nc.vector.tensor_tensor_scan(h[:, d, e, way], aa[:, e, way], i_[:, e, way], 0.0, ALU.mult, ALU.add)
                    dve.drain().then_inc(s.scanned, 1)
                nc.vector.tensor_tensor(h[:, 0, :, :], h[:, 0, :, :], h[:, 1, :, :], ALU.add)
                dve.wait_ge(s.y_done, n + 1)
                dve.drain()
                nc.vector.tensor_tensor(out[:, 2 * n:2 * n + 2, :], h[:, 0, :, :], y[:, :, :],
                                        ALU.mult).then_inc(s.tile_done, 1)
            out_vector(nc, dve, g, s)


GROUPS, PER_GROUP = 4, 8
EXPERTS = GROUPS * PER_GROUP
F = 512
CAP = 64
PAIRS = EXPERTS // 2
EXTRA = 8
SLOTS = (PAIRS + EXTRA) * P
BIG = 1e30


def route(nc, g, a, layer):
    names = NORM_SEMS + """ gain_in gainrow_in router_in bias_in sent logits_full logits_done shifted exp_g shifted2 exp_e picked ranked spread row_full first_pair stored"""
    with memory(nc, f"route{layer}") as mem, stage(nc, f"route{layer}", names) as (block, s):
        m = Norm(rows=g.YA, stat=mem("stat", [P, 4 * T]))
        gain = mem("gain", [P, K])
        gain_row = mem("gain_row", [P, D])
        NR = GROUPS + EXPERTS
        w = mem("w", [P, K, NR])
        brow = mem("brow", [P, NR])
        lg = mem("lg", [P, T, NR])
        sm = mem("sm", [P, 12, T])
        gm = mem("gm", [P, 3, T, GROUPS])
        le = mem("le", [P, T, EXPERTS])
        q = mem("q", [P, T, EXPERTS])
        one = mem("one", [P, 2, T, EXPERTS])
        both = mem("both", [P, T, EXPERTS])
        ex = mem("ex", [P, 6, EXPERTS])
        cmp = mem("cmp", [P, 2 * EXTRA, EXPERTS])
        ovx = mem("ovx", [P, 2 * EXTRA + 1])
        slot = mem("slot", [P, 4, T])
        diag = mem("diag", [P, 4, S])

        @block.sync
        def _(sp):
            sp.dma_start(gain[:, :], a.norm_ffn[layer]).then_inc(s.gain_in, 16)
            sp.dma_start(gain_row[:, :], a.norm_ffn_row[layer].partition_broadcast(P)).then_inc(s.gainrow_in, 16)
            sp.dma_start(w[:, :, 0:GROUPS], a.w_router_group[layer]).then_inc(s.router_in, 16)
            sp.dma_start(w[:, :, GROUPS:], a.w_router_expert[layer]).then_inc(s.router_in, 16)
            sp.dma_start(brow[:, 0:GROUPS], a.b_router_group[layer].partition_broadcast(P)).then_inc(s.bias_in, 16)
            sp.dma_start(brow[:, GROUPS:], a.b_router_expert[layer].partition_broadcast(P)).then_inc(s.bias_in, 16)
            for t in range(T):
                sp.wait_ge(s.sent, t + 1)
                sp.dma_start(g.rows_dram[t * P:(t + 1) * P, :], g.YB[:, t, :]).then_inc(s.stored, 16)
            for u in range(2):
                for dst, src in expert_loads(a, g.W, layer, u, u):
                    sp.dma_start(dst, src).then_inc(s.first_pair, 16)
            sp.wait_ge(s.stored, 16 * T)
            sp.wait_ge(s.first_pair, 16 * 6)

        @block.tensor
        def _(pe):
            norm_tensor(nc, pe, g, s, m)
            pe.wait_ge(s.router_in, 32)
            for t in range(T):
                to_rows(nc, g, g.PS[:, t, 0:NR], w, t, 0, NR).then_inc(s.logits_full, 1)
            pe.wait_ge(s.picked, 1)
            for t in range(T + 1):
                terms = [(g.ones, e) for e in range(t)] + ([(g.before, t)] if t < T else [])
                for n, (left, e) in enumerate(terms):
                    last = nc.tensor.matmul(g.PS[:, 4, t * EXPERTS:(t + 1) * EXPERTS], left, both[:, e, :],
                                            start=n == 0, stop=n == len(terms) - 1)
            last.then_inc(s.ranked, 1)
            for n in range(4):
                pe.wait_ge(s.spread, n + 1)
                nc.tensor.matmul(g.PS[:, n, :], g.ones, diag[:, n, :], start=True, stop=True).then_inc(s.row_full, 1)

        @block.scalar
        def _(act):
            act.wait_ge(s.gain_in, 16)
            norm_scalar(nc, act, g, s, m, gain)
            for t in range(T):
                act.wait_ge(s.logits_full, t + 1)
                nc.scalar.activation(lg[:, t, :], g.PS[:, t, 0:NR], ACT.Copy).then_inc(s.logits_done, 1)
            act.wait_ge(s.shifted, 1)
            nc.scalar.activation(gm[:, 0, :, :], gm[:, 0, :, :], ACT.Exp).then_inc(s.exp_g, 1)
            act.wait_ge(s.shifted2, 1)
            nc.scalar.activation(sm[:, 6, :], sm[:, 6, :], ACT.Exp).then_inc(s.exp_e, 1)
            for n in range(4):
                act.wait_ge(s.row_full, n + 1)
                dst = (g.slot_row, g.weight_row)[n // 2][:, n % 2, :]
                nc.scalar.activation(dst, g.PS[:, n, :], ACT.Copy)

        @block.vector
        def _(dve):
            def first_of(dst, val, top, width, tmp):
                nc.vector.tensor_tensor(dst, val, over(top, width), ALU.is_equal)
                dve.drain()
                nc.vector.tensor_tensor(dst, dst, each(g.fall[:, 0:width], T), ALU.mult)
                dve.drain()
                nc.vector.tensor_reduce(tmp, dst, AX.X, ALU.max)
                dve.drain()
                nc.vector.tensor_tensor(dst, dst, over(tmp, width), ALU.is_equal)
                dve.drain()

            dve.wait_ge(s.gain_in, 16)
            norm_vector(nc, dve, g, s, m, gain)
            dve.wait_ge(s.gainrow_in, 16)
            for t in range(T):
                nc.vector.tensor_tensor(g.YB[:, t, :], g.YA[:, t, :], gain_row[:, :], ALU.mult).then_inc(s.sent, 1)
            dve.wait_ge(s.logits_done, T)
            dve.wait_ge(s.bias_in, 32)
            nc.vector.tensor_tensor(lg[:, :, :], lg[:, :, :], each(brow[:, :], T), ALU.add)
            dve.drain()
            lgg = lg[:, :, 0:GROUPS]
            nc.vector.tensor_reduce(sm[:, 0, :], lgg, AX.X, ALU.max)
            dve.drain()
            nc.vector.tensor_tensor(gm[:, 0, :, :], lgg, over(sm[:, 0, :], GROUPS), ALU.subtract)
            dve.drain().then_inc(s.shifted, 1)
            og = gm[:, 1, :, :]
            first_of(og, lgg, sm[:, 0, :], GROUPS, sm[:, 1, :])
            nc.vector.tensor_scalar(gm[:, 2, :, :], og, 1.0, BIG, ALU.subtract, ALU.mult)
            for t in range(T):
                nc.vector.tensor_tensor(le[:, t, :].rearrange("p (g e) -> p g e", g=GROUPS),
                                        lg[:, t, GROUPS:].rearrange("p (g e) -> p g e", g=GROUPS),
                                        over(gm[:, 1, t, :], PER_GROUP), ALU.mult)
            dve.drain()
            for t in range(T):
                v = le[:, t, :].rearrange("p (g e) -> p g e", g=GROUPS)
                nc.vector.tensor_tensor(v, v, over(gm[:, 2, t, :], PER_GROUP), ALU.add)
            dve.drain()
            nc.vector.tensor_reduce(sm[:, 2, :], le[:, :, :], AX.X, ALU.max)
            dve.drain()
            first_of(one[:, 0, :, :], le[:, :, :], sm[:, 2, :], EXPERTS, sm[:, 1, :])
            nc.vector.scalar_tensor_tensor(le[:, :, :], one[:, 0, :, :], -1e36, le[:, :, :], ALU.mult, ALU.add)
            dve.drain()
            nc.vector.tensor_reduce(sm[:, 3, :], le[:, :, :], AX.X, ALU.max)
            dve.drain()
            first_of(one[:, 1, :, :], le[:, :, :], sm[:, 3, :], EXPERTS, sm[:, 1, :])
            nc.vector.tensor_tensor(both[:, :, :], one[:, 0, :, :], one[:, 1, :, :], ALU.add)
            dve.drain().then_inc(s.picked, 1)
            nc.vector.tensor_tensor(sm[:, 6, :], sm[:, 3, :], sm[:, 2, :], ALU.subtract)
            dve.drain().then_inc(s.shifted2, 1)
            dve.wait_ge(s.exp_g, 1)
            nc.vector.tensor_reduce(sm[:, 4, :], gm[:, 0, :, :], AX.X, ALU.add)
            dve.wait_ge(s.exp_e, 1)
            nc.vector.tensor_scalar(sm[:, 5, :], sm[:, 6, :], 1.0, None, ALU.add)
            dve.drain()
            nc.vector.tensor_tensor(sm[:, 5, :], sm[:, 5, :], sm[:, 4, :], ALU.mult)
            dve.drain()
            nc.vector.reciprocal(slot[:, 2, :], sm[:, 5, :])
            dve.drain()
            nc.vector.tensor_tensor(slot[:, 3, :], slot[:, 2, :], sm[:, 6, :], ALU.mult)
            dve.wait_ge(s.ranked, 1)
            count = g.PS[:, 4, T * EXPERTS:(T + 1) * EXPERTS]
            nc.vector.tensor_copy(ex[:, 0, :], count)
            dve.drain()
            nc.vector.tensor_scalar(ex[:, 1, :], ex[:, 0, :], float(CAP), None, ALU.is_gt)
            for b in range(2, S // CAP):
                dve.drain()
                nc.vector.scalar_tensor_tensor(ex[:, 1, :], ex[:, 0, :], float(b * CAP), ex[:, 1, :], ALU.is_gt, ALU.add)
            dve.drain()
            nc.vector.tensor_tensor_scan(ex[:, 2, :], g.ones[:, 0:EXPERTS], ex[:, 1, :], 0.0, ALU.mult, ALU.add)
            dve.drain()
            nc.vector.tensor_tensor(ex[:, 3, :], ex[:, 2, :], ex[:, 1, :], ALU.subtract)
            dve.drain()
            nc.vector.tensor_scalar(ex[:, 3, :], ex[:, 3, :], float(CAP), float(EXPERTS * CAP - CAP), ALU.mult, ALU.add)
            nc.vector.tensor_scalar(ex[:, 4, :], g.rise[:, 0:EXPERTS], float(CAP), None, ALU.mult)
            nc.vector.tensor_tensor(cmp[:, :, :], each(ex[:, 2, :], 2 * EXTRA), over(g.rise[:, 0:2 * EXTRA], EXPERTS),
                                    ALU.is_le)
            dve.drain()
            nc.vector.tensor_reduce(ovx[:, 0:2 * EXTRA], cmp[:, :, :], AX.X, ALU.add)
            nc.vector.tensor_scalar(ovx[:, 2 * EXTRA:], ex[:, 2, EXPERTS - 1:], 0.5, 0.25, ALU.mult, ALU.add)
            dve.drain()
            nc.vector.tensor_scalar(ovx[:, 0:2 * EXTRA], ovx[:, 0:2 * EXTRA], float(EXPERTS - 1), None, ALU.min)
            dve.drain()
            nc.vector.tensor_copy(g.extra[:, :], ovx[:, :])
            for j in range(2):
                for c, row in enumerate((g.PS[:, 4, 0:T * EXPERTS].rearrange("p (t e) -> p t e", t=T),
                                         each(ex[:, 4, :], T), each(ex[:, 3, :], T))):
                    nc.vector.tensor_tensor(q[:, :, :], one[:, j, :, :], row, ALU.mult)
                    dve.drain()
                    nc.vector.tensor_reduce(sm[:, 7 + c, :], q[:, :, :], AX.X, ALU.add)
                    dve.drain()
                nc.vector.tensor_tensor(sm[:, 9, :], sm[:, 9, :], sm[:, 8, :], ALU.subtract)
                nc.vector.tensor_tensor(sm[:, 8, :], sm[:, 8, :], sm[:, 7, :], ALU.add)
                dve.drain()
                nc.vector.scalar_tensor_tensor(sm[:, 9, :], sm[:, 7, :], float(CAP), sm[:, 9, :], ALU.is_ge, ALU.mult)
                dve.drain()
                nc.vector.tensor_tensor(slot[:, j, :], sm[:, 9, :], sm[:, 8, :], ALU.add)
                dve.drain()
            for n in range(4):
                nc.vector.tensor_tensor(diag[:, n, :].rearrange("p (t c) -> p t c", t=T), each(g.ident, T),
                                        over(slot[:, n, :], P), ALU.mult).then_inc(s.spread, 1)


def expert_loads(a, w, layer, e, u):
    return [(slab(w[u]), a.w_exp_gate[layer, e]),
            (slab(w[2 + u]), a.w_exp_up[layer, e]),
            (slab(w[4 + u], D), a.w_exp_down[layer, e])]


def experts(nc, g, a, layer, extra):
    names = """g0 g1 u0 u1 d0 d1 g_free u_free d_free index_done rows_free turned
        xt_a xt_v gate_full up_full silu_done hidden_done hidden_turned ht_done y_full y_a y_v
        weights_done sum_full summed"""
    tag = ("extra" if extra else "experts") + str(layer)
    with memory(nc, tag) as mem, stage(nc, tag, names, rows_in=g.pool_sems[0]) as (block, s):
        w = g.W
        wg = [slab(w[u]) for u in range(2)]
        wu = [slab(w[2 + u]) for u in range(2)]
        wd = [slab(w[4 + u], D) for u in range(2)]
        full = ((s.g0, s.g1), (s.u0, s.u1), (s.d0, s.d1))
        free = (s.g_free, s.u_free, s.d_free)
        number = mem("number", [P, 1])
        found = mem("found", [P, 2])
        index = mem("index", [P, PAIRS + 1], I32)
        taken = mem("taken", [P, 1], I32)
        match = mem("match", [P, 2, S])
        rows = mem("rows", [P, D])
        xt = mem("xt", [P, K, P])
        silu = mem("silu", [P, F])
        hid = mem("hid", [P, F])
        ht = mem("ht", [P, F // P, P])
        y = mem("y", [P, D])
        sums = [(t, half) for t in range(T) for half in range(2)]
        SUM_BANKS = (0, 1, 7)

        @contextmanager
        def pairs(eng):
            if not extra:
                with eng.Fori(0, PAIRS) as j:
                    yield j
            else:
                n = eng.value_load(g.extra[0:1, 2 * EXTRA:2 * EXTRA + 1], min_val=0, max_val=EXTRA)
                with eng.If(n > 0):
                    with eng.Fori(0, n) as j:
                        yield j

        @block.sync
        def _(sp):
            if not extra:
                for part in range(3):
                    for u in range(2):
                        sp.sem_inc(full[part][u], 16)
                with sp.Fori(1, PAIRS) as j:
                    for part in range(3):
                        sp.wait_ge(free[part], j)
                        for u in range(2):
                            dst, src = expert_loads(a, w, layer, 2 * j + u, u)[part]
                            sp.dma_start(dst, src).then_inc(full[part][u], 16)
            else:
                with pairs(sp) as j:
                    e = [sp.value_load(g.extra[0:1, bass.ds(2 * j + u, 1)], min_val=0, max_val=EXPERTS - 1)
                         for u in range(2)]
                    for part in range(3):
                        sp.wait_ge(free[part], j + 1)
                        for u in range(2):
                            dst, src = expert_loads(a, w, layer, e[u], u)[part]
                            sp.dma_start(dst, src).then_inc(full[part][u], 16)

        @block.gpsimd
        def _(pool):
            with pairs(pool) as j:
                pool.wait_ge(s.rows_free, j + 1)
                pool.wait_ge(s.index_done, j + 1)
                nc.gpsimd.tensor_copy(taken[:, :], index[:, bass.ds(j, 1)])
                pool.drain()
                pool.indirect_dma_start(rows[:, :], None, g.rows_dram,
                                        bass.IndirectOffsetOnAxis(taken[:, 0:1].bitcast(U32), 0)).then_inc(s.rows_in, 16)

        @block.tensor
        def _(pe):
            if extra:
                for sem in free:
                    pe.sem_inc(sem, 1)
            pe.sem_inc(s.rows_free, 1)
            with pairs(pe) as j:
                pe.wait_ge(s.rows_in, 16 * j + 16)
                pe.wait_ge(s.summed, 8 * j + 1)
                for k in range(K):
                    last = nc.tensor.transpose(g.PS[:, k // 4, (k % 4) * P:(k % 4 + 1) * P], rows[:, k * P:(k + 1) * P],
                                               g.ident)
                    if k % 4 == 3:
                        last.then_inc(s.turned, 1)
                pe.wait_ge(s.xt_a, j + 1)
                pe.wait_ge(s.xt_v, j + 1)
                for part, weights, bank, done in ((0, wg, 2, s.gate_full), (1, wu, 3, s.up_full)):
                    for u in range(2):
                        pe.wait_ge(full[part][u], 16 * j + 16)
                    for k in range(K):
                        for u in range(2):
                            last = nc.tensor.matmul(g.PS[u * CAP:(u + 1) * CAP, bank, :],
                                                    xt[:, k, u * CAP:(u + 1) * CAP], weights[u][:, k, :],
                                                    start=k == 0, stop=k == K - 1)
                    last.then_inc(done, 1)
                    pe.drain().then_inc(free[part], 1)
                pe.wait_ge(s.hidden_done, j + 1)
                for i in range(F // P):
                    last = nc.tensor.transpose(g.PS[:, 4, i * P:(i + 1) * P], hid[:, i * P:(i + 1) * P], g.ident)
                last.then_inc(s.hidden_turned, 1)
                pe.wait_ge(s.ht_done, j + 1)
                for u in range(2):
                    pe.wait_ge(full[2][u], 16 * j + 16)
                for half in range(2):
                    for i in range(F // P):
                        for u in range(2):
                            last = nc.tensor.matmul(g.PS[u * CAP:(u + 1) * CAP, 5 + half, :],
                                                    ht[:, i, u * CAP:(u + 1) * CAP],
                                                    wd[u][:, i, half * 512:(half + 1) * 512],
                                                    start=i == 0, stop=i == F // P - 1)
                    last.then_inc(s.y_full, 1)
                pe.drain().then_inc(free[2], 1)
                pe.wait_ge(s.weights_done, j + 1)
                pe.wait_ge(s.y_a, j + 1)
                pe.wait_ge(s.y_v, j + 1)
                for n, (t, half) in enumerate(sums):
                    if n >= 3:
                        pe.wait_ge(s.summed, 8 * j + n - 1)
                    nc.tensor.matmul(g.PS[:, SUM_BANKS[n % 3], :], match[:, 0, t * P:(t + 1) * P],
                                     y[:, half * 512:(half + 1) * 512], start=True, stop=True).then_inc(s.sum_full, 1)

        @block.scalar
        def _(act):
            with pairs(act) as j:
                act.wait_ge(s.turned, 2 * j + 1)
                nc.scalar.activation(xt[:, 0:4, :].rearrange("p k c -> p (k c)"), g.PS[:, 0, :], ACT.Copy).then_inc(s.xt_a, 1)
                act.wait_ge(s.gate_full, j + 1)
                nc.scalar.activation(silu[:, :], g.PS[:, 2, :], ACT.Silu).then_inc(s.silu_done, 1)
                act.wait_ge(s.hidden_turned, j + 1)
                nc.scalar.activation(ht[:, :, :].rearrange("p i c -> p (i c)"), g.PS[:, 4, :], ACT.Copy).then_inc(s.ht_done, 1)
                act.wait_ge(s.y_full, 2 * j + 1)
                nc.scalar.activation(y[:, 0:512], g.PS[:, 5, :], ACT.Copy).then_inc(s.y_a, 1)

        @block.vector
        def _(dve):
            def find_index(column):
                for i in range(2):
                    nc.vector.scalar_tensor_tensor(match[:, 1, :], g.slot_row[:, i, :], number[:, :], g.token_row,
                                                   ALU.is_equal, ALU.mult, accum_out=found[:, i:i + 1])
                    dve.drain()
                nc.vector.tensor_tensor(column, found[:, 0:1], found[:, 1:2], ALU.add).then_inc(s.index_done, 1)

            dve.sem_inc(s.summed, 1)
            nc.vector.tensor_scalar(number[:, :], g.fall[:, 0:1], 0.0, float(PAIRS * P if extra else 0), ALU.mult, ALU.add)
            dve.drain()
            nc.vector.tensor_tensor(number[:, :], number[:, :], g.lane, ALU.add)
            dve.drain()
            find_index(index[:, 0:1])
            with pairs(dve) as j:
                dve.wait_ge(s.turned, 2 * j + 2)
                nc.vector.tensor_copy(xt[:, 4:8, :].rearrange("p k c -> p (k c)"), g.PS[:, 1, :]).then_inc(s.xt_v, 1)
                dve.sem_inc(s.rows_free, 1)
                for i in range(2):
                    nc.vector.scalar_tensor_tensor(match[:, i, :], g.slot_row[:, i, :], number[:, :],
                                                   g.weight_row[:, i, :], ALU.is_equal, ALU.mult)
                dve.drain()
                nc.vector.tensor_tensor(match[:, 0, :], match[:, 0, :], match[:, 1, :], ALU.add).then_inc(s.weights_done, 1)
                nc.vector.tensor_scalar(number[:, :], number[:, :], float(P), None, ALU.add)
                dve.drain()
                find_index(index[:, bass.ds(j + 1, 1)])
                dve.wait_ge(s.up_full, j + 1)
                dve.wait_ge(s.silu_done, j + 1)
                nc.vector.tensor_tensor(hid[:, :], silu[:, :], g.PS[:, 3, :], ALU.mult).then_inc(s.hidden_done, 1)
                dve.wait_ge(s.y_full, 2 * j + 2)
                nc.vector.tensor_copy(y[:, 512:], g.PS[:, 6, :]).then_inc(s.y_v, 1)
                for n, (t, half) in enumerate(sums):
                    dve.wait_ge(s.sum_full, 8 * j + n + 1)
                    x = g.X[:, t, half * 512:(half + 1) * 512]
                    nc.vector.tensor_tensor(x, x, g.PS[:, SUM_BANKS[n % 3], :], ALU.add).then_inc(s.summed, 1)
                dve.drain()


def per_layer(nc, g, a, layer):
    names = NORM_SEMS + """ gain_in brow_in p_in wp_in w0 w1 p_turned pt_done gate_full
        added gate_on ple_full gated"""
    with memory(nc, f"ple{layer}") as mem, stage(nc, f"ple{layer}", names) as (block, s):
        m = Norm(rows=g.YA, stat=mem("stat", [P, 4 * T]))
        gain = mem("gain", [P, K])
        brow = mem("brow", [P, D])
        w = [slab(g.W[i]) for i in range(2)]
        wp = g.W[2][:, 0:2 * D].rearrange("p (k c) -> p k c", k=2)
        p_rows = mem("p_rows", [P, T, 2 * P])
        pt = mem("pt", [P, 2, S])
        part = mem("part", [P, 2, 512])
        STEPS = [(half, t) for half in range(2) for t in range(T)]

        @block.sync
        def _(sp):
            sp.dma_start(gain[:, :], a.norm_ple[layer]).then_inc(s.gain_in, 16)
            sp.dma_start(brow[:, :], a.b_ple_gate[layer].partition_broadcast(P)).then_inc(s.brow_in, 16)
            sp.dma_start(p_rows[:, :, :], a.p[layer, 0].rearrange("(t p) c -> p t c", p=P)).then_inc(s.p_in, 16)
            sp.dma_start(wp[:, :, :], a.w_ple[layer]).then_inc(s.wp_in, 16)
            for half, sem in enumerate((s.w0, s.w1)):
                sp.dma_start(w[half][:, :, :], a.w_ple_gate[layer][:, :, half * 512:(half + 1) * 512]).then_inc(sem, 16)

        @block.tensor
        def _(pe):
            pe.wait_ge(s.p_in, 16)
            for c in range(2):
                for t in range(T):
                    last = nc.tensor.transpose(g.PS[:, c, t * P:(t + 1) * P], p_rows[:, t, c * P:(c + 1) * P], g.ident)
            last.then_inc(s.p_turned, 1)
            pe.wait_ge(s.pt_done, 1)
            norm_tensor(nc, pe, g, s, m)
            pe.wait_ge(s.wp_in, 16)
            for n, (half, t) in enumerate(STEPS):
                if n % T == 0:
                    pe.wait_ge((s.w0, s.w1)[half], 16)
                if n >= 4:
                    pe.wait_ge(s.added, n - 3)
                    pe.wait_ge(s.gated, n - 3)
                to_rows(nc, g, g.PS[:, n % 4, :], w[half], t, 0, 512).then_inc(s.gate_full, 1)
                for c in range(2):
                    last = nc.tensor.matmul(g.PS[:, 4 + n % 4, :], pt[:, c, t * P:(t + 1) * P],
                                            wp[:, c, half * 512:(half + 1) * 512], start=c == 0, stop=c == 1)
                last.then_inc(s.ple_full, 1)

        @block.scalar
        def _(act):
            act.wait_ge(s.p_turned, 1)
            nc.scalar.activation(pt[:, :, :], g.PS[:, 0:2, :], ACT.Copy).then_inc(s.pt_done, 1)
            act.wait_ge(s.gain_in, 16)
            norm_scalar(nc, act, g, s, m, gain)
            for n in range(len(STEPS)):
                act.wait_ge(s.added, n + 1)
                nc.scalar.activation(part[:, n % 2, :], part[:, n % 2, :], ACT.Sigmoid).then_inc(s.gate_on, 1)

        @block.vector
        def _(dve):
            dve.wait_ge(s.gain_in, 16)
            norm_vector(nc, dve, g, s, m, gain)
            dve.wait_ge(s.brow_in, 16)

            def add(n):
                half, t = STEPS[n]
                dve.wait_ge(s.gate_full, n + 1)
                nc.vector.tensor_tensor(part[:, n % 2, :], g.PS[:, n % 4, :], brow[:, half * 512:(half + 1) * 512],
                                        ALU.add).then_inc(s.added, 1)

            add(0)
            for n, (half, t) in enumerate(STEPS):
                if n + 1 < len(STEPS):
                    add(n + 1)
                dve.wait_ge(s.gate_on, n + 1)
                dve.wait_ge(s.ple_full, n + 1)
                nc.vector.tensor_tensor(part[:, n % 2, :], part[:, n % 2, :], g.PS[:, 4 + n % 4, :],
                                        ALU.mult).then_inc(s.gated, 1)
                dve.drain()
                x = g.X[:, t, half * 512:(half + 1) * 512]
                nc.vector.tensor_tensor(x, x, part[:, n % 2, :], ALU.add)
                dve.drain()


def norm_rows(nc, g, gain, out, tag):
    with memory(nc, tag) as mem, stage(nc, tag, "row_in squared meaned rooted ready stored") as (block, s):
        dst = g.X if out is None else g.YA
        row = mem("row", [P, D])
        stat = mem("stat", [P, 4 * T])

        @block.sync
        def _(sp):
            sp.dma_start(row[:, :], gain.partition_broadcast(P)).then_inc(s.row_in, 16)
            if out is not None:
                for t in range(T):
                    sp.wait_ge(s.ready, t + 1)
                    sp.dma_start(out[0, t * P:(t + 1) * P, :], g.YA[:, t, :]).then_inc(s.stored, 16)
                sp.wait_ge(s.stored, 16 * T)

        @block.scalar
        def _(act):
            for t in range(T):
                nc.scalar.activation(g.YA[:, t, :], g.X[:, t, :], ACT.Square,
                                     accum_out=stat[:, t:t + 1]).then_inc(s.squared, 1)
            act.wait_ge(s.meaned, 1)
            nc.scalar.activation(stat[:, 2 * T:3 * T], stat[:, T:2 * T], ACT.Sqrt).then_inc(s.rooted, 1)

        @block.vector
        def _(dve):
            dve.wait_ge(s.squared, T)
            nc.vector.tensor_scalar(stat[:, T:2 * T], stat[:, 0:T], 1.0 / D, EPS, ALU.mult, ALU.add).then_inc(s.meaned, 1)
            dve.wait_ge(s.rooted, 1)
            nc.vector.reciprocal(stat[:, 3 * T:], stat[:, 2 * T:3 * T])
            dve.wait_ge(s.row_in, 16)
            dve.drain()
            for t in range(T):
                nc.vector.scalar_tensor_tensor(dst[:, t, :], g.X[:, t, :], stat[:, 3 * T + t:3 * T + t + 1], row[:, :],
                                               ALU.mult, ALU.mult).then_inc(s.ready, 1)


def program(nc, a, out):
    with ExitStack() as ctx:
        def sb(name, shape, dt=F32):
            return ctx.enter_context(nc.sbuf_tensor(name, shape, dt))

        n_const = len(CONSTS) * P + 2 + S + P + 1
        g = Parts()
        g.C = sb("consts_sb", [P, n_const])
        col = {n: g.C[:, i * P:(i + 1) * P] for i, n in enumerate(CONSTS)}
        g.ident, g.upto, g.before, g.ones, g.causal = (col[n] for n in CONSTS[:5])
        g.rot_a, g.rot_i = col["rot_a"], col["rot_i"]
        g.low = [col[f"low{i}"] for i in range(LEVELS)]
        g.up = [col[f"up{i}"] for i in range(LEVELS)]
        at = len(CONSTS) * P
        g.freq = g.C[:, at:at + 2]
        g.token_row = g.C[:, at + 2:at + 2 + S]
        g.rise, g.fall = g.C[:, at + 2:at + 2 + P], g.C[:, at + 2 + S:at + 2 + S + P]
        g.lane = g.C[:, at + 2 + S + P:at + 3 + S + P]
        g.X = sb("X", [P, T, D])
        g.feat = sb("feat", [P, K, S])
        g.YA = sb("YA", [P, T, D])
        g.YB = sb("YB", [P, T, D])
        g.PS = ctx.enter_context(nc.psum_tensor("PS", [P, 8, 512], F32))
        g.pool_sems = [ctx.enter_context(nc.semaphore(f"pool_dma{i}")) for i in range(4)]
        g.bias_at = [0, P, 3 * P, 6 * P]
        g.rows_dram = nc.dram_tensor("moe_rows", (S, D), F32, kind="Internal").ap()
        with ExitStack() as first:
            def sb1(name, shape):
                return first.enter_context(nc.sbuf_tensor(name, shape, F32))
            g.TAB = sb1("TAB", [P, 4, S])
            g.KT = sb1("KT", [P, KV_HEADS, S])
            g.V = sb1("V", [P, T, KV_HEADS * DH])
            g.BIAS = sb1("BIAS", [P, 10 * P])
            g.beta = sb1("beta", [P, T, HEADS])
            g.decay = sb1("decay", [P, T, HEADS])
            g.beta_pair = sb1("beta_pair", [P, T, 2])
            setup(nc, g, a)
            with nc.Fori(0, DEPTH) as layer:
                mixer_inputs(nc, g, a, layer)
                attention(nc, g, a, layer)
                with nc.Fori(0, HEADS // 2) as pair:
                    delta_heads(nc, g, a, layer, pair)
                merge(nc, g, a, layer)
        norm_rows(nc, g, a.final_gain, None, "between")
        g.slot_row = sb("slot_row", [P, 2, S])
        g.weight_row = sb("weight_row", [P, 2, S])
        g.W = [sb(f"W{i}", [P, K * F]) for i in range(6)]
        g.extra = sb("extra", [P, 2 * EXTRA + 1], I32)
        for layer in range(DEPTH):
            (short_conv if layer % 2 == 0 else rg_lru)(nc, g, a, layer)
            route(nc, g, a, layer)
            experts(nc, g, a, layer, extra=False)
            experts(nc, g, a, layer, extra=True)
            per_layer(nc, g, a, layer)
        norm_rows(nc, g, a.norm_final, out, "last")


_LAID_OUT = {
    "norm_gain": lambda v: v.reshape(DEPTH, K, P).transpose(0, 2, 1),
    "conv_w": lambda v: v.reshape(DEPTH, CONV, 3, HEADS // 2, 2, P).transpose(0, 3, 5, 4, 2, 1),
    "norm_mix_2": lambda v: v.reshape(DEPTH, K, P).transpose(0, 2, 1),
    "norm_ple_2": lambda v: v.reshape(DEPTH, K, P).transpose(0, 2, 1),
    "conv_a_2": lambda v: v.reshape(3, K, P).transpose(2, 1, 0),
}
_PLAIN = ["x", "positions", "w_in", "a_log", "dt_bias", "gdn_norm_gain", "idx_k_gain", "w_out", "p_2", "w_in_a_2",
          "w_out_a_2", "w_in_b_2", "w_rgate_b_2", "w_igate_b_2", "w_out_b_2", "norm_ffn_2", "w_router_group_2",
          "b_router_group_2", "w_router_expert_2", "b_router_expert_2", "w_exp_gate_2", "w_exp_up_2", "w_exp_down_2",
          "final_gain", "w_ple_2", "w_ple_gate_2", "b_ple_gate_2", "norm_final_2"]


def lay_out(inputs):
    arrays = {f"in_{n}": np.ascontiguousarray(inputs[n]) for n in _PLAIN}
    for n, order in _LAID_OUT.items():
        arrays[f"in_{n}"] = np.ascontiguousarray(order(np.asarray(inputs[n])))
    arrays["in_norm_ffn_cols"] = np.ascontiguousarray(
        np.asarray(inputs["norm_ffn_2"]).reshape(DEPTH, K, P).transpose(0, 2, 1))
    cols = np.concatenate([np.asarray(inputs[n]).reshape(-1, K, P) for n in
                           ("conv_b_2", "conv_bias_b_2", "b_rgate_b_2", "b_igate_b_2", "lam_b_2")])
    arrays["in_lru_cols"] = np.ascontiguousarray(cols.transpose(2, 0, 1))
    arrays["in_consts"] = shape_constants()
    return arrays


def views(aps):
    def slabs(name):
        return aps[name].rearrange("l (k p) c -> l p k c", p=P)

    a = Parts()
    a.x, a.positions, a.consts = aps["in_x"], aps["in_positions"], aps["in_consts"]
    a.norm_gain, a.conv_w = aps["in_norm_gain"], aps["in_conv_w"]
    a.w_in = slabs("in_w_in")
    a.w_heads = aps["in_w_in"][:, :, C_QKV:C_ZB].rearrange("l (k p) (s r h c) -> l r h k p s c", p=P, s=3, r=HEADS // 2, h=2)
    a.a_log, a.dt_bias = aps["in_a_log"], aps["in_dt_bias"]
    a.gdn_norm_gain, a.idx_k_gain = aps["in_gdn_norm_gain"], aps["in_idx_k_gain"]
    a.w_out = slabs("in_w_out")
    a.final_gain = aps["in_final_gain"]
    a.p = aps["in_p_2"]
    a.norm_mix = aps["in_norm_mix_2"]
    a.w_in_a = aps["in_w_in_a_2"][0].rearrange("(k p) (s f c) -> f k p s c", p=P, s=3, f=K)
    a.conv_a = aps["in_conv_a_2"]
    a.w_out_a, a.w_out_b = slabs("in_w_out_a_2")[0], slabs("in_w_out_b_2")[0]
    a.w_in_b = aps["in_w_in_b_2"][0].rearrange("(k p) (s c) -> p k s c", p=P, s=2)
    a.lru_cols = aps["in_lru_cols"]
    a.w_rgate = aps["in_w_rgate_b_2"][0].rearrange("d n (k p) e -> d n p k e", p=P)
    a.w_igate = aps["in_w_igate_b_2"][0].rearrange("d n (k p) e -> d n p k e", p=P)
    a.norm_ffn, a.norm_ffn_row = aps["in_norm_ffn_cols"], aps["in_norm_ffn_2"]
    a.w_router_group, a.w_router_expert = slabs("in_w_router_group_2"), slabs("in_w_router_expert_2")
    a.b_router_group, a.b_router_expert = aps["in_b_router_group_2"], aps["in_b_router_expert_2"]
    a.w_exp_gate = aps["in_w_exp_gate_2"].rearrange("l e (k p) f -> l e p k f", p=P)
    a.w_exp_up = aps["in_w_exp_up_2"].rearrange("l e (k p) f -> l e p k f", p=P)
    a.w_exp_down = aps["in_w_exp_down_2"].rearrange("l e (k p) d -> l e p k d", p=P)
    a.norm_ple = aps["in_norm_ple_2"]
    a.w_ple, a.w_ple_gate = slabs("in_w_ple_2"), slabs("in_w_ple_gate_2")
    a.b_ple_gate, a.norm_final = aps["in_b_ple_gate_2"], aps["in_norm_final_2"]
    return a


def kernel(**inputs):
    import concourse.bacc as bacc
    from concourse.bass_utils import run_bass_kernel_spmd

    nc = bacc.Bacc("TRN2", target_bir_lowering=False, num_devices=1)
    arrays = lay_out(inputs)
    aps = {n: nc.dram_tensor(n, v.shape, mybir.dt.from_np(v.dtype), kind="ExternalInput").ap() for n, v in arrays.items()}
    out = nc.dram_tensor("out", (1, S, D), F32, kind="ExternalOutput").ap()
    program(nc, views(aps), out)
    result = run_bass_kernel_spmd(nc, [arrays], core_ids=[0])
    return result.results[0]["out"]
```

```python
from collections import namedtuple
from contextlib import ExitStack, contextmanager

import concourse.bass as bass
import numpy as np
from concourse import mybir

F32 = mybir.dt.float32
I32 = mybir.dt.int32
U32 = mybir.dt.uint32
ALU = mybir.AluOpType
ACT = mybir.ActivationFunctionType
AX = mybir.AxisListType

P = 128
S = 512
T = S // P
D = 1024
K = D // P
DEPTH = 2
EPS = 1e-6

HEADS, KV_HEADS, DH = 8, 2, 128
GROUP = HEADS // KV_HEADS
IDX_HEADS, IDX_DIM = 8, 64
TOPK = min(256, S // 4)
C_Q = 0
C_K = C_Q + HEADS * DH
C_V = C_K + KV_HEADS * DH
C_Z = C_V + KV_HEADS * DH
C_QI = C_Z + HEADS * DH
C_KI = C_QI + IDX_HEADS * IDX_DIM
C_WI = C_KI + IDX_DIM
C_QKV = C_WI + IDX_HEADS
C_ZB = C_QKV + 3 * D
C_BETA = C_ZB + D
C_A = C_BETA + HEADS
C_GATE = C_A + HEADS
IN_COLS = C_GATE + 2 * D
SMALL = IDX_DIM + IDX_HEADS
ROPE_THETA = 500000.0
ROT_A, ROT_I = DH // 4, IDX_DIM // 4
CONV = 4
NEVER = -1e30
TAKEN = -3e38

LEVELS = 7
CONSTS = ["ident", "upto", "before", "ones", "causal", "rot_a", "rot_i"] + \
         [f"low{i}" for i in range(LEVELS)] + [f"up{i}" for i in range(LEVELS)]


def shape_constants():
    i = np.arange(P)
    row, col = i[:, None], i[None, :]
    parts = {
        "ident": row == col,
        "upto": row <= col,
        "before": row < col,
        "ones": np.ones((P, P)),
        "causal": np.where(col > row, NEVER, 0.0),
    }
    for name, dim, rot in (("rot_a", DH, ROT_A), ("rot_i", IDX_DIM, ROT_I)):
        half = rot // 2
        m = np.zeros((P, P))
        for base in range(0, P, dim):
            for j in range(half):
                m[base + j, base + j + half] = -1.0
                m[base + j + half, base + j] = 1.0
        parts[name] = m.T
    for lvl in range(LEVELS):
        b = 1 << lvl
        low = (row // (2 * b) == col // (2 * b)) & (row % (2 * b) >= b) & (col % (2 * b) < b)
        parts[f"low{lvl}"], parts[f"up{lvl}"] = low, low.T
    table = np.concatenate([np.asarray(parts[n], np.float32) for n in CONSTS], axis=1)
    freq = np.zeros((P, 2), np.float32)
    for c, (dim, rot) in enumerate(((DH, ROT_A), (IDX_DIM, ROT_I))):
        half = rot // 2
        inv = np.float32(ROPE_THETA) ** (-np.arange(0, rot, 2, dtype=np.float32) / np.float32(rot))
        for base in range(0, P, dim):
            freq[base:base + half, c] = inv
            freq[base + half:base + rot, c] = inv
    token = np.tile(np.arange(S, dtype=np.float32), (P, 1))
    fall = np.tile(P - np.arange(P, dtype=np.float32), (P, 1))
    return np.concatenate([table, freq, token, fall, i[:, None].astype(np.float32)], axis=1)


class Parts:
    pass


Norm = namedtuple("Norm", "squares stat diag scale")


def slab(w, c=512):
    return w[:, :].rearrange("p (k c) -> p k c", c=c)


def over(ap, n):
    return ap.unsqueeze(2).to_broadcast([ap.shape[0], ap.shape[1], n])


def each(ap, n):
    return ap.unsqueeze(1).to_broadcast([ap.shape[0], n, ap.shape[1]])


@contextmanager
def stage(nc, tag, names, **kept):
    with ExitStack() as ctx:
        sems = {n: ctx.enter_context(nc.semaphore(f"{n}_{tag}")) for n in names.split()}
        with nc.Block() as block:
            yield block, namedtuple("Signals", [*sems, *kept])(*sems.values(), *kept.values())
        if kept:
            first = min(sem.num for sem in kept.values())
            nc.gpsimd.dma_reset(range(first, first + len(kept)))
        for sem in (*sems.values(), *kept.values()):
            nc.gpsimd.sem_clear(sem)
        nc.all_engine_barrier()


@contextmanager
def memory(nc, tag):
    with ExitStack() as ctx:
        def tensor(name, shape, dt=F32):
            return ctx.enter_context(nc.sbuf_tensor(f"{name}_{tag}", shape, dt))
        yield tensor


NORM_SEMS = "squared meaned rooted scaled scale_full scale_kept turned normed"


def norm_buffers(mem, g):
    return Norm(squares=g.YA, stat=mem("stat", [P, 4 * T]), diag=mem("diag_scale", [P, T, P]),
                scale=mem("scale", [P, S]))


def norm_scalar(nc, act, g, s, m, gain):
    for t in range(T // 2):
        nc.scalar.activation(m.squares[:, t, :], g.X[:, t, :], ACT.Square,
                             accum_out=m.stat[:, t:t + 1]).then_inc(s.squared, 1)
    act.wait_ge(s.meaned, 1)
    nc.scalar.activation(m.stat[:, 2 * T:3 * T], m.stat[:, T:2 * T], ACT.Sqrt).then_inc(s.rooted, 1)
    act.wait_ge(s.scale_full, 1)
    nc.scalar.activation(m.scale[:, :], g.PS[:, K - 1, :], ACT.Copy).then_inc(s.scale_kept, 1)


def norm_vector(nc, dve, g, s, m, gain):
    for t in range(T // 2, T):
        nc.vector.scalar_tensor_tensor(m.squares[:, t, :], g.X[:, t, :], 1.0, g.X[:, t, :], ALU.mult, ALU.mult,
                                       accum_out=m.stat[:, t:t + 1])
    dve.wait_ge(s.squared, T // 2)
    dve.drain()
    nc.vector.tensor_scalar(m.stat[:, T:2 * T], m.stat[:, 0:T], 1.0 / D, EPS,
                            ALU.mult, ALU.add).then_inc(s.meaned, 1)
    dve.wait_ge(s.rooted, 1)
    nc.vector.reciprocal(m.stat[:, 3 * T:4 * T], m.stat[:, 2 * T:3 * T])
    dve.drain()
    nc.vector.tensor_tensor(m.diag[:, :, :], each(g.ident, T), over(m.stat[:, 3 * T:4 * T], P),
                            ALU.mult).then_inc(s.scaled, 1)
    dve.wait_ge(s.gain_in, 16)
    dve.wait_ge(s.scale_kept, 1)
    for k in range(K):
        dve.wait_ge(s.turned, k + 1)
        nc.vector.scalar_tensor_tensor(g.feat[:, k, :], g.PS[:, k, :], gain[:, k:k + 1], m.scale[:, :],
                                       ALU.mult, ALU.mult).then_inc(s.normed, 1)


def norm_tensor(nc, pe, g, s, m):
    def turn(k):
        for t in range(T):
            last = nc.tensor.transpose(g.PS[:, k, t * P:(t + 1) * P], g.X[:, t, k * P:(k + 1) * P], g.ident)
        last.then_inc(s.turned, 1)

    for k in range(K - 1):
        turn(k)
    pe.wait_ge(s.scaled, 1)
    nc.tensor.matmul(g.PS[:, K - 1, :], g.ones, m.diag[:, :, :], start=True, stop=True).then_inc(s.scale_full, 1)
    pe.wait_ge(s.scale_kept, 1)
    turn(K - 1)
    pe.wait_ge(s.normed, K)


def to_feat(nc, g, out, weight, c0, width=P):
    for k in range(K):
        last = nc.tensor.matmul(out, weight[:, k, c0:c0 + width], g.feat[:, k, :], start=k == 0, stop=k == K - 1)
    return last


def to_rows(nc, g, out, weight, t, c0, width):
    for k in range(K):
        last = nc.tensor.matmul(out, g.feat[:, k, t * P:(t + 1) * P], weight[:, k, c0:c0 + width],
                                start=k == 0, stop=k == K - 1)
    return last


def gate_tensor(nc, pe, g, s, slabs, loaded):
    n = 0
    for i, slab in enumerate(slabs):
        pe.wait_ge(loaded[i], 16)
        for t in range(T):
            if n >= 8:
                pe.wait_ge(s.gate_on, n - 7)
            to_rows(nc, g, g.PS[:, n % 8, :], slab, t, 0, 512).then_inc(s.gate_full, 1)
            n += 1


def gate_scalar(nc, act, g, s, buf, funcs):
    n = 0
    for func in funcs:
        for t in range(T):
            act.wait_ge(s.gate_full, n + 1)
            if n >= 4:
                act.wait_ge(s.gated, n - 3)
            nc.scalar.activation(buf[:, n % 4, :], g.PS[:, n % 8, :], func).then_inc(s.gate_on, 1)
            n += 1


def gate_vector(nc, dve, s, buf, y, halves):
    n = 0
    for half in halves:
        for t in range(T):
            dve.wait_ge(s.gate_on, n + 1)
            part = y[:, t, half * 512:(half + 1) * 512]
            dve.drain()
            nc.vector.tensor_tensor(part, part, buf[:, n % 4, :], ALU.mult).then_inc(s.gated, 1)
            n += 1


def setup(nc, g, a):
    with memory(nc, "setup") as mem, stage(nc, "setup", "x_in const_in pos_in wrapped table") as (block, s):
        pos_i = mem("pos_i", [P, S], I32)
        pos = mem("pos", [P, S])
        ang = mem("ang", [P, 4, S])
        turn = mem("turn", [P, 4, S])
        whole = mem("whole", [P, 4, S], I32)

        @block.sync
        def _(sp):
            sp.dma_start(g.C[:, :], a.consts).then_inc(s.const_in, 16)
            sp.dma_start(pos_i[:, :], a.positions[0, :].partition_broadcast(P)).then_inc(s.pos_in, 16)
            sp.dma_start(g.X[:, :, :], a.x[0].rearrange("(t p) d -> p t d", p=P)).then_inc(s.x_in, 16)
            sp.wait_ge(s.x_in, 16)

        @block.vector
        def _(dve):
            dve.wait_ge(s.pos_in, 16)
            dve.wait_ge(s.const_in, 16)
            nc.vector.tensor_copy(pos[:, :], pos_i[:, :])
            dve.drain()
            for n in range(4):
                nc.vector.tensor_scalar(ang[:, n, :], pos[:, :], g.freq[:, n // 2:n // 2 + 1], None, ALU.mult)
            dve.drain()
            for n in range(4):
                nc.vector.tensor_scalar(turn[:, n, :], ang[:, n, :], 1.0 / (2 * np.pi), 0.25 * (1 - n % 2),
                                        ALU.mult, ALU.add)
            dve.drain()
            nc.vector.tensor_copy(whole[:, :, :], turn[:, :, :])
            dve.drain()
            nc.vector.tensor_copy(turn[:, :, :], whole[:, :, :])
            dve.drain()
            for part in (6.28125, 2 * np.pi - 6.28125):
                nc.vector.scalar_tensor_tensor(ang[:, :, :], turn[:, :, :], -part, ang[:, :, :], ALU.mult, ALU.add)
                dve.drain()
            for n in (0, 2):
                nc.vector.tensor_scalar(ang[:, n, :], ang[:, n, :], float(np.pi / 2), None, ALU.add)
            dve.drain()
            edge = 3.1415925
            nc.vector.tensor_scalar(ang[:, :, :], ang[:, :, :], edge, -edge, ALU.min, ALU.max).then_inc(s.wrapped, 1)

        @block.scalar
        def _(act):
            act.wait_ge(s.wrapped, 1)
            nc.scalar.activation(g.TAB[:, :, :], ang[:, :, :], ACT.Sin).then_inc(s.table, 1)


def rotary_vector(nc, dst, raw, rot, cos, sin, dve, tmp):
    nc.vector.tensor_tensor(tmp, rot, sin, ALU.mult)
    nc.vector.tensor_tensor(dst, raw, cos, ALU.mult)
    dve.drain()
    return nc.vector.tensor_tensor(dst, dst, tmp, ALU.add)


def mixer_inputs(nc, g, a, layer):
    names = NORM_SEMS + """ gain_in small_in kv_in qi_in row_in small_full small_done v_full v_done
        proj_full raw_done rot_full roped ki_squared ki_rooted ki_ready parted soft_e
        score_full relu_done summed wz0 wz1 wz2 wz3 gate_full gate_on gated next_in"""
    with memory(nc, "inputs") as mem, stage(nc, "inputs", names) as (block, s):
        m = norm_buffers(mem, g)
        gain = mem("gain", [P, K])
        w_small = mem("w_small", [P, K, 2 * SMALL])
        w_kv = mem("w_kv", [P, K, 512])
        w_qi = mem("w_qi", [P, K, 512])
        small = mem("small", [P, T, 2 * SMALL])
        raw = mem("raw", [P, 2, S])
        tmp = mem("tmp", [P, S])
        qi = mem("qi", [P, IDX_HEADS // 2, S])
        ki = mem("ki", [P, 2, S])
        ki_rows = mem("ki_rows", [P, T, 2, P])
        ki_sq = mem("ki_sq", [P, T, IDX_DIM])
        ki_gain = mem("ki_gain", [P, IDX_DIM])
        wi = mem("wi", [P, T, IDX_HEADS])
        rowp = mem("rowp", [P, 2 * HEADS])
        soft = mem("soft", [P, 6, T * HEADS])
        relu = mem("relu", [P, 4, S])
        top8 = mem("top8", [P, 8])
        w_z = mem("w_z", [P, K, 512])
        gates = (w_z, w_kv, w_qi, w_z)
        loaded = (s.wz0, s.wz1, s.wz2, s.wz3)
        sigm = mem("sigm", [P, 4, 512])
        GATES = [(i, t) for i in range(4) for t in range(T)]
        UNITS = [("k", j) for j in range(KV_HEADS)] + [("q", j) for j in range(IDX_HEADS // 2)] + \
                [("i", j) for j in range(2)]

        @block.sync
        def _(sp):
            sp.dma_start(gain[:, :], a.norm_gain[layer]).then_inc(s.gain_in, 16)
            sp.dma_start(w_small[:, :, 0:SMALL], a.w_in[layer][:, :, C_KI:C_KI + SMALL]).then_inc(s.small_in, 16)
            sp.dma_start(w_small[:, :, SMALL:], a.w_in[layer][:, :, C_BETA:C_BETA + SMALL]).then_inc(s.small_in, 16)
            sp.dma_start(w_kv[:, :, :], a.w_in[layer][:, :, C_K:C_Z]).then_inc(s.kv_in, 16)
            sp.dma_start(w_qi[:, :, :], a.w_in[layer][:, :, C_QI:C_KI]).then_inc(s.qi_in, 16)
            sp.dma_start(ki_gain[:, :], a.idx_k_gain[layer].partition_broadcast(P)).then_inc(s.row_in, 16)
            sp.dma_start(rowp[:, 0:HEADS], a.dt_bias[layer].partition_broadcast(P)).then_inc(s.row_in, 16)
            sp.dma_start(rowp[:, HEADS:], a.a_log[layer].partition_broadcast(P)).then_inc(s.row_in, 16)
            for i, (c, units) in enumerate(((C_Z, 0), (C_Z + 512, 2), (C_GATE, 6), (C_GATE + 512, 0))):
                if units:
                    sp.wait_ge(s.proj_full, units)
                if i == 3:
                    sp.wait_ge(s.gate_full, T)
                sp.dma_start(gates[i][:, :, :], a.w_in[layer][:, :, c:c + 512]).then_inc(loaded[i], 16)
            sp.dma_start(slab(g.W_odd[1]), a.w_in[layer][:, :, C_Q:C_Q + 512]).then_inc(s.next_in, 16)
            sp.wait_ge(s.next_in, 16)

        @block.tensor
        def _(pe):
            norm_tensor(nc, pe, g, s, m)
            pe.wait_ge(s.small_in, 32)
            for t in range(T):
                to_rows(nc, g, g.PS[:, 4 + t, 0:2 * SMALL], w_small, t, 0, 2 * SMALL).then_inc(s.small_full, 1)
            pe.wait_ge(s.kv_in, 16)
            for t in range(T):
                pe.wait_ge(s.small_done, t + 1)
                to_rows(nc, g, g.PS[:, 4 + t, 0:256], w_kv, t, 256, 256).then_inc(s.v_full, 1)

            def project(u):
                kind, j = UNITS[u]
                if u >= 2:
                    pe.wait_ge(s.raw_done, u - 1)
                if kind == "k":
                    to_feat(nc, g, g.PS[:, u % 2, :], w_kv, j * P).then_inc(s.proj_full, 1)
                elif kind == "q":
                    if j == 0:
                        pe.wait_ge(s.qi_in, 16)
                    to_feat(nc, g, g.PS[:, u % 2, :], w_qi, j * P).then_inc(s.proj_full, 1)
                else:
                    if j == 0:
                        pe.wait_ge(s.ki_ready, 1)
                    for t in range(T):
                        last = nc.tensor.transpose(g.PS[:, u % 2, t * P:(t + 1) * P], ki_rows[:, t, j, :], g.ident)
                    last.then_inc(s.proj_full, 1)

            project(0)
            for u, (kind, _j) in enumerate(UNITS):
                if u + 1 < len(UNITS):
                    project(u + 1)
                pe.wait_ge(s.raw_done, u + 1)
                if u >= 2:
                    pe.wait_ge(s.roped, u - 1)
                nc.tensor.matmul(g.PS[:, 2 + u % 2, :], g.rot_a if kind == "k" else g.rot_i, raw[:, u % 2, :],
                                 start=True, stop=True).then_inc(s.rot_full, 1)
            pe.wait_ge(s.roped, len(UNITS))
            pe.wait_ge(s.v_done, T)

            def gate(i, k):
                slab_of, t = GATES[i]
                if k == 0:
                    if t == 0:
                        pe.wait_ge(loaded[slab_of], 16)
                    if i >= 4:
                        pe.wait_ge(s.gate_on, i - 3)
                last = nc.tensor.matmul(g.PS[:, 4 + i % 4, :], g.feat[:, k, t * P:(t + 1) * P], gates[slab_of][:, k, :],
                                        start=k == 0, stop=k == K - 1)
                if k == K - 1:
                    last.then_inc(s.gate_full, 1)

            n = 0
            for tb in range(1, T):
                keys = P * (tb + 1)
                for h in range(IDX_HEADS):
                    if n >= 4:
                        pe.wait_ge(s.relu_done, n - 3)
                    if n >= 1:
                        gate((n - 1) // K, (n - 1) % K)
                    nc.tensor.matmul(g.PS[:, n % 4, 0:keys], qi[:, h // 2, tb * P:(tb + 1) * P],
                                     ki[:, h % 2, 0:keys], start=True, stop=True).then_inc(s.score_full, 1)
                    n += 1
            for part in range(n - 1, K * len(GATES)):
                gate(part // K, part % K)

        @block.scalar
        def _(act):
            norm_scalar(nc, act, g, s, m, gain)
            for t in range(T):
                act.wait_ge(s.small_full, t + 1)
                nc.scalar.activation(small[:, t, :], g.PS[:, 4 + t, 0:2 * SMALL], ACT.Copy).then_inc(s.small_done, 1)
            for t in range(T):
                act.wait_ge(s.v_full, t + 1)
                nc.scalar.activation(g.V[:, t, :], g.PS[:, 4 + t, 0:256], ACT.Copy).then_inc(s.v_done, 1)
            act.wait_ge(s.ki_squared, 1)
            nc.scalar.activation(m.stat[:, 2 * T:3 * T], m.stat[:, T:2 * T], ACT.Sqrt).then_inc(s.ki_rooted, 1)
            for u in range(len(UNITS)):
                act.wait_ge(s.proj_full, u + 1)
                if u >= 2:
                    act.wait_ge(s.roped, u - 1)
                nc.scalar.activation(raw[:, u % 2, :], g.PS[:, u % 2, :], ACT.Copy).then_inc(s.raw_done, 1)
            for t in range(T):
                nc.scalar.activation(g.beta[:, t, :], small[:, t, SMALL:SMALL + HEADS], ACT.Sigmoid)
            act.wait_ge(s.parted, 1)
            act.wait_ge(s.row_in, 48)
            nc.scalar.activation(soft[:, 2, :], soft[:, 1, :], ACT.Exp, scale=-1.0)
            nc.scalar.activation(soft[:, 4, 0:HEADS], rowp[:, HEADS:], ACT.Exp).then_inc(s.soft_e, 1)

            def gate(i):
                slab_of, t = GATES[i]
                act.wait_ge(s.gate_full, i + 1)
                if slab_of < 2:
                    nc.scalar.activation(g.YB[:, t, slab_of * 512:(slab_of + 1) * 512], g.PS[:, 4 + i % 4, :],
                                         ACT.Silu).then_inc(s.gate_on, 1)
                else:
                    if i >= 12:
                        act.wait_ge(s.gated, i - 11)
                    nc.scalar.activation(sigm[:, i % 4, :], g.PS[:, 4 + i % 4, :], ACT.Sigmoid).then_inc(s.gate_on, 1)

            n = 0
            for tb in range(1, T):
                keys = P * (tb + 1)
                for h in range(IDX_HEADS):
                    act.wait_ge(s.score_full, n + 1)
                    if n >= 4:
                        act.wait_ge(s.summed, n - 3)
                    nc.scalar.activation(relu[:, n % 4, 0:keys], g.PS[:, n % 4, 0:keys],
                                         ACT.Relu).then_inc(s.relu_done, 1)
                    if n % K == 0 and n > 0:
                        gate(n // K - 1)
                    n += 1
            for i in range((n - 1) // K, len(GATES)):
                gate(i)

        @block.gpsimd
        def _(pool):
            for i, (slab_of, t) in enumerate(GATES):
                if slab_of >= 2:
                    pool.wait_ge(s.gate_on, i + 1)
                    part = g.YB[:, t, (slab_of - 2) * 512:(slab_of - 1) * 512]
                    nc.gpsimd.tensor_tensor(part, part, sigm[:, i % 4, :], ALU.mult).then_inc(s.gated, 1)

        @block.vector
        def _(dve):
            norm_vector(nc, dve, g, s, m, gain)
            nc.vector.memset(ki_rows[:, :, :, :], 0.0)
            dve.wait_ge(s.small_done, T)
            dve.wait_ge(s.row_in, 48)
            nc.vector.tensor_tensor(ki_sq[:, :, :], small[:, :, 0:IDX_DIM], small[:, :, 0:IDX_DIM], ALU.mult)
            nc.vector.tensor_scalar(wi[:, :, :], small[:, :, IDX_DIM:SMALL],
                                    IDX_HEADS ** -0.5 * IDX_DIM ** -0.5, None, ALU.mult)
            dve.drain()
            nc.vector.tensor_reduce(m.stat[:, 0:T], ki_sq[:, :, :], AX.X, ALU.add)
            dve.drain()
            nc.vector.tensor_scalar(m.stat[:, T:2 * T], m.stat[:, 0:T], 1.0 / IDX_DIM, EPS,
                                    ALU.mult, ALU.add).then_inc(s.ki_squared, 1)
            dve.wait_ge(s.ki_rooted, 1)
            nc.vector.reciprocal(m.stat[:, 3 * T:4 * T], m.stat[:, 2 * T:3 * T])
            dve.drain()
            nc.vector.tensor_tensor(ki_sq[:, :, :], small[:, :, 0:IDX_DIM], over(m.stat[:, 3 * T:4 * T], IDX_DIM),
                                    ALU.mult)
            dve.drain()
            for j in range(2):
                last = nc.vector.tensor_tensor(ki_rows[:, :, j, j * IDX_DIM:(j + 1) * IDX_DIM], ki_sq[:, :, :],
                                               each(ki_gain[:, :], T), ALU.mult)
            dve.drain().then_inc(s.ki_ready, 1)
            nc.vector.tensor_tensor(soft[:, 0, :].rearrange("p (t h) -> p t h", t=T),
                                    small[:, :, SMALL + HEADS:SMALL + 2 * HEADS], each(rowp[:, 0:HEADS], T), ALU.add)
            dve.drain()
            nc.vector.scalar_tensor_tensor(soft[:, 1, :], soft[:, 0, :], -1.0, soft[:, 0, :], ALU.mult, ALU.max)
            dve.drain().then_inc(s.parted, 1)
            for u, (kind, j) in enumerate(UNITS):
                dve.wait_ge(s.rot_full, u + 1)
                dst = {"k": g.KT, "q": qi, "i": ki}[kind][:, j, :]
                table = 0 if kind == "k" else 2
                rotary_vector(nc, dst, raw[:, u % 2, :], g.PS[:, 2 + u % 2, :], g.TAB[:, table, :],
                              g.TAB[:, table + 1, :], dve, tmp[:, :]).then_inc(s.roped, 1)
                dve.drain()
            dve.wait_ge(s.soft_e, 1)
            log1p_vector(nc, dve, soft[:, 2, :], soft[:, 3, :], soft[:, 5, :], soft[:, 1, :])
            nc.vector.scalar_tensor_tensor(soft[:, 0, :], soft[:, 0, :], 0.0, soft[:, 2, :], ALU.max, ALU.add)
            dve.drain()
            nc.vector.scalar_tensor_tensor(g.decay[:, :, :], soft[:, 0, :].rearrange("p (t h) -> p t h", t=T), -1.0,
                                           each(soft[:, 4, 0:HEADS], T), ALU.mult, ALU.mult)
            nc.vector.tensor_copy(g.BIAS[:, 0:P], g.causal)
            n = 0
            for tb in range(1, T):
                keys, at = P * (tb + 1), g.bias_at[tb]
                score = g.BIAS[:, at:at + keys]
                for h in range(IDX_HEADS):
                    dve.wait_ge(s.relu_done, n + 1)
                    w = wi[:, tb, h:h + 1]
                    if h == 0:
                        nc.vector.tensor_scalar(score, relu[:, n % 4, 0:keys], w, None, ALU.mult).then_inc(s.summed, 1)
                    else:
                        nc.vector.scalar_tensor_tensor(score, relu[:, n % 4, 0:keys], w, score, ALU.mult,
                                                       ALU.add).then_inc(s.summed, 1)
                    dve.drain()
                    n += 1
                edge = g.BIAS[:, at + keys - P:at + keys]
                nc.vector.tensor_tensor(edge, edge, g.causal, ALU.add)
                dve.drain()
            for tb in range(1, T):
                keys, at = P * (tb + 1), g.bias_at[tb]
                score = g.BIAS[:, at:at + keys]
                for _round in range(TOPK // 8):
                    nc.vector.max(top8[:, :], score)
                    dve.drain()
                    nc.vector.match_replace(score, top8[:, :], score, TAKEN)
                    dve.drain()
                nc.vector.tensor_scalar(score, score, -2e38, NEVER, ALU.is_gt, ALU.mult)


def log1p_vector(nc, dve, x, z, z2, acc):
    nc.vector.tensor_scalar(z, x, 2.0, None, ALU.add)
    dve.drain()
    nc.vector.reciprocal(z, z)
    dve.drain()
    nc.vector.tensor_tensor(z, z, x, ALU.mult)
    dve.drain()
    nc.vector.tensor_tensor(z2, z, z, ALU.mult)
    dve.drain()
    nc.vector.tensor_scalar(acc, z2, 1.0 / 15, 1.0 / 13, ALU.mult, ALU.add)
    dve.drain()
    for odd in (11, 9, 7, 5, 3, 1):
        nc.vector.tensor_tensor(acc, acc, z2, ALU.mult)
        dve.drain()
        nc.vector.tensor_scalar(acc, acc, 1.0 / odd, None, ALU.add)
        dve.drain()
    nc.vector.scalar_tensor_tensor(x, acc, 2.0, z, ALU.mult, ALU.mult)
    dve.drain()


UNITS_OF_PAIR = [(h, j) for h in range(2) for j in range(3)]


def pair_weights(g, h):
    each_head = K * 3 * P
    return g.w_pair[:, h * each_head:(h + 1) * each_head].rearrange("p (k j c) -> p k j c", k=K, j=3)


def gate_slab(g):
    return slab(g.w_pair[:, 0:K * 512])


def gate_kept(g):
    return g.pad[:, :, :, :].rearrange("p h j t -> p (h j t)")[:, 0:T * 512].rearrange("p (t c) -> p t c", t=T)


def pair_loads(g, a, layer, pair):
    return [(pair_weights(g, h)[:, :, j, :], a.w_heads[layer, pair][h, j]) for h, j in UNITS_OF_PAIR]


def project_unit(nc, g, u, bank):
    h, j = UNITS_OF_PAIR[u]
    for k in range(K):
        last = nc.tensor.matmul(g.PS[:, bank, :], pair_weights(g, h)[:, k, j, :], g.feat[:, k, :],
                                start=k == 0, stop=k == K - 1)
    return last


def keep_unit(nc, g, u, bank):
    h, j = UNITS_OF_PAIR[u]
    return nc.scalar.activation(g.pad[:, h, j, CONV - 1:], g.PS[:, bank, :], ACT.Copy)


def attention(nc, g, a, layer):
    names = """wq1 proj_full raw_done rot_full roped score_full masked max_done exp_done
        turned turned_done out_full out_done w0 w1 w2 w3 w4 w5 next_in taps_in unit_full padded"""
    scale = DH ** -0.5
    with memory(nc, "attn") as mem, stage(nc, "attn", names) as (block, s):
        loaded = (s.w0, s.w1, s.w2, s.w3, s.w4, s.w5)
        U = len(UNITS_OF_PAIR)
        w = [g.W_odd[1], mem("w1", [P, K * 512])]
        w = [slab(v) for v in w]
        q_raw = mem("q_raw", [P, S])
        tmp = mem("tmp", [P, S])
        qt = mem("qt", [P, 2, S])
        score = mem("score", [P, 2, S])
        prob = mem("prob", [P, 2, S])
        prob_t = mem("prob_t", [P, 2, S])
        neg_max = mem("neg_max", [P, HEADS * T])
        total = mem("total", [P, HEADS * T])
        steps = [(h, tb) for h in range(HEADS) for tb in range(T)]
        N = len(steps)

        @block.sync
        def _(sp):
            sp.dma_start(w[1], a.w_in[layer][:, :, C_Q + 512:C_Q + 1024]).then_inc(s.wq1, 16)
            sp.dma_start(g.taps[:, :, :, :], a.conv_w[layer, 0]).then_inc(s.taps_in, 16)
            for (dst, src), sem in zip(pair_loads(g, a, layer, 0), loaded):
                sp.dma_start(dst, src).then_inc(sem, 16)
            for u, (dst, src) in enumerate(pair_loads(g, a, layer, 1)):
                sp.wait_ge(s.unit_full, u + 1)
                sp.dma_start(dst, src).then_inc(s.next_in, 16)
            sp.wait_ge(s.taps_in, 16)
            sp.wait_ge(s.next_in, 16 * U)

        @block.tensor
        def _(pe):
            def project(h):
                if h == GROUP:
                    pe.wait_ge(s.wq1, 16)
                if h >= 1:
                    pe.wait_ge(s.raw_done, h)
                if h >= 2:
                    pe.wait_ge(s.padded, h - 1)
                to_feat(nc, g, g.PS[:, 0, :], w[h // GROUP], (h % GROUP) * P).then_inc(s.proj_full, 1)

            def pair_unit(u):
                pe.wait_ge(loaded[u], 16)
                pe.wait_ge(s.raw_done, u + 2)
                project_unit(nc, g, u, 0).then_inc(s.unit_full, 1)

            def rotate(h):
                pe.wait_ge(s.raw_done, h + 1)
                if h >= 1:
                    pe.wait_ge(s.roped, h)
                nc.tensor.matmul(g.PS[:, 1, :], g.rot_a, q_raw[:, :], start=True, stop=True).then_inc(s.rot_full, 1)

            def turn(n):
                tb = steps[n][1]
                pe.wait_ge(s.exp_done, n + 1)
                if n >= 2:
                    pe.wait_ge(s.turned_done, n - 1)
                for kb in range(tb + 1):
                    last = nc.tensor.transpose(g.PS[:, 4 + n % 2, kb * P:(kb + 1) * P],
                                               prob[:, n % 2, kb * P:(kb + 1) * P], g.ident)
                last.then_inc(s.turned, 1)

            def weigh(n):
                h, tb = steps[n]
                v0 = (h // GROUP) * DH
                pe.wait_ge(s.turned_done, n + 1)
                if n >= 2:
                    pe.wait_ge(s.out_done, n - 1)
                for kb in range(tb + 1):
                    last = nc.tensor.matmul(g.PS[:, 6 + n % 2, 0:DH], prob_t[:, n % 2, kb * P:(kb + 1) * P],
                                            g.V[:, kb, v0:v0 + DH], start=kb == 0, stop=kb == tb)
                last.then_inc(s.out_full, 1)

            project(0)
            rotate(0)
            for n, (h, tb) in enumerate(steps):
                if tb == 0:
                    pe.wait_ge(s.roped, h + 1)
                if n >= 2:
                    pe.wait_ge(s.masked, n - 1)
                keys = P * (tb + 1)
                nc.tensor.matmul(g.PS[:, 2 + n % 2, 0:keys], qt[:, h % 2, tb * P:(tb + 1) * P],
                                 g.KT[:, h // GROUP, 0:keys], start=True, stop=True).then_inc(s.score_full, 1)
                if tb == 0 and h + 1 < HEADS:
                    project(h + 1)
                if tb == 2 and h + 1 < HEADS:
                    rotate(h + 1)
                if tb == 2 and h < U:
                    pair_unit(h)
                if n >= 1:
                    turn(n - 1)
                if n >= 2:
                    weigh(n - 2)
            turn(N - 1)
            weigh(N - 2)
            weigh(N - 1)

        @block.scalar
        def _(act):
            def keep(h):
                act.wait_ge(s.proj_full, h + 1)
                if h >= 1:
                    act.wait_ge(s.roped, h)
                nc.scalar.activation(q_raw[:, :], g.PS[:, 0, :], ACT.Copy).then_inc(s.raw_done, 1)

            def move(n):
                keys = P * (steps[n][1] + 1)
                act.wait_ge(s.turned, n + 1)
                if n >= 2:
                    act.wait_ge(s.out_full, n - 1)
                nc.scalar.activation(prob_t[:, n % 2, 0:keys], g.PS[:, 4 + n % 2, 0:keys],
                                     ACT.Copy).then_inc(s.turned_done, 1)

            keep(0)
            for n, (h, tb) in enumerate(steps):
                keys = P * (tb + 1)
                if tb == 0 and 1 <= h <= U:
                    act.wait_ge(s.unit_full, h)
                    keep_unit(nc, g, h - 1, 0).then_inc(s.padded, 1)
                act.wait_ge(s.max_done, n + 1)
                if n >= 2:
                    act.wait_ge(s.turned, n - 1)
                nc.scalar.activation(prob[:, n % 2, 0:keys], score[:, n % 2, 0:keys], ACT.Exp,
                                     bias=neg_max[:, n:n + 1], accum_out=total[:, n:n + 1]).then_inc(s.exp_done, 1)
                if tb == 1 and h + 1 < HEADS:
                    keep(h + 1)
                if n >= 1:
                    move(n - 1)
            move(N - 1)

        @block.vector
        def _(dve):
            def rope(h):
                dve.wait_ge(s.rot_full, h + 1)
                if h >= 2:
                    dve.wait_ge(s.score_full, T * (h - 1))
                rotary_vector(nc, qt[:, h % 2, :], q_raw[:, :], g.PS[:, 1, :], g.TAB[:, 0, :], g.TAB[:, 1, :],
                              dve, tmp[:, :]).then_inc(s.roped, 1)

            def finish(n):
                h, tb = steps[n]
                dve.wait_ge(s.out_full, n + 1)
                nc.vector.reciprocal(total[:, n:n + 1], total[:, n:n + 1])
                dve.drain()
                nc.vector.scalar_tensor_tensor(g.YB[:, tb, h * DH:(h + 1) * DH], g.PS[:, 6 + n % 2, 0:DH],
                                               total[:, n:n + 1], g.YB[:, tb, h * DH:(h + 1) * DH],
                                               ALU.mult, ALU.mult).then_inc(s.out_done, 1)

            for h in range(2):
                nc.vector.memset(g.pad[:, h, :, 0:CONV - 1], 0.0)
            rope(0)
            for n, (h, tb) in enumerate(steps):
                keys, at = P * (tb + 1), g.bias_at[tb]
                dve.wait_ge(s.score_full, n + 1)
                if n >= 2:
                    dve.wait_ge(s.exp_done, n - 1)
                nc.vector.scalar_tensor_tensor(score[:, n % 2, 0:keys], g.PS[:, 2 + n % 2, 0:keys], scale,
                                               g.BIAS[:, at:at + keys], ALU.mult, ALU.add).then_inc(s.masked, 1)
                dve.drain()
                nc.vector.tensor_reduce(neg_max[:, n:n + 1], score[:, n % 2, 0:keys], AX.X, ALU.max,
                                        negate=True).then_inc(s.max_done, 1)
                if tb == 3 and h + 1 < HEADS:
                    rope(h + 1)
                if n >= 2:
                    finish(n - 2)
            finish(N - 2)
            finish(N - 1)


def delta_heads(nc, g, a, layer, pair, ahead):
    names = """next_in cw_in proj_full padded silu_done conv_done q_squared k_turned v_turned norm_in stat_done root_done
        factors cum_full cum_copied rows_full diag_done clipped decayed qk_full kk_full masks_done first_full
        y_full y_done xy_full yx_full xt_done x_done x_sub xt_sub dk_done
        ks_full r_done vn_full vn_done qs_full o_full o_done su_full s_done"""
    A2 = range(2)
    tag = f"delta{ahead}"
    with memory(nc, tag) as mem, stage(nc, tag, names) as (block, s):
        cw, pad = g.taps, g.pad
        cv = mem("cv", [P, 2, 3, S])
        sq = mem("sq", [P, 2, S])
        kd = mem("kd", [P, 2, T, P])
        bv = mem("bv", [P, 2, T, P])
        st = mem("st", [P, 12, T, 2])
        cum = mem("cum", [P, 3, T, 2])
        diag = mem("diag", [P, 2, 2, S])
        et = mem("et", [P, 2, S])
        ea = mem("ea", [P, 2, S])
        qkt = mem("qkt", [P, 2, S])
        lt = mem("lt", [P, 2, S])
        x = mem("x", [P, 2, S])
        xt = mem("xt", [P, 2, S])
        y = mem("y", [P, 2, S])
        mx = mem("mx", [P, 2, S])
        mxt = mem("mxt", [P, 2, S])
        state = mem("state", [P, 2, P])
        r = mem("r", [P, 2, P])
        vn = mem("vn", [P, 2, P])
        o1 = mem("o1", [P, 2, P])
        PS = g.PS
        QK = ((6, 7), (2, 4))

        def tile(ap, h, t):
            return ap[:, h, t * P:(t + 1) * P]

        def tiles(ap):
            return ap.rearrange("p (t c) -> p t c", t=T)

        end_decay = cum[:, 2, :, :]

        @block.sync
        def _(sp):
            if ahead >= 1:
                sp.wait_ge(s.silu_done, 6)
                sp.dma_start(cw[:, :, :, :], a.conv_w[layer, pair + 1]).then_inc(s.cw_in, 16)
            if ahead >= 2:
                for u, (dst, src) in enumerate(pair_loads(g, a, layer, pair + 2)):
                    sp.wait_ge(s.proj_full, u + 1)
                    sp.dma_start(dst, src).then_inc(s.next_in, 16)
                sp.wait_ge(s.next_in, 16 * len(UNITS_OF_PAIR))
            else:
                sp.wait_ge(s.proj_full, 6 if ahead == 1 else T)
                c = C_ZB if ahead == 1 else C_ZB + 512
                sp.dma_start(gate_slab(g), a.w_in[layer][:, :, c:c + 512]).then_inc(s.next_in, 16)
                sp.wait_ge(s.next_in, 16)
            if ahead >= 1:
                sp.wait_ge(s.cw_in, 16)

        @block.tensor
        def _(pe):
            def project(u):
                if ahead >= 1 or u < T:
                    if u >= 2:
                        pe.wait_ge(s.padded, u - 1)
                    if ahead >= 1:
                        last = project_unit(nc, g, u, u % 2)
                    else:
                        last = to_rows(nc, g, PS[:, u % 2, :], gate_slab(g), u, 0, 512)
                    last.then_inc(s.proj_full, 1)

            pe.wait_ge(s.dk_done, 1)
            nc.tensor.matmul(PS[:, 6, 0:2 * T], g.upto, cum[:, 0, :, :].rearrange("p t h -> p (t h)"), start=True, stop=True)
            nc.tensor.matmul(PS[:, 6, 2 * T:4 * T], g.ones, cum[:, 0, :, :].rearrange("p t h -> p (t h)"),
                             start=True, stop=True).then_inc(s.cum_full, 1)
            project(0)
            for h in A2:
                project(1 + h)
                pe.wait_ge(s.conv_done, 3 * (h + 1))
                for t in range(T):
                    last = nc.tensor.transpose(PS[:, 2 + 2 * h, t * P:(t + 1) * P], cv[:, h, 1, t * P:(t + 1) * P], g.ident)
                last.then_inc(s.k_turned, 1)
                for t in range(T):
                    last = nc.tensor.transpose(PS[:, 3 + 2 * h, t * P:(t + 1) * P], cv[:, h, 2, t * P:(t + 1) * P], g.ident)
                last.then_inc(s.v_turned, 1)
                pe.wait_ge(s.q_squared, h + 1)
                if h == 1:
                    pe.wait_ge(s.cum_copied, 1)
                for t in range(T):
                    last = nc.tensor.matmul(PS[:, 7 - h, t:t + 1], tile(sq, h, t), g.ones[:, 0:1],
                                            start=True, stop=True)
                last.then_inc(s.norm_in, 1)
            project(3)
            for h in A2:
                pe.wait_ge(s.diag_done, h + 1)
                for j in A2:
                    last = nc.tensor.matmul(PS[:, 2 + 2 * h + j, :], g.ones, diag[:, h, j, :], start=True, stop=True)
                last.then_inc(s.rows_full, 1)
            for h in A2:
                if h == 1:
                    project(4)
                    pe.wait_ge(s.clipped, 2)
                for j in A2:
                    for t in range(T):
                        last = nc.tensor.matmul(PS[:, QK[h][j], t * P:(t + 1) * P],
                                                cv[:, h, 1, t * P:(t + 1) * P], cv[:, h, j, t * P:(t + 1) * P],
                                                start=True, stop=True)
                last.then_inc(s.qk_full, 1)
            project(5)
            for h in A2:
                pe.wait_ge(s.masks_done, h + 1)
                for t in range(T):
                    last = nc.tensor.matmul(PS[:, 6 + h, t * P:(t + 1) * P], tile(lt, h, t), g.ident, start=True, stop=True)
                last.then_inc(s.first_full, 1)
            for lvl in range(1, LEVELS):
                for h in A2:
                    pe.wait_ge(s.x_sub, 2 * (lvl - 1) + h + 1)
                    for t in range(T):
                        last = nc.tensor.matmul(PS[:, 2 + h, t * P:(t + 1) * P], tile(lt, h, t), tile(x, h, t),
                                                start=True, stop=True)
                    last.then_inc(s.y_full, 1)
                for h in A2:
                    n = 2 * (lvl - 1) + h
                    pe.wait_ge(s.y_done, n + 1)
                    if lvl > 1:
                        pe.wait_ge(s.xt_sub, n - 1)
                    for t in range(T):
                        last = nc.tensor.matmul(PS[:, 4 + h, t * P:(t + 1) * P], tile(y, h, t), tile(xt, h, t),
                                                start=True, stop=True)
                    last.then_inc(s.yx_full, 1)
                    if lvl < LEVELS - 1:
                        for t in range(T):
                            last = nc.tensor.matmul(PS[:, 6 + h, t * P:(t + 1) * P], tile(xt, h, t), tile(y, h, t),
                                                    start=True, stop=True)
                        last.then_inc(s.xy_full, 1)
            for t in range(T):
                for h in A2:
                    n = 2 * t + h
                    if t == 0:
                        pe.wait_ge(s.xt_sub, 2 * (LEVELS - 2) + h + 1)
                    if t > 0:
                        if n == 2:
                            pe.wait_ge(s.padded, 6 if ahead >= 1 else T)
                        pe.wait_ge(s.s_done, n - 1)
                        nc.tensor.matmul(PS[:, h, 0:P], cv[:, h, 1, t * P:(t + 1) * P], state[:, h, :],
                                         start=True, stop=True).then_inc(s.ks_full, 1)
                        pe.wait_ge(s.o_done, n - 1)
                        nc.tensor.matmul(PS[:, 4 + h, 0:P], cv[:, h, 0, t * P:(t + 1) * P], state[:, h, :],
                                         start=True, stop=True).then_inc(s.qs_full, 1)
                for h in A2:
                    n = 2 * t + h
                    pe.wait_ge(s.r_done, n + 1)
                    nc.tensor.matmul(PS[:, 2 + h, 0:P], tile(xt, h, t), r[:, h, :], start=True,
                                     stop=True).then_inc(s.vn_full, 1)
                for h in A2:
                    n = 2 * t + h
                    pe.wait_ge(s.vn_done, n + 1)
                    nc.tensor.matmul(PS[:, 6 + h, P:2 * P], tile(qkt, h, t), vn[:, h, :], start=True,
                                     stop=True).then_inc(s.o_full, 1)
                    if t < T - 1:
                        nc.tensor.matmul(PS[:, 2 + h, P:2 * P], kd[:, h, t, :], vn[:, h, :], start=True,
                                         stop=True).then_inc(s.su_full, 1)

        @block.scalar
        def _(act):
            def keep(u):
                if ahead >= 1 or u < T:
                    act.wait_ge(s.proj_full, u + 1)
                    if ahead >= 1:
                        last = keep_unit(nc, g, u, u % 2)
                    else:
                        last = nc.scalar.activation(gate_kept(g)[:, u, :], PS[:, u % 2, :], ACT.Silu)
                    last.then_inc(s.padded, 1)

            act.wait_ge(s.cum_full, 1)
            nc.scalar.activation(cum[:, 1:3, :, :].rearrange("p a t h -> p (a t h)"), PS[:, 6, 0:4 * T],
                                 ACT.Copy).then_inc(s.cum_copied, 1)
            act.drain()
            nc.scalar.activation(st[:, 10, :, :], cum[:, 1, :, :], ACT.Exp)
            for h in A2:
                for j in range(3):
                    act.wait_ge(s.silu_done, 3 * h + j + 1)
                    nc.scalar.activation(cv[:, h, j, :], cv[:, h, j, :], ACT.Silu).then_inc(s.conv_done, 1)
                act.drain()
                nc.scalar.activation(sq[:, h, :], cv[:, h, 0, :], ACT.Square).then_inc(s.q_squared, 1)
                keep(h)
            keep(2)
            act.wait_ge(s.stat_done, 1)
            nc.scalar.activation(st[:, 2:4, :, :], st[:, 0:2, :, :], ACT.Sqrt).then_inc(s.root_done, 1)
            act.wait_ge(s.factors, 1)
            nc.scalar.activation(st[:, 11, :, :], st[:, 11, :, :], ACT.Exp)
            nc.scalar.activation(end_decay, end_decay, ACT.Exp).then_inc(s.decayed, 1)
            keep(3)
            for h in A2:
                act.wait_ge(s.clipped, h + 1)
                nc.scalar.activation(et[:, h, :], et[:, h, :], ACT.Exp).then_inc(s.decayed, 1)
            keep(4)
            keep(5)
            for lvl in range(1, LEVELS):
                for h in A2:
                    n = 2 * (lvl - 1) + h
                    act.wait_ge(s.y_full, n + 1)
                    nc.scalar.activation(y[:, h, :], PS[:, 2 + h, :], ACT.Copy).then_inc(s.y_done, 1)
            for t in range(T):
                for h in A2:
                    act.wait_ge(s.vn_full, 2 * t + h + 1)
                    if t > 0:
                        act.wait_ge(s.su_full, 2 * t + h - 1)
                        act.wait_ge(s.o_full, 2 * t + h - 1)
                    nc.scalar.activation(vn[:, h, :], PS[:, 2 + h, 0:P], ACT.Copy).then_inc(s.vn_done, 1)

        @block.vector
        def _(dve):
            nc.vector.tensor_copy(cum[:, 0, :, :], g.decay[:, :, bass.ds(2 * pair, 2)])
            nc.vector.tensor_copy(g.beta_pair[:, :, :], g.beta[:, :, bass.ds(2 * pair, 2)])
            dve.drain().then_inc(s.dk_done, 1)
            for h in A2:
                for j in range(3):
                    acc = cv[:, h, j, :]
                    nc.vector.tensor_scalar(acc, pad[:, h, j, 0:S], cw[:, h, j, 0:1], None, ALU.mult)
                    for tap in range(1, CONV):
                        dve.drain()
                        last = nc.vector.scalar_tensor_tensor(acc, pad[:, h, j, tap:tap + S], cw[:, h, j, tap:tap + 1],
                                                              acc, ALU.mult, ALU.add)
                    last.then_inc(s.silu_done, 1)
            for h in A2:
                dve.wait_ge(s.k_turned, h + 1)
                nc.vector.tensor_copy(kd[:, h, :, :], tiles(PS[:, 2 + 2 * h, :]))
                dve.wait_ge(s.v_turned, h + 1)
                nc.vector.tensor_tensor(bv[:, h, :, :], tiles(PS[:, 3 + 2 * h, :]), over(g.beta_pair[:, :, h], P), ALU.mult)
                dve.drain()
                nc.vector.tensor_tensor(tiles(ea[:, h, :]), kd[:, h, :, :], kd[:, h, :, :], ALU.mult)
                dve.drain()
                nc.vector.tensor_reduce(st[:, 1, :, h], tiles(ea[:, h, :]), AX.X, ALU.add)
                dve.wait_ge(s.norm_in, h + 1)
                nc.vector.tensor_copy(st[:, 0, :, h], PS[:, 7 - h, 0:T])
            dve.drain()
            nc.vector.tensor_scalar(st[:, 0:2, :, :], st[:, 0:2, :, :], EPS, None, ALU.add)
            dve.drain().then_inc(s.stat_done, 1)
            dve.wait_ge(s.root_done, 1)
            nc.vector.reciprocal(st[:, 4:6, :, :], st[:, 2:4, :, :])
            dve.drain()
            nc.vector.tensor_scalar(st[:, 4, :, :], st[:, 4, :, :], DH ** -0.5, None, ALU.mult)
            nc.vector.tensor_tensor(st[:, 6, :, :], st[:, 5, :, :], g.beta_pair[:, :, :], ALU.mult)
            dve.wait_ge(s.cum_copied, 1)
            nc.vector.tensor_tensor(st[:, 11, :, :], end_decay, cum[:, 1, :, :], ALU.subtract)
            dve.drain().then_inc(s.factors, 1)
            for h in A2:
                nc.vector.tensor_tensor(tiles(diag[:, h, 0, :]), each(g.upto, T), over(cum[:, 0, :, h], P), ALU.mult)
                nc.vector.tensor_tensor(tiles(diag[:, h, 1, :]), each(g.ident, T), over(st[:, 6, :, h], P), ALU.mult)
                dve.drain().then_inc(s.diag_done, 1)
            dve.wait_ge(s.decayed, 1)
            nc.vector.tensor_tensor(st[:, 7, :, :], st[:, 6, :, :], st[:, 10, :, :], ALU.mult)
            nc.vector.tensor_tensor(st[:, 8, :, :], st[:, 4, :, :], st[:, 10, :, :], ALU.mult)
            nc.vector.tensor_tensor(st[:, 9, :, :], st[:, 5, :, :], st[:, 11, :, :], ALU.mult)
            dve.drain()
            nc.vector.tensor_scalar(st[:, 7, :, :], st[:, 7, :, :], -1.0, None, ALU.mult)
            for h in A2:
                nc.vector.tensor_tensor(kd[:, h, :, :], kd[:, h, :, :], over(st[:, 9, :, h], P), ALU.mult)
                dve.wait_ge(s.rows_full, h + 1)
                nc.vector.tensor_tensor(tiles(et[:, h, :]), tiles(PS[:, 2 + 2 * h, :]), over(cum[:, 1, :, h], P), ALU.subtract)
                dve.drain()
                nc.vector.tensor_scalar(et[:, h, :], et[:, h, :], 0.0, None, ALU.min)
                dve.drain().then_inc(s.clipped, 1)
            for h in A2:
                dve.wait_ge(s.decayed, h + 2)
                nc.vector.tensor_tensor(tiles(ea[:, h, :]), tiles(et[:, h, :]), over(st[:, 5, :, h], P), ALU.mult)
                dve.drain()
                nc.vector.tensor_tensor(tiles(ea[:, h, :]), tiles(ea[:, h, :]), each(g.upto, T), ALU.mult)
                dve.drain()
                dve.wait_ge(s.qk_full, h + 1)
                nc.vector.tensor_tensor(qkt[:, h, :], PS[:, QK[h][0], :], ea[:, h, :], ALU.mult)
                nc.vector.tensor_tensor(lt[:, h, :], PS[:, QK[h][1], :], ea[:, h, :], ALU.mult)
                dve.drain()
                nc.vector.tensor_tensor(lt[:, h, :], lt[:, h, :], PS[:, 3 + 2 * h, :], ALU.mult)
                dve.drain()
                nc.vector.tensor_tensor(tiles(mxt[:, h, :]), tiles(lt[:, h, :]), each(g.up[0], T), ALU.mult)
                dve.drain()
                nc.vector.tensor_tensor(tiles(xt[:, h, :]), each(g.ident, T), tiles(mxt[:, h, :]), ALU.subtract)
                dve.drain().then_inc(s.masks_done, 1)
            for h in A2:
                dve.wait_ge(s.first_full, h + 1)
                nc.vector.tensor_tensor(tiles(mx[:, h, :]), tiles(PS[:, 6 + h, :]), each(g.low[0], T), ALU.mult)
                dve.drain()
                nc.vector.tensor_tensor(tiles(x[:, h, :]), each(g.ident, T), tiles(mx[:, h, :]), ALU.subtract).then_inc(s.x_sub, 1)
            for lvl in range(1, LEVELS):
                for h in A2:
                    n = 2 * (lvl - 1) + h
                    dve.wait_ge(s.yx_full, n + 1)
                    nc.vector.tensor_tensor(tiles(mxt[:, h, :]), tiles(PS[:, 4 + h, :]), each(g.up[lvl], T), ALU.mult)
                    if lvl < LEVELS - 1:
                        dve.wait_ge(s.xy_full, n + 1)
                        nc.vector.tensor_tensor(tiles(mx[:, h, :]), tiles(PS[:, 6 + h, :]), each(g.low[lvl], T), ALU.mult)
                        dve.drain()
                        nc.vector.tensor_tensor(x[:, h, :], x[:, h, :], mx[:, h, :], ALU.subtract).then_inc(s.x_sub, 1)
                    else:
                        dve.drain()
                    nc.vector.tensor_tensor(xt[:, h, :], xt[:, h, :], mxt[:, h, :], ALU.subtract).then_inc(s.xt_sub, 1)
            for t in range(T):
                for h in A2:
                    if t == 0:
                        nc.vector.tensor_copy(r[:, h, :], bv[:, h, t, :]).then_inc(s.r_done, 1)
                    else:
                        dve.wait_ge(s.ks_full, 2 * (t - 1) + h + 1)
                        nc.vector.scalar_tensor_tensor(r[:, h, :], PS[:, h, 0:P], st[:, 7, t, h:h + 1], bv[:, h, t, :],
                                                       ALU.mult, ALU.add).then_inc(s.r_done, 1)
                for h in A2:
                    if t < T - 1:
                        dve.wait_ge(s.su_full, 2 * t + h + 1)
                        if t == 0:
                            nc.vector.tensor_copy(state[:, h, :], PS[:, 2 + h, P:2 * P]).then_inc(s.s_done, 1)
                        else:
                            nc.vector.scalar_tensor_tensor(state[:, h, :], state[:, h, :], end_decay[:, t, h:h + 1],
                                                           PS[:, 2 + h, P:2 * P], ALU.mult, ALU.add).then_inc(s.s_done, 1)
                for h in A2:
                    dst = g.YA[:, t, bass.ds((2 * pair + h) * P, P)]
                    dve.wait_ge(s.o_full, 2 * t + h + 1)
                    if t == 0:
                        nc.vector.tensor_scalar(dst, PS[:, 6 + h, P:2 * P], st[:, 4, t, h:h + 1], None,
                                                ALU.mult).then_inc(s.o_done, 1)
                    else:
                        dve.wait_ge(s.qs_full, 2 * (t - 1) + h + 1)
                        nc.vector.tensor_scalar(o1[:, h, :], PS[:, 4 + h, 0:P], st[:, 8, t, h:h + 1], None, ALU.mult)
                        dve.drain()
                        nc.vector.scalar_tensor_tensor(dst, PS[:, 6 + h, P:2 * P], st[:, 4, t, h:h + 1], o1[:, h, :],
                                                       ALU.mult, ALU.add).then_inc(s.o_done, 1)


def out_tensor(nc, pe, g, s, feat, slabs, sems):
    n = 0
    for half in range(2):
        pe.wait_ge(sems[half], 16)
        for t in range(T):
            for k in range(K):
                last = nc.tensor.matmul(g.PS[:, n, :], feat[:, k, t * P:(t + 1) * P], slabs[half][:, k, :],
                                        start=k == 0, stop=k == K - 1)
            last.then_inc(s.out_full, 1)
            n += 1


def out_vector(nc, dve, g, s):
    n = 0
    for half in range(2):
        for t in range(T):
            dve.wait_ge(s.out_full, n + 1)
            part = g.X[:, t, half * 512:(half + 1) * 512]
            nc.vector.tensor_tensor(part, g.PS[:, n, :], part, ALU.add)
            n += 1


def merge(nc, g, a, layer):
    names = """wg1 wg2 wg3 wo0 wo1 row_in squared rooted gate_full gate_on gated mixed turned feat_a feat_v out_full"""
    with memory(nc, "merge") as mem, stage(nc, "merge", names) as (block, s):
        loaded = (s.wg1, s.wg2, s.wg3)
        w = [gate_slab(g), *(mem(f"w{i}", [P, K, 512]) for i in (2, 3))]
        row = mem("row", [P, DH])
        square = mem("square", [P, D])
        stat = mem("stat", [P, 4, T * HEADS])
        part = mem("part", [P, 4, 512])
        GATES = (C_ZB + 512, C_GATE + D, C_GATE + D + 512)

        @block.sync
        def _(sp):
            sp.dma_start(row[:, :], a.gdn_norm_gain[layer].partition_broadcast(P)).then_inc(s.row_in, 16)
            for i, c in enumerate(GATES):
                if i == 0:
                    continue
                sp.dma_start(w[i][:, :, :], a.w_in[layer][:, :, c:c + 512]).then_inc(loaded[i], 16)
            for half, sem in enumerate((s.wo0, s.wo1)):
                sp.wait_ge(s.gate_full, T * (half + 1))
                sp.dma_start(w[half][:, :, :], a.w_out[layer][:, :, half * 512:(half + 1) * 512]).then_inc(sem, 16)

        @block.tensor
        def _(pe):
            pe.sem_inc(s.wg1, 16)
            gate_tensor(nc, pe, g, s, w, loaded)
            for k in range(K):
                for t in range(T):
                    if k == 0:
                        pe.wait_ge(s.mixed, t + 1)
                    last = nc.tensor.transpose(g.PS[:, k, t * P:(t + 1) * P], g.YA[:, t, k * P:(k + 1) * P], g.ident)
                last.then_inc(s.turned, 1)
            pe.wait_ge(s.feat_a, K // 2)
            pe.wait_ge(s.feat_v, K // 2)
            out_tensor(nc, pe, g, s, g.feat, w, (s.wo0, s.wo1))

        @block.scalar
        def _(act):
            act.wait_ge(s.squared, 1)
            nc.scalar.activation(stat[:, 2, :], stat[:, 1, :], ACT.Sqrt).then_inc(s.rooted, 1)
            gate_scalar(nc, act, g, s, part, [ACT.Silu] + [ACT.Sigmoid] * 2)
            for k in range(0, K, 2):
                act.wait_ge(s.turned, k + 1)
                nc.scalar.activation(g.feat[:, k, :], g.PS[:, k, :], ACT.Copy).then_inc(s.feat_a, 1)

        @block.vector
        def _(dve):
            for t in range(T):
                nc.vector.tensor_tensor(square[:, :], g.YA[:, t, :], g.YA[:, t, :], ALU.mult)
                dve.drain()
                nc.vector.tensor_reduce(stat[:, 0, t * HEADS:(t + 1) * HEADS],
                                        square[:, :].rearrange("p (h c) -> p h c", h=HEADS), AX.X, ALU.add)
                dve.drain()
            nc.vector.tensor_scalar(stat[:, 1, :], stat[:, 0, :], 1.0 / DH, EPS, ALU.mult, ALU.add).then_inc(s.squared, 1)
            dve.wait_ge(s.rooted, 1)
            nc.vector.reciprocal(stat[:, 3, :], stat[:, 2, :])
            dve.wait_ge(s.row_in, 16)
            dve.drain()
            for t in range(T):
                y = g.YA[:, t, :].rearrange("p (h c) -> p h c", h=HEADS)
                nc.vector.tensor_tensor(y, y, over(stat[:, 3, t * HEADS:(t + 1) * HEADS], DH), ALU.mult)
                dve.drain()
                nc.vector.tensor_tensor(y, y, each(row[:, :], HEADS), ALU.mult)
            dve.drain()
            for t in range(T):
                y = g.YA[:, t, 0:512]
                nc.vector.tensor_tensor(y, y, gate_kept(g)[:, t, :], ALU.mult)
            gate_vector(nc, dve, s, part, g.YA, [1, 0, 1])
            dve.drain()
            for t in range(T):
                nc.vector.tensor_tensor(g.YA[:, t, :], g.YA[:, t, :], g.YB[:, t, :], ALU.add).then_inc(s.mixed, 1)
            for k in range(1, K, 2):
                dve.wait_ge(s.turned, k + 1)
                nc.vector.tensor_copy(g.feat[:, k, :], g.PS[:, k, :]).then_inc(s.feat_v, 1)
            out_vector(nc, dve, g, s)


def short_conv(nc, g, a, layer):
    names = NORM_SEMS + " gain_in taps_in w0 w1 w2 wo0 wo1 full c_done tile_done out_full"
    with memory(nc, "conv") as mem, stage(nc, "conv", names) as (block, s):
        m = norm_buffers(mem, g)
        gain = mem("gain", [P, K])
        taps = mem("taps", [P, K, 3])
        w = [g.W[i][:, 0:K * 3 * P].rearrange("p (k s c) -> p k s c", k=K, s=3) for i in range(3)]
        w_sems = (s.w0, s.w1, s.w2)
        wo = [slab(g.W[3 + i]) for i in range(2)]
        c = mem("c", [P, 2, S])
        pad = mem("pad", [P, S + 2])
        u = mem("u", [P, S])
        out = g.YA[:, :, :].rearrange("p t d -> p (t d)").rearrange("p (k t) -> p k t", k=K)

        @block.sync
        def _(sp):
            sp.dma_start(gain[:, :], a.norm_mix[layer]).then_inc(s.gain_in, 16)
            sp.dma_start(taps[:, :, :], a.conv_a).then_inc(s.taps_in, 16)
            for f in range(K):
                if f >= 3:
                    sp.wait_ge(s.full, f - 2)
                for k in range(K):
                    sp.dma_start(w[f % 3][:, k, :, :], a.w_in_a[f, k]).then_inc(w_sems[f % 3], 16)
            for half, sem in enumerate((s.wo0, s.wo1)):
                sp.dma_start(wo[half][:, :, :], a.w_out_a[:, :, half * 512:(half + 1) * 512]).then_inc(sem, 16)

        @block.tensor
        def _(pe):
            norm_tensor(nc, pe, g, s, m)
            for f in range(K):
                pe.wait_ge(w_sems[f % 3], 16 * K * (f // 3 + 1))
                if f >= 2:
                    pe.wait_ge(s.tile_done, f - 1)
                for j in range(3):
                    for k in range(K):
                        last = nc.tensor.matmul(g.PS[:, 3 * (f % 2) + j, :], w[f % 3][:, k, j, :], g.feat[:, k, :],
                                                start=k == 0, stop=k == K - 1)
                last.then_inc(s.full, 1)
            pe.wait_ge(s.tile_done, K)
            out_tensor(nc, pe, g, s, out, wo, (s.wo0, s.wo1))

        @block.scalar
        def _(act):
            norm_scalar(nc, act, g, s, m, gain)
            for f in range(K):
                act.wait_ge(s.full, f + 1)
                if f >= 2:
                    act.wait_ge(s.tile_done, f - 1)
                nc.scalar.activation(c[:, f % 2, :], g.PS[:, 3 * (f % 2) + 1, :], ACT.Copy).then_inc(s.c_done, 1)

        @block.vector
        def _(dve):
            norm_vector(nc, dve, g, s, m, gain)
            nc.vector.memset(pad[:, 0:1], 0.0)
            nc.vector.memset(pad[:, S + 1:S + 2], 0.0)
            dve.wait_ge(s.taps_in, 16)
            for f in range(K):
                dve.wait_ge(s.c_done, f + 1)
                nc.vector.tensor_tensor(pad[:, 1:S + 1], c[:, f % 2, :], g.PS[:, 3 * (f % 2) + 2, :], ALU.mult)
                dve.drain()
                nc.vector.tensor_scalar(u[:, :], pad[:, 0:S], taps[:, f, 0:1], None, ALU.mult)
                for tap in (1, 2):
                    dve.drain()
                    nc.vector.scalar_tensor_tensor(u[:, :], pad[:, tap:tap + S], taps[:, f, tap:tap + 1], u[:, :],
                                                   ALU.mult, ALU.add)
                dve.drain()
                nc.vector.tensor_tensor(out[:, f, :], u[:, :], g.PS[:, 3 * (f % 2), :], ALU.mult).then_inc(s.tile_done, 1)
            out_vector(nc, dve, g, s)


LRU_BLOCKS = 4
LRU = D // LRU_BLOCKS
RG_C = 8.0


def rg_lru(nc, g, a, layer):
    names = NORM_SEMS + """ gain_in cols_in wb0 wb1 wg0 wg1 wo0 wo1 neg_abs exp_lam u_full yu_full y_done u_done conv_done
        ri_full r_done i_done a_done th_done root_in root_done scanned tile_done out_full"""
    with memory(nc, "lru") as mem, stage(nc, "lru", names) as (block, s):
        m = norm_buffers(mem, g)
        gain = mem("gain", [P, K])
        cols = mem("cols", [P, 11, K])
        wb = [g.W[i][:, :].rearrange("p (k a c) -> p k a c", k=K, a=2) for i in range(2)]
        wg = [g.W[2 + i][:, 0:8 * LRU].rearrange("p (k a c) -> p k a c", k=2, a=4) for i in range(2)]
        wo = [slab(g.YB[:, :, :].rearrange("p t d -> p (t d)")), slab(g.W[0])]
        rate = mem("rate", [P, 6, 2 * K])
        pad = mem("pad", [P, 2, S + CONV - 1])
        y, u, r, i_ = (slab(g.W[4])[:, n:n + 2, :] for n in range(0, 8, 2))
        aa, th = (slab(g.W[5])[:, n:n + 2, :] for n in (0, 2))
        h = g.W[5][:, 4 * S:].rearrange("p (d e c) -> p d e c", d=2, e=2)
        out = g.YA[:, :, :].rearrange("p t d -> p (t d)").rearrange("p (k t) -> p k t", k=K)
        NB = LRU_BLOCKS

        @block.sync
        def _(sp):
            sp.dma_start(gain[:, :], a.norm_mix[layer]).then_inc(s.gain_in, 16)
            sp.dma_start(cols[:, :, :], a.lru_cols).then_inc(s.cols_in, 16)
            for n in range(NB):
                if n >= 2:
                    sp.wait_ge(s.ri_full, 4 * (n - 1))
                if n == 2:
                    sp.dma_start(wo[0], a.w_out_b[:, :, 0:512]).then_inc(s.wo0, 16)
                for j in range(2):
                    sp.dma_start(wb[n % 2][:, :, j, :], a.w_in_b[:, :, j, n * LRU:(n + 1) * LRU]).then_inc((s.wb0, s.wb1)[n % 2], 16)
                for d in range(2):
                    for j, gate in enumerate((a.w_rgate, a.w_igate)):
                        sp.dma_start(wg[n % 2][:, :, 2 * d + j, :], gate[d, n]).then_inc((s.wg0, s.wg1)[n % 2], 16)
            sp.wait_ge(s.yu_full, NB - 1)
            sp.dma_start(wo[1], a.w_out_b[:, :, 512:1024]).then_inc(s.wo1, 16)

        @block.tensor
        def _(pe):
            norm_tensor(nc, pe, g, s, m)
            for n in range(NB):
                pe.wait_ge((s.wb0, s.wb1)[n % 2], 32 * (n // 2 + 1))
                if n >= 1:
                    pe.wait_ge(s.y_done, n)
                    pe.wait_ge(s.u_done, n)
                for j in (2, 3, 0, 1):
                    for k in range(K):
                        last = nc.tensor.matmul(g.PS[:, j, :], wb[n % 2][:, k, j // 2, (j % 2) * P:(j % 2 + 1) * P],
                                                g.feat[:, k, :], start=k == 0, stop=k == K - 1)
                    if j == 3:
                        last.then_inc(s.u_full, 1)
                last.then_inc(s.yu_full, 1)
                pe.wait_ge((s.wg0, s.wg1)[n % 2], 64 * (n // 2 + 1))
                pe.wait_ge(s.conv_done, n + 1)
                for d in range(2):
                    for j in range(2):
                        if 2 * n + d >= 1:
                            pe.wait_ge((s.r_done, s.i_done)[j], 2 * (2 * n + d))
                        for e in range(2):
                            for kk in range(2):
                                last = nc.tensor.matmul(g.PS[:, 4 + 2 * j + e, :],
                                                        wg[n % 2][:, kk, 2 * d + j, e * P:(e + 1) * P], u[:, kk, :],
                                                        start=kk == 0, stop=kk == 1)
                        last.then_inc(s.ri_full, 1)
            pe.wait_ge(s.wo0, 16)
            pe.wait_ge(s.y_done, NB)
            pe.wait_ge(s.tile_done, NB - 1)
            for t in range(T):
                for k in range(K - 2):
                    nc.tensor.matmul(g.PS[:, t, :], out[:, k, t * P:(t + 1) * P], wo[0][:, k, :], start=k == 0, stop=False)
            pe.wait_ge(s.tile_done, NB)
            for t in range(T):
                for k in range(K - 2, K):
                    last = nc.tensor.matmul(g.PS[:, t, :], out[:, k, t * P:(t + 1) * P], wo[0][:, k, :], start=False,
                                            stop=k == K - 1)
                last.then_inc(s.out_full, 1)
            pe.wait_ge(s.wo1, 16)
            for t in range(T):
                for k in range(K):
                    last = nc.tensor.matmul(g.PS[:, T + t, :], out[:, k, t * P:(t + 1) * P], wo[1][:, k, :],
                                            start=k == 0, stop=k == K - 1)
                last.then_inc(s.out_full, 1)

        @block.scalar
        def _(act):
            norm_scalar(nc, act, g, s, m, gain)
            act.wait_ge(s.neg_abs, 1)
            nc.scalar.activation(rate[:, 1, :], rate[:, 0, :], ACT.Exp, scale=-1.0).then_inc(s.exp_lam, 1)
            for n in range(NB):
                act.wait_ge(s.u_full, n + 1)
                if n >= 1:
                    act.wait_ge(s.conv_done, n)
                nc.scalar.activation(pad[:, :, 2:S + 2], g.PS[:, 2:4, :], ACT.Copy).then_inc(s.u_done, 1)
                act.wait_ge(s.yu_full, n + 1)
                if n >= 1:
                    act.wait_ge(s.tile_done, n)
                nc.scalar.activation(y[:, :, :], g.PS[:, 0:2, :], ACT.Gelu_apprx_tanh).then_inc(s.y_done, 1)
                for d in range(2):
                    step = 2 * n + d
                    if step >= 1:
                        act.wait_ge(s.scanned, step)
                    act.wait_ge(s.ri_full, 2 * step + 1)
                    for e in range(2):
                        f = 2 * n + e
                        nc.scalar.activation(r[:, e, :], g.PS[:, 4 + e, :], ACT.Sigmoid,
                                             bias=cols[:, 5 + d, f:f + 1]).then_inc(s.r_done, 1)
                    act.wait_ge(s.ri_full, 2 * step + 2)
                    for e in range(2):
                        f = 2 * n + e
                        nc.scalar.activation(i_[:, e, :], g.PS[:, 6 + e, :], ACT.Sigmoid,
                                             bias=cols[:, 7 + d, f:f + 1]).then_inc(s.i_done, 1)
                    act.drain()
                    if step == 0:
                        act.wait_ge(s.conv_done, 1)
                    for e in range(2):
                        f = 8 * d + 2 * n + e
                        nc.scalar.activation(aa[:, e, :], r[:, e, :], ACT.Exp, scale=rate[:, 4, f:f + 1]).then_inc(s.a_done, 1)
                    for e in range(2):
                        f = 8 * d + 2 * n + e
                        nc.scalar.activation(th[:, e, :], r[:, e, :], ACT.Tanh, scale=rate[:, 5, f:f + 1]).then_inc(s.th_done, 1)
                    act.wait_ge(s.root_in, step + 1)
                    nc.scalar.activation(th[:, :, :], th[:, :, :], ACT.Sqrt).then_inc(s.root_done, 1)

        @block.vector
        def _(dve):
            norm_vector(nc, dve, g, s, m, gain)
            nc.vector.memset(pad[:, :, 0:2], 0.0)
            nc.vector.memset(pad[:, :, S + 2:], 0.0)
            dve.wait_ge(s.cols_in, 16)
            lam = cols[:, 9:11, :].rearrange("p d k -> p (d k)")
            nc.vector.scalar_tensor_tensor(rate[:, 0, :], lam, -1.0, lam, ALU.mult, ALU.max)
            dve.drain().then_inc(s.neg_abs, 1)
            dve.wait_ge(s.exp_lam, 1)
            log1p_vector(nc, dve, rate[:, 1, :], rate[:, 2, :], rate[:, 3, :], rate[:, 5, :])
            nc.vector.tensor_scalar(rate[:, 2, :], lam, -1.0, 0.0, ALU.mult, ALU.max)
            dve.drain()
            nc.vector.tensor_tensor(rate[:, 1, :], rate[:, 1, :], rate[:, 2, :], ALU.add)
            dve.drain()
            nc.vector.tensor_scalar(rate[:, 4, :], rate[:, 1, :], -RG_C, None, ALU.mult)
            nc.vector.tensor_scalar(rate[:, 5, :], rate[:, 1, :], RG_C, None, ALU.mult)
            for n in range(NB):
                dve.wait_ge(s.u_done, n + 1)
                for e in range(2):
                    f = 2 * n + e
                    nc.vector.tensor_scalar(u[:, e, :], pad[:, e, 0:S], cols[:, 0, f:f + 1], cols[:, 4, f:f + 1],
                                            ALU.mult, ALU.add)
                    for tap in range(1, CONV):
                        dve.drain()
                        nc.vector.scalar_tensor_tensor(u[:, e, :], pad[:, e, tap:tap + S], cols[:, tap, f:f + 1],
                                                       u[:, e, :], ALU.mult, ALU.add)
                dve.drain().then_inc(s.conv_done, 1)
                for d in range(2):
                    step = 2 * n + d
                    dve.wait_ge(s.i_done, 2 * step + 2)
                    nc.vector.tensor_tensor(i_[:, :, :], i_[:, :, :], u[:, :, :], ALU.mult)
                    dve.wait_ge(s.a_done, 2 * step + 2)
                    dve.wait_ge(s.th_done, 2 * step + 2)
                    nc.vector.tensor_tensor(r[:, :, :], aa[:, :, :], aa[:, :, :], ALU.mult)
                    dve.drain()
                    nc.vector.scalar_tensor_tensor(th[:, :, :], r[:, :, :], 1.0, th[:, :, :], ALU.add, ALU.mult)
                    dve.drain().then_inc(s.root_in, 1)
                    dve.wait_ge(s.root_done, step + 1)
                    nc.vector.tensor_tensor(i_[:, :, :], i_[:, :, :], th[:, :, :], ALU.mult)
                    dve.drain()
                    for e in range(2):
                        way = slice(None, None, -1) if d else slice(None)
                        nc.vector.tensor_tensor_scan(h[:, d, e, way], aa[:, e, way], i_[:, e, way], 0.0, ALU.mult, ALU.add)
                    dve.drain().then_inc(s.scanned, 1)
                nc.vector.tensor_tensor(h[:, 0, :, :], h[:, 0, :, :], h[:, 1, :, :], ALU.add)
                dve.wait_ge(s.y_done, n + 1)
                dve.drain()
                nc.vector.tensor_tensor(out[:, 2 * n:2 * n + 2, :], h[:, 0, :, :], y[:, :, :],
                                        ALU.mult).then_inc(s.tile_done, 1)
            out_vector(nc, dve, g, s)


GROUPS, PER_GROUP = 4, 8
EXPERTS = GROUPS * PER_GROUP
F = 512
CAP = 64
PAIRS = EXPERTS // 2
EXTRA = 8
SLOTS = (PAIRS + EXTRA) * P
BIG = 1e30


def route(nc, g, a, layer):
    names = NORM_SEMS + """ gain_in gainrow_in router_in bias_in sent logits_full logits_done shifted exp_g shifted2 exp_e picked ranked spread row_full
        first_pair second_gate stored"""
    with memory(nc, f"route{layer}") as mem, stage(nc, f"route{layer}", names) as (block, s):
        m = norm_buffers(mem, g)
        gain = mem("gain", [P, K])
        gain_row = mem("gain_row", [P, D])
        NR = GROUPS + EXPERTS
        w = mem("w", [P, K, NR])
        brow = mem("brow", [P, NR])
        lg = mem("lg", [P, T, NR])
        sm = mem("sm", [P, 12, T])
        gm = mem("gm", [P, 3, T, GROUPS])
        le = mem("le", [P, T, EXPERTS])
        q = mem("q", [P, T, EXPERTS])
        one = mem("one", [P, 2, T, EXPERTS])
        both = mem("both", [P, T, EXPERTS])
        ex = mem("ex", [P, 6, EXPERTS])
        cmp = mem("cmp", [P, 2 * EXTRA, EXPERTS])
        ovx = mem("ovx", [P, 2 * EXTRA + 1])
        slot = mem("slot", [P, 4, T])
        diag = mem("diag", [P, 4, S])

        @block.sync
        def _(sp):
            sp.dma_start(gain[:, :], a.norm_ffn[layer]).then_inc(s.gain_in, 16)
            sp.dma_start(gain_row[:, :], a.norm_ffn_row[layer].partition_broadcast(P)).then_inc(s.gainrow_in, 16)
            sp.dma_start(w[:, :, 0:GROUPS], a.w_router_group[layer]).then_inc(s.router_in, 16)
            sp.dma_start(w[:, :, GROUPS:], a.w_router_expert[layer]).then_inc(s.router_in, 16)
            sp.dma_start(brow[:, 0:GROUPS], a.b_router_group[layer].partition_broadcast(P)).then_inc(s.bias_in, 16)
            sp.dma_start(brow[:, GROUPS:], a.b_router_expert[layer].partition_broadcast(P)).then_inc(s.bias_in, 16)
            for u in range(2):
                for dst, src in expert_loads(a, g.W, layer, u, u):
                    sp.dma_start(dst, src).then_inc(s.first_pair, 16)
            for t in range(T):
                sp.wait_ge(s.sent, t + 1)
                sp.dma_start(g.rows_dram[t * P:(t + 1) * P, :], g.YB[:, t, :]).then_inc(s.stored, 16)
            sp.wait_ge(s.logits_full, T)
            for u in range(2):
                sp.dma_start(slab(g.W_odd[u]), a.w_exp_gate[layer, 2 + u]).then_inc(s.second_gate, 16)
            sp.wait_ge(s.stored, 16 * T)
            sp.wait_ge(s.first_pair, 16 * 6)
            sp.wait_ge(s.second_gate, 16 * 2)

        @block.tensor
        def _(pe):
            norm_tensor(nc, pe, g, s, m)
            pe.wait_ge(s.router_in, 32)
            for t in range(T):
                to_rows(nc, g, g.PS[:, t, 0:NR], w, t, 0, NR).then_inc(s.logits_full, 1)
            pe.wait_ge(s.picked, 1)
            for t in range(T + 1):
                terms = [(g.ones, e) for e in range(t)] + ([(g.before, t)] if t < T else [])
                for n, (left, e) in enumerate(terms):
                    last = nc.tensor.matmul(g.PS[:, 4, t * EXPERTS:(t + 1) * EXPERTS], left, both[:, e, :],
                                            start=n == 0, stop=n == len(terms) - 1)
            last.then_inc(s.ranked, 1)
            for n in range(4):
                pe.wait_ge(s.spread, n + 1)
                nc.tensor.matmul(g.PS[:, n, :], g.ones, diag[:, n, :], start=True, stop=True).then_inc(s.row_full, 1)

        @block.scalar
        def _(act):
            norm_scalar(nc, act, g, s, m, gain)
            for t in range(T):
                act.wait_ge(s.logits_full, t + 1)
                nc.scalar.activation(lg[:, t, :], g.PS[:, t, 0:NR], ACT.Copy).then_inc(s.logits_done, 1)
            act.wait_ge(s.shifted, 1)
            nc.scalar.activation(gm[:, 0, :, :], gm[:, 0, :, :], ACT.Exp).then_inc(s.exp_g, 1)
            act.wait_ge(s.shifted2, 1)
            nc.scalar.activation(sm[:, 6, :], sm[:, 6, :], ACT.Exp).then_inc(s.exp_e, 1)
            for n in range(4):
                act.wait_ge(s.row_full, n + 1)
                dst = (g.slot_row, g.weight_row)[n // 2][:, n % 2, :]
                nc.scalar.activation(dst, g.PS[:, n, :], ACT.Copy)

        @block.vector
        def _(dve):
            def first_of(dst, val, top, width, tmp):
                nc.vector.tensor_tensor(dst, val, over(top, width), ALU.is_equal)
                dve.drain()
                nc.vector.tensor_tensor(dst, dst, each(g.fall[:, 0:width], T), ALU.mult)
                dve.drain()
                nc.vector.tensor_reduce(tmp, dst, AX.X, ALU.max)
                dve.drain()
                nc.vector.tensor_tensor(dst, dst, over(tmp, width), ALU.is_equal)
                dve.drain()

            norm_vector(nc, dve, g, s, m, gain)
            dve.wait_ge(s.gainrow_in, 16)
            for t in range(T):
                nc.vector.scalar_tensor_tensor(g.YB[:, t, :], g.X[:, t, :], m.stat[:, 3 * T + t:3 * T + t + 1],
                                               gain_row[:, :], ALU.mult, ALU.mult).then_inc(s.sent, 1)
            dve.wait_ge(s.logits_done, T)
            dve.wait_ge(s.bias_in, 32)
            nc.vector.tensor_tensor(lg[:, :, :], lg[:, :, :], each(brow[:, :], T), ALU.add)
            dve.drain()
            lgg = lg[:, :, 0:GROUPS]
            nc.vector.tensor_reduce(sm[:, 0, :], lgg, AX.X, ALU.max)
            dve.drain()
            nc.vector.tensor_tensor(gm[:, 0, :, :], lgg, over(sm[:, 0, :], GROUPS), ALU.subtract)
            dve.drain().then_inc(s.shifted, 1)
            og = gm[:, 1, :, :]
            first_of(og, lgg, sm[:, 0, :], GROUPS, sm[:, 1, :])
            nc.vector.tensor_scalar(gm[:, 2, :, :], og, 1.0, BIG, ALU.subtract, ALU.mult)
            for t in range(T):
                nc.vector.tensor_tensor(le[:, t, :].rearrange("p (g e) -> p g e", g=GROUPS),
                                        lg[:, t, GROUPS:].rearrange("p (g e) -> p g e", g=GROUPS),
                                        over(gm[:, 1, t, :], PER_GROUP), ALU.mult)
            dve.drain()
            for t in range(T):
                v = le[:, t, :].rearrange("p (g e) -> p g e", g=GROUPS)
                nc.vector.tensor_tensor(v, v, over(gm[:, 2, t, :], PER_GROUP), ALU.add)
            dve.drain()
            nc.vector.tensor_reduce(sm[:, 2, :], le[:, :, :], AX.X, ALU.max)
            dve.drain()
            first_of(one[:, 0, :, :], le[:, :, :], sm[:, 2, :], EXPERTS, sm[:, 1, :])
            nc.vector.scalar_tensor_tensor(le[:, :, :], one[:, 0, :, :], -1e36, le[:, :, :], ALU.mult, ALU.add)
            dve.drain()
            nc.vector.tensor_reduce(sm[:, 3, :], le[:, :, :], AX.X, ALU.max)
            dve.drain()
            first_of(one[:, 1, :, :], le[:, :, :], sm[:, 3, :], EXPERTS, sm[:, 1, :])
            nc.vector.tensor_tensor(both[:, :, :], one[:, 0, :, :], one[:, 1, :, :], ALU.add)
            dve.drain().then_inc(s.picked, 1)
            nc.vector.tensor_tensor(sm[:, 6, :], sm[:, 3, :], sm[:, 2, :], ALU.subtract)
            dve.drain().then_inc(s.shifted2, 1)
            dve.wait_ge(s.exp_g, 1)
            nc.vector.tensor_reduce(sm[:, 4, :], gm[:, 0, :, :], AX.X, ALU.add)
            dve.wait_ge(s.exp_e, 1)
            nc.vector.tensor_scalar(sm[:, 5, :], sm[:, 6, :], 1.0, None, ALU.add)
            dve.drain()
            nc.vector.tensor_tensor(sm[:, 5, :], sm[:, 5, :], sm[:, 4, :], ALU.mult)
            dve.drain()
            nc.vector.reciprocal(slot[:, 2, :], sm[:, 5, :])
            dve.drain()
            nc.vector.tensor_tensor(slot[:, 3, :], slot[:, 2, :], sm[:, 6, :], ALU.mult)
            dve.wait_ge(s.ranked, 1)
            count = g.PS[:, 4, T * EXPERTS:(T + 1) * EXPERTS]
            nc.vector.tensor_copy(ex[:, 0, :], count)
            dve.drain()
            nc.vector.tensor_scalar(ex[:, 1, :], ex[:, 0, :], float(CAP), None, ALU.is_gt)
            for b in range(2, S // CAP):
                dve.drain()
                nc.vector.scalar_tensor_tensor(ex[:, 1, :], ex[:, 0, :], float(b * CAP), ex[:, 1, :], ALU.is_gt, ALU.add)
            dve.drain()
            nc.vector.tensor_tensor_scan(ex[:, 2, :], g.ones[:, 0:EXPERTS], ex[:, 1, :], 0.0, ALU.mult, ALU.add)
            dve.drain()
            nc.vector.tensor_tensor(ex[:, 3, :], ex[:, 2, :], ex[:, 1, :], ALU.subtract)
            dve.drain()
            nc.vector.tensor_scalar(ex[:, 3, :], ex[:, 3, :], float(CAP), float(EXPERTS * CAP - CAP), ALU.mult, ALU.add)
            nc.vector.tensor_scalar(ex[:, 4, :], g.rise[:, 0:EXPERTS], float(CAP), None, ALU.mult)
            nc.vector.tensor_tensor(cmp[:, :, :], each(ex[:, 2, :], 2 * EXTRA), over(g.rise[:, 0:2 * EXTRA], EXPERTS),
                                    ALU.is_le)
            dve.drain()
            nc.vector.tensor_reduce(ovx[:, 0:2 * EXTRA], cmp[:, :, :], AX.X, ALU.add)
            nc.vector.tensor_scalar(ovx[:, 2 * EXTRA:], ex[:, 2, EXPERTS - 1:], 0.5, 0.25, ALU.mult, ALU.add)
            dve.drain()
            nc.vector.tensor_scalar(ovx[:, 0:2 * EXTRA], ovx[:, 0:2 * EXTRA], float(EXPERTS - 1), None, ALU.min)
            dve.drain()
            nc.vector.tensor_copy(g.extra[:, :], ovx[:, :])
            for j in range(2):
                for c, row in enumerate((g.PS[:, 4, 0:T * EXPERTS].rearrange("p (t e) -> p t e", t=T),
                                         each(ex[:, 4, :], T), each(ex[:, 3, :], T))):
                    nc.vector.tensor_tensor(q[:, :, :], one[:, j, :, :], row, ALU.mult)
                    dve.drain()
                    nc.vector.tensor_reduce(sm[:, 7 + c, :], q[:, :, :], AX.X, ALU.add)
                    dve.drain()
                nc.vector.tensor_tensor(sm[:, 9, :], sm[:, 9, :], sm[:, 8, :], ALU.subtract)
                nc.vector.tensor_tensor(sm[:, 8, :], sm[:, 8, :], sm[:, 7, :], ALU.add)
                dve.drain()
                nc.vector.scalar_tensor_tensor(sm[:, 9, :], sm[:, 7, :], float(CAP), sm[:, 9, :], ALU.is_ge, ALU.mult)
                dve.drain()
                nc.vector.tensor_tensor(slot[:, j, :], sm[:, 9, :], sm[:, 8, :], ALU.add)
                dve.drain()
            for n in range(4):
                nc.vector.tensor_tensor(diag[:, n, :].rearrange("p (t c) -> p t c", t=T), each(g.ident, T),
                                        over(slot[:, n, :], P), ALU.mult).then_inc(s.spread, 1)


def expert_loads(a, w, layer, e, u):
    return [(slab(w[u]), a.w_exp_gate[layer, e]),
            (slab(w[2 + u]), a.w_exp_up[layer, e]),
            (slab(w[4 + u], D), a.w_exp_down[layer, e])]


def experts(nc, g, a, layer, extra):
    names = """g0 g1 g2 g3 u0 u1 d0 d1 g_free u_free d_free index_done rows_free turned
        xt_a xt_v gate_full up_full silu_done hidden_done hidden_turned ht_done y_full y_a y_v
        weights_done sum_full summed"""
    tag = ("extra" if extra else "experts") + str(layer)
    with memory(nc, tag) as mem, stage(nc, tag, names, rows0=g.pool_sems[0], rows1=g.pool_sems[1]) as (block, s):
        w = g.W
        BODY = 1 if extra else 2
        W = [w, [*g.W_odd, *w[2:]]]
        full = [((s.g0, s.g1), (s.u0, s.u1), (s.d0, s.d1)), ((s.g2, s.g3), (s.u0, s.u1), (s.d0, s.d1))]
        free = (s.g_free, s.u_free, s.d_free)
        number = mem("number", [P, 1])
        later = mem("later", [P, 1])
        rows_in = (s.rows0, s.rows1)
        found = mem("found", [P, 2])
        index = mem("index", [P, PAIRS + 2], I32)
        taken = mem("taken", [P, 2], I32)
        match = mem("match", [P, 2, S])
        rows = [g.YB[:, b, :] for b in range(2)]
        xt = mem("xt", [P, K, P])
        silu = mem("silu", [P, F])
        hid = mem("hid", [P, F])
        ht = mem("ht", [P, F // P, P])
        y = mem("y", [P, D])
        sums = [(t, half) for t in range(T) for half in range(2)]
        SUM_BANKS = (0, 1, 7)

        @contextmanager
        def bodies(eng):
            if not extra:
                with eng.Fori(0, PAIRS // BODY) as i:
                    yield i
            else:
                n = eng.value_load(g.extra[0:1, 2 * EXTRA:2 * EXTRA + 1], min_val=0, max_val=EXTRA)
                with eng.If(n > 0):
                    with eng.Fori(0, n) as i:
                        yield i

        @block.sync
        def _(sp):
            if not extra:
                for part in range(3):
                    for u in range(2):
                        sp.sem_inc(full[0][part][u], 16)
                for u in range(2):
                    sp.sem_inc(full[1][0][u], 16)

                def load(j, odd, parts):
                    for part in parts:
                        sp.wait_ge(free[part], j if part > 0 else j - 1)
                        for u in range(2):
                            dst, src = expert_loads(a, W[odd], layer, 2 * j + u, u)[part]
                            sp.dma_start(dst, src).then_inc(full[odd][part][u], 16)

                load(1, 1, (1, 2))
                with sp.Fori(1, PAIRS // BODY) as i:
                    for odd in range(2):
                        load(2 * i + odd, odd, (0, 1, 2))
            else:
                with bodies(sp) as j:
                    e = [sp.value_load(g.extra[0:1, bass.ds(2 * j + u, 1)], min_val=0, max_val=EXPERTS - 1)
                         for u in range(2)]
                    for part in range(3):
                        sp.wait_ge(free[part], j + 1)
                        for u in range(2):
                            dst, src = expert_loads(a, w, layer, e[u], u)[part]
                            sp.dma_start(dst, src).then_inc(full[0][part][u], 16)

        @block.gpsimd
        def _(pool):
            with bodies(pool) as i:
                for odd in range(BODY):
                    j = BODY * i + odd
                    pool.wait_ge(s.rows_free, j + 1)
                    pool.wait_ge(s.index_done, j + 1)
                    nc.gpsimd.tensor_copy(taken[:, odd:odd + 1], index[:, bass.ds(j, 1)])
                    pool.drain()
                    pool.indirect_dma_start(rows[odd], None, g.rows_dram,
                                            bass.IndirectOffsetOnAxis(taken[:, odd:odd + 1].bitcast(U32), 0)).then_inc(rows_in[odd], 16)

        @block.tensor
        def _(pe):
            if extra:
                for sem in free:
                    pe.sem_inc(sem, 1)
            pe.sem_inc(s.rows_free, BODY)
            with bodies(pe) as i:
                for odd in range(BODY):
                    j = BODY * i + odd
                    pe.wait_ge(rows_in[odd], 16 * i + 16)
                    pe.wait_ge(s.summed, 8 * j + 1)
                    for k in range(K):
                        last = nc.tensor.transpose(g.PS[:, k // 4, (k % 4) * P:(k % 4 + 1) * P], rows[odd][:, k * P:(k + 1) * P],
                                                   g.ident)
                        if k % 4 == 3:
                            last.then_inc(s.turned, 1)
                    pe.wait_ge(s.xt_a, j + 1)
                    pe.wait_ge(s.xt_v, j + 1)
                    for part, bank, done in ((0, 2, s.gate_full), (1, 3, s.up_full)):
                        for u in range(2):
                            pe.wait_ge(full[odd][part][u], 16 * (i if part == 0 else j) + 16)
                        for k in range(K):
                            for u in range(2):
                                last = nc.tensor.matmul(g.PS[u * CAP:(u + 1) * CAP, bank, :],
                                                        xt[:, k, u * CAP:(u + 1) * CAP], slab(W[odd][2 * part + u])[:, k, :],
                                                        start=k == 0, stop=k == K - 1)
                        last.then_inc(done, 1)
                        pe.drain().then_inc(free[part], 1)
                    pe.wait_ge(s.hidden_done, j + 1)
                    for f in range(F // P):
                        last = nc.tensor.transpose(g.PS[:, 4, f * P:(f + 1) * P], hid[:, f * P:(f + 1) * P], g.ident)
                    last.then_inc(s.hidden_turned, 1)
                    pe.wait_ge(s.ht_done, j + 1)
                    for u in range(2):
                        pe.wait_ge(full[odd][2][u], 16 * j + 16)
                    for half in range(2):
                        for f in range(F // P):
                            for u in range(2):
                                last = nc.tensor.matmul(g.PS[u * CAP:(u + 1) * CAP, 5 + half, :],
                                                        ht[:, f, u * CAP:(u + 1) * CAP],
                                                        slab(w[4 + u], D)[:, f, half * 512:(half + 1) * 512],
                                                        start=f == 0, stop=f == F // P - 1)
                        last.then_inc(s.y_full, 1)
                    pe.drain().then_inc(free[2], 1)
                    pe.wait_ge(s.weights_done, j + 1)
                    pe.wait_ge(s.y_a, j + 1)
                    pe.wait_ge(s.y_v, j + 1)
                    for n, (t, half) in enumerate(sums):
                        if n >= 3:
                            pe.wait_ge(s.summed, 8 * j + n - 1)
                        nc.tensor.matmul(g.PS[:, SUM_BANKS[n % 3], :], match[:, 0, t * P:(t + 1) * P],
                                         y[:, half * 512:(half + 1) * 512], start=True, stop=True).then_inc(s.sum_full, 1)

        @block.scalar
        def _(act):
            with bodies(act) as i:
                for odd in range(BODY):
                    j = BODY * i + odd
                    act.wait_ge(s.turned, 2 * j + 1)
                    nc.scalar.activation(xt[:, 0:4, :].rearrange("p k c -> p (k c)"), g.PS[:, 0, :], ACT.Copy).then_inc(s.xt_a, 1)
                    act.wait_ge(s.gate_full, j + 1)
                    nc.scalar.activation(silu[:, :], g.PS[:, 2, :], ACT.Silu).then_inc(s.silu_done, 1)
                    act.wait_ge(s.hidden_turned, j + 1)
                    nc.scalar.activation(ht[:, :, :].rearrange("p i c -> p (i c)"), g.PS[:, 4, :], ACT.Copy).then_inc(s.ht_done, 1)
                    act.wait_ge(s.y_full, 2 * j + 1)
                    nc.scalar.activation(y[:, 0:512], g.PS[:, 5, :], ACT.Copy).then_inc(s.y_a, 1)

        @block.vector
        def _(dve):
            def find_index(column):
                for c in range(2):
                    nc.vector.scalar_tensor_tensor(match[:, 1, :], g.slot_row[:, c, :], later[:, :], g.token_row,
                                                   ALU.is_equal, ALU.mult, accum_out=found[:, c:c + 1])
                    dve.drain()
                nc.vector.tensor_tensor(column, found[:, 0:1], found[:, 1:2], ALU.add).then_inc(s.index_done, 1)

            dve.sem_inc(s.summed, 1)
            nc.vector.tensor_scalar(number[:, :], g.fall[:, 0:1], 0.0, float(PAIRS * P if extra else 0), ALU.mult, ALU.add)
            dve.drain()
            nc.vector.tensor_tensor(number[:, :], number[:, :], g.lane, ALU.add)
            dve.drain()
            for b in range(BODY):
                nc.vector.tensor_scalar(later[:, :], number[:, :], float(b * P), None, ALU.add)
                dve.drain()
                find_index(index[:, b:b + 1])
            with bodies(dve) as i:
                for odd in range(BODY):
                    j = BODY * i + odd
                    dve.wait_ge(s.turned, 2 * j + 2)
                    nc.vector.tensor_copy(xt[:, 4:8, :].rearrange("p k c -> p (k c)"), g.PS[:, 1, :]).then_inc(s.xt_v, 1)
                    dve.sem_inc(s.rows_free, 1)
                    for c in range(2):
                        nc.vector.scalar_tensor_tensor(match[:, c, :], g.slot_row[:, c, :], number[:, :],
                                                       g.weight_row[:, c, :], ALU.is_equal, ALU.mult)
                    dve.drain()
                    nc.vector.tensor_tensor(match[:, 0, :], match[:, 0, :], match[:, 1, :], ALU.add).then_inc(s.weights_done, 1)
                    nc.vector.tensor_scalar(later[:, :], number[:, :], float(BODY * P), None, ALU.add)
                    nc.vector.tensor_scalar(number[:, :], number[:, :], float(P), None, ALU.add)
                    dve.drain()
                    find_index(index[:, bass.ds(j + BODY, 1)])
                    dve.wait_ge(s.up_full, j + 1)
                    dve.wait_ge(s.silu_done, j + 1)
                    nc.vector.tensor_tensor(hid[:, :], silu[:, :], g.PS[:, 3, :], ALU.mult).then_inc(s.hidden_done, 1)
                    dve.wait_ge(s.y_full, 2 * j + 2)
                    nc.vector.tensor_copy(y[:, 512:], g.PS[:, 6, :]).then_inc(s.y_v, 1)
                    for n, (t, half) in enumerate(sums):
                        dve.wait_ge(s.sum_full, 8 * j + n + 1)
                        x = g.X[:, t, half * 512:(half + 1) * 512]
                        nc.vector.tensor_tensor(x, x, g.PS[:, SUM_BANKS[n % 3], :], ALU.add).then_inc(s.summed, 1)
                    dve.drain()


def per_layer(nc, g, a, layer):
    names = NORM_SEMS + """ gain_in brow_in p_in wp_in w0 w1 p_turned pt_done gate_full
        added gate_on ple_full gated"""
    with memory(nc, f"ple{layer}") as mem, stage(nc, f"ple{layer}", names) as (block, s):
        m = norm_buffers(mem, g)
        gain = mem("gain", [P, K])
        brow = mem("brow", [P, D])
        w = [slab(g.W[i]) for i in range(2)]
        wp = g.W[2][:, 0:2 * D].rearrange("p (k c) -> p k c", k=2)
        p_rows = mem("p_rows", [P, T, 2 * P])
        pt = mem("pt", [P, 2, S])
        part = mem("part", [P, 2, 512])
        STEPS = [(half, t) for half in range(2) for t in range(T)]

        @block.sync
        def _(sp):
            sp.dma_start(gain[:, :], a.norm_ple[layer]).then_inc(s.gain_in, 16)
            sp.dma_start(brow[:, :], a.b_ple_gate[layer].partition_broadcast(P)).then_inc(s.brow_in, 16)
            sp.dma_start(p_rows[:, :, :], a.p[layer, 0].rearrange("(t p) c -> p t c", p=P)).then_inc(s.p_in, 16)
            sp.dma_start(wp[:, :, :], a.w_ple[layer]).then_inc(s.wp_in, 16)
            for half, sem in enumerate((s.w0, s.w1)):
                sp.dma_start(w[half][:, :, :], a.w_ple_gate[layer][:, :, half * 512:(half + 1) * 512]).then_inc(sem, 16)

        @block.tensor
        def _(pe):
            pe.wait_ge(s.p_in, 16)
            for c in range(2):
                for t in range(T):
                    last = nc.tensor.transpose(g.PS[:, c, t * P:(t + 1) * P], p_rows[:, t, c * P:(c + 1) * P], g.ident)
            last.then_inc(s.p_turned, 1)
            pe.wait_ge(s.pt_done, 1)
            norm_tensor(nc, pe, g, s, m)
            pe.wait_ge(s.wp_in, 16)
            for n, (half, t) in enumerate(STEPS):
                if n % T == 0:
                    pe.wait_ge((s.w0, s.w1)[half], 16)
                if n >= 4:
                    pe.wait_ge(s.added, n - 3)
                    pe.wait_ge(s.gated, n - 3)
                to_rows(nc, g, g.PS[:, n % 4, :], w[half], t, 0, 512).then_inc(s.gate_full, 1)
                for c in range(2):
                    last = nc.tensor.matmul(g.PS[:, 4 + n % 4, :], pt[:, c, t * P:(t + 1) * P],
                                            wp[:, c, half * 512:(half + 1) * 512], start=c == 0, stop=c == 1)
                last.then_inc(s.ple_full, 1)

        @block.scalar
        def _(act):
            act.wait_ge(s.p_turned, 1)
            nc.scalar.activation(pt[:, :, :], g.PS[:, 0:2, :], ACT.Copy).then_inc(s.pt_done, 1)
            norm_scalar(nc, act, g, s, m, gain)
            for n in range(len(STEPS)):
                act.wait_ge(s.added, n + 1)
                nc.scalar.activation(part[:, n % 2, :], part[:, n % 2, :], ACT.Sigmoid).then_inc(s.gate_on, 1)

        @block.vector
        def _(dve):
            norm_vector(nc, dve, g, s, m, gain)
            dve.wait_ge(s.brow_in, 16)

            def add(n):
                half, t = STEPS[n]
                dve.wait_ge(s.gate_full, n + 1)
                nc.vector.tensor_tensor(part[:, n % 2, :], g.PS[:, n % 4, :], brow[:, half * 512:(half + 1) * 512],
                                        ALU.add).then_inc(s.added, 1)

            add(0)
            for n, (half, t) in enumerate(STEPS):
                if n + 1 < len(STEPS):
                    add(n + 1)
                dve.wait_ge(s.gate_on, n + 1)
                dve.wait_ge(s.ple_full, n + 1)
                nc.vector.tensor_tensor(part[:, n % 2, :], part[:, n % 2, :], g.PS[:, 4 + n % 4, :],
                                        ALU.mult).then_inc(s.gated, 1)
                dve.drain()
                x = g.X[:, t, half * 512:(half + 1) * 512]
                nc.vector.tensor_tensor(x, x, part[:, n % 2, :], ALU.add)
                dve.drain()


def norm_rows(nc, g, gain, out, tag):
    with memory(nc, tag) as mem, stage(nc, tag, "row_in squared meaned rooted ready stored") as (block, s):
        dst = g.X if out is None else g.YA
        row = mem("row", [P, D])
        stat = mem("stat", [P, 4 * T])

        @block.sync
        def _(sp):
            sp.dma_start(row[:, :], gain.partition_broadcast(P)).then_inc(s.row_in, 16)
            if out is not None:
                for t in range(T):
                    sp.wait_ge(s.ready, t + 1)
                    sp.dma_start(out[0, t * P:(t + 1) * P, :], g.YA[:, t, :]).then_inc(s.stored, 16)
                sp.wait_ge(s.stored, 16 * T)

        @block.scalar
        def _(act):
            for t in range(T):
                nc.scalar.activation(g.YA[:, t, :], g.X[:, t, :], ACT.Square,
                                     accum_out=stat[:, t:t + 1]).then_inc(s.squared, 1)
            act.wait_ge(s.meaned, 1)
            nc.scalar.activation(stat[:, 2 * T:3 * T], stat[:, T:2 * T], ACT.Sqrt).then_inc(s.rooted, 1)

        @block.vector
        def _(dve):
            dve.wait_ge(s.squared, T)
            nc.vector.tensor_scalar(stat[:, T:2 * T], stat[:, 0:T], 1.0 / D, EPS, ALU.mult, ALU.add).then_inc(s.meaned, 1)
            dve.wait_ge(s.rooted, 1)
            nc.vector.reciprocal(stat[:, 3 * T:], stat[:, 2 * T:3 * T])
            dve.wait_ge(s.row_in, 16)
            dve.drain()
            for t in range(T):
                nc.vector.scalar_tensor_tensor(dst[:, t, :], g.X[:, t, :], stat[:, 3 * T + t:3 * T + t + 1], row[:, :],
                                               ALU.mult, ALU.mult).then_inc(s.ready, 1)


def program(nc, a, out):
    with ExitStack() as ctx:
        def sb(name, shape, dt=F32):
            return ctx.enter_context(nc.sbuf_tensor(name, shape, dt))

        n_const = len(CONSTS) * P + 2 + S + P + 1
        g = Parts()
        g.C = sb("consts_sb", [P, n_const])
        col = {n: g.C[:, i * P:(i + 1) * P] for i, n in enumerate(CONSTS)}
        g.ident, g.upto, g.before, g.ones, g.causal = (col[n] for n in CONSTS[:5])
        g.rot_a, g.rot_i = col["rot_a"], col["rot_i"]
        g.low = [col[f"low{i}"] for i in range(LEVELS)]
        g.up = [col[f"up{i}"] for i in range(LEVELS)]
        at = len(CONSTS) * P
        g.freq = g.C[:, at:at + 2]
        g.token_row = g.C[:, at + 2:at + 2 + S]
        g.rise, g.fall = g.C[:, at + 2:at + 2 + P], g.C[:, at + 2 + S:at + 2 + S + P]
        g.lane = g.C[:, at + 2 + S + P:at + 3 + S + P]
        g.X = sb("X", [P, T, D])
        g.feat = sb("feat", [P, K, S])
        g.YA = sb("YA", [P, T, D])
        g.YB = sb("YB", [P, T, D])
        g.W_odd = [g.feat[:, :, :].rearrange("p k c -> p (k c)"), g.YA[:, :, :].rearrange("p t d -> p (t d)")]
        g.PS = ctx.enter_context(nc.psum_tensor("PS", [P, 8, 512], F32))
        g.pool_sems = [ctx.enter_context(nc.semaphore(f"pool_dma{i}")) for i in range(4)]
        g.bias_at = [0, P, 3 * P, 6 * P]
        g.rows_dram = nc.dram_tensor("moe_rows", (S, D), F32, kind="Internal").ap()
        with ExitStack() as first:
            def sb1(name, shape):
                return first.enter_context(nc.sbuf_tensor(name, shape, F32))
            g.TAB = sb1("TAB", [P, 4, S])
            g.KT = sb1("KT", [P, KV_HEADS, S])
            g.V = sb1("V", [P, T, KV_HEADS * DH])
            g.BIAS = sb1("BIAS", [P, 10 * P])
            g.beta = sb1("beta", [P, T, HEADS])
            g.decay = sb1("decay", [P, T, HEADS])
            g.beta_pair = sb1("beta_pair", [P, T, 2])
            setup(nc, g, a)
            with nc.Fori(0, DEPTH) as layer:
                mixer_inputs(nc, g, a, layer)
                with ExitStack() as delta:
                    g.w_pair = delta.enter_context(nc.sbuf_tensor("w_pair", [P, 2 * K * 3 * P], F32))
                    g.pad = delta.enter_context(nc.sbuf_tensor("pad", [P, 2, 3, S + CONV - 1], F32))
                    g.taps = delta.enter_context(nc.sbuf_tensor("taps", [P, 2, 3, CONV], F32))
                    attention(nc, g, a, layer)
                    with nc.Fori(0, HEADS // 2 - 2) as pair:
                        delta_heads(nc, g, a, layer, pair, ahead=2)
                    delta_heads(nc, g, a, layer, HEADS // 2 - 2, ahead=1)
                    delta_heads(nc, g, a, layer, HEADS // 2 - 1, ahead=0)
                    merge(nc, g, a, layer)
        norm_rows(nc, g, a.final_gain, None, "between")
        g.slot_row = sb("slot_row", [P, 2, S])
        g.weight_row = sb("weight_row", [P, 2, S])
        g.W = [sb(f"W{i}", [P, K * F]) for i in range(6)]
        g.extra = sb("extra", [P, 2 * EXTRA + 1], I32)
        for layer in range(DEPTH):
            (short_conv if layer % 2 == 0 else rg_lru)(nc, g, a, layer)
            route(nc, g, a, layer)
            experts(nc, g, a, layer, extra=False)
            experts(nc, g, a, layer, extra=True)
            per_layer(nc, g, a, layer)
        norm_rows(nc, g, a.norm_final, out, "last")


_LAID_OUT = {
    "norm_gain": lambda v: v.reshape(DEPTH, K, P).transpose(0, 2, 1),
    "conv_w": lambda v: v.reshape(DEPTH, CONV, 3, HEADS // 2, 2, P).transpose(0, 3, 5, 4, 2, 1),
    "norm_mix_2": lambda v: v.reshape(DEPTH, K, P).transpose(0, 2, 1),
    "norm_ple_2": lambda v: v.reshape(DEPTH, K, P).transpose(0, 2, 1),
    "conv_a_2": lambda v: v.reshape(3, K, P).transpose(2, 1, 0),
}
_PLAIN = ["x", "positions", "w_in", "a_log", "dt_bias", "gdn_norm_gain", "idx_k_gain", "w_out", "p_2", "w_in_a_2",
          "w_out_a_2", "w_in_b_2", "w_rgate_b_2", "w_igate_b_2", "w_out_b_2", "norm_ffn_2", "w_router_group_2",
          "b_router_group_2", "w_router_expert_2", "b_router_expert_2", "w_exp_gate_2", "w_exp_up_2", "w_exp_down_2",
          "final_gain", "w_ple_2", "w_ple_gate_2", "b_ple_gate_2", "norm_final_2"]


def lay_out(inputs):
    arrays = {f"in_{n}": np.ascontiguousarray(inputs[n]) for n in _PLAIN}
    for n, order in _LAID_OUT.items():
        arrays[f"in_{n}"] = np.ascontiguousarray(order(np.asarray(inputs[n])))
    arrays["in_norm_ffn_cols"] = np.ascontiguousarray(
        np.asarray(inputs["norm_ffn_2"]).reshape(DEPTH, K, P).transpose(0, 2, 1))
    cols = np.concatenate([np.asarray(inputs[n]).reshape(-1, K, P) for n in
                           ("conv_b_2", "conv_bias_b_2", "b_rgate_b_2", "b_igate_b_2", "lam_b_2")])
    arrays["in_lru_cols"] = np.ascontiguousarray(cols.transpose(2, 0, 1))
    arrays["in_consts"] = shape_constants()
    return arrays


def views(aps):
    def slabs(name):
        return aps[name].rearrange("l (k p) c -> l p k c", p=P)

    a = Parts()
    a.x, a.positions, a.consts = aps["in_x"], aps["in_positions"], aps["in_consts"]
    a.norm_gain, a.conv_w = aps["in_norm_gain"], aps["in_conv_w"]
    a.w_in = slabs("in_w_in")
    a.w_heads = aps["in_w_in"][:, :, C_QKV:C_ZB].rearrange("l (k p) (s r h c) -> l r h s p k c", p=P, s=3, r=HEADS // 2, h=2)
    a.a_log, a.dt_bias = aps["in_a_log"], aps["in_dt_bias"]
    a.gdn_norm_gain, a.idx_k_gain = aps["in_gdn_norm_gain"], aps["in_idx_k_gain"]
    a.w_out = slabs("in_w_out")
    a.final_gain = aps["in_final_gain"]
    a.p = aps["in_p_2"]
    a.norm_mix = aps["in_norm_mix_2"]
    a.w_in_a = aps["in_w_in_a_2"][0].rearrange("(k p) (s f c) -> f k p s c", p=P, s=3, f=K)
    a.conv_a = aps["in_conv_a_2"]
    a.w_out_a, a.w_out_b = slabs("in_w_out_a_2")[0], slabs("in_w_out_b_2")[0]
    a.w_in_b = aps["in_w_in_b_2"][0].rearrange("(k p) (s c) -> p k s c", p=P, s=2)
    a.lru_cols = aps["in_lru_cols"]
    a.w_rgate = aps["in_w_rgate_b_2"][0].rearrange("d n (k p) e -> d n p k e", p=P)
    a.w_igate = aps["in_w_igate_b_2"][0].rearrange("d n (k p) e -> d n p k e", p=P)
    a.norm_ffn, a.norm_ffn_row = aps["in_norm_ffn_cols"], aps["in_norm_ffn_2"]
    a.w_router_group, a.w_router_expert = slabs("in_w_router_group_2"), slabs("in_w_router_expert_2")
    a.b_router_group, a.b_router_expert = aps["in_b_router_group_2"], aps["in_b_router_expert_2"]
    a.w_exp_gate = aps["in_w_exp_gate_2"].rearrange("l e (k p) f -> l e p k f", p=P)
    a.w_exp_up = aps["in_w_exp_up_2"].rearrange("l e (k p) f -> l e p k f", p=P)
    a.w_exp_down = aps["in_w_exp_down_2"].rearrange("l e (k p) d -> l e p k d", p=P)
    a.norm_ple = aps["in_norm_ple_2"]
    a.w_ple, a.w_ple_gate = slabs("in_w_ple_2"), slabs("in_w_ple_gate_2")
    a.b_ple_gate, a.norm_final = aps["in_b_ple_gate_2"], aps["in_norm_final_2"]
    return a


def kernel(**inputs):
    import concourse.bacc as bacc
    from concourse.bass_utils import run_bass_kernel_spmd

    nc = bacc.Bacc("TRN2", target_bir_lowering=False, num_devices=1)
    arrays = lay_out(inputs)
    aps = {n: nc.dram_tensor(n, v.shape, mybir.dt.from_np(v.dtype), kind="ExternalInput").ap() for n, v in arrays.items()}
    out = nc.dram_tensor("out", (1, S, D), F32, kind="ExternalOutput").ap()
    program(nc, views(aps), out)
    result = run_bass_kernel_spmd(nc, [arrays], core_ids=[0])
    return result.results[0]["out"]
```
